# Optimizing a Trainium2 kernel written in Bass

```python
import math
import functools
import jax
import jax.numpy as jnp
from jax import lax
import numpy as np

D_MODEL = 1024
BATCH = 1
SEQ = 512
DEPTH = 2
DEC_BATCH = 1
DEC_SEQ = 32
PAST_LEN = 512

CHUNK = 64
Q_BLOCK = 128
HEAD_DIM = 64
H_A = 8
H_B = 8
IDX_HEADS = 8
IDX_DIM = 64
IDX_TOPK_MAX = 256
H_C = 8
DK_C = 128
DV_C = 128
CONV_W = 4
D_FF = 4 * D_MODEL
REL_BUCKETS = 32
REL_MAX_DIST = 256
FFN_RES = 0.5
EPS = 1e-6

D_A = H_A * HEAD_DIM
D_B = H_B * HEAD_DIM
AB_SIZES = (D_A, D_A, D_A, IDX_HEADS * IDX_DIM, IDX_DIM, IDX_HEADS, D_B, D_B, D_B, H_B)
AB_IN = sum(AB_SIZES)
C_QKV = 2 * H_C * DK_C + H_C * DV_C
C_SIZES = (C_QKV, H_C * DV_C, H_C, H_C)
C_IN = sum(C_SIZES)

kernel_name = 'hybrid_dsa_fox_gdn_stream_step'

def split_cols(z, sizes):
    return jnp.split(z, [int(i) for i in np.cumsum(sizes)[:-1]], axis=-1)

def rms_norm(x, g):
    xf = x.astype(jnp.float32)
    y = xf * lax.rsqrt(jnp.mean(xf * xf, axis=-1, keepdims=True) + EPS)
    return (y * g.astype(jnp.float32)).astype(x.dtype)

def l2_normalize(x):
    return x * lax.rsqrt(jnp.sum(x * x, axis=-1, keepdims=True) + EPS)

def modulate(x, g, shift, scale):
    return rms_norm(x, g) * (1.0 + scale[:, None, :]) + shift[:, None, :]

def add_branch(x, y, g, gate, weight):
    return x + weight * gate[:, None, :] * rms_norm(y, g)

def swiglu(h, w_gate, w_up, w_down):
    return (jax.nn.silu(h @ w_gate) * (h @ w_up)) @ w_down

def t5_bucket(rel):
    nb = REL_BUCKETS // 2
    max_exact = nb // 2
    base = jnp.where(rel > 0, nb, 0)
    n = jnp.abs(rel)
    nf = jnp.maximum(n, 1).astype(jnp.float32)
    large = max_exact + (jnp.log(nf / max_exact) / math.log(REL_MAX_DIST / max_exact)
                         * (nb - max_exact)).astype(jnp.int32)
    large = jnp.minimum(large, nb - 1)
    return base + jnp.where(n < max_exact, n, large)

def over_query_blocks(fn, q_pos, *q_arrays):
    tq = q_pos.shape[0]
    if tq <= Q_BLOCK:
        return fn(q_pos, *q_arrays)
    nb = tq // Q_BLOCK
    pos_b = q_pos.reshape(nb, Q_BLOCK)
    arrs_b = [jnp.moveaxis(a.reshape(a.shape[0], nb, Q_BLOCK, *a.shape[2:]), 1, 0) for a in q_arrays]
    out = lax.map(lambda xs: fn(*xs), (pos_b, *arrs_b))
    out = jnp.moveaxis(out, 0, 1)
    return out.reshape(out.shape[0], tq, *out.shape[3:])

def dsa_block(k, v, ki, rel_table, top_k, q_pos, q, qi, wi):
    n_keys = k.shape[1]
    s = jnp.einsum('bqhd,bsd->bqhs', qi, ki) * IDX_DIM ** -0.5
    score = jnp.einsum('bqhs,bqh->bqs', jax.nn.relu(s), wi).astype(jnp.float32) * IDX_HEADS ** -0.5
    admissible = (jnp.arange(n_keys) // CHUNK)[None, :] <= (q_pos // CHUNK)[:, None]
    score = jnp.where(admissible[None], score, -jnp.inf)
    top_score, top_idx = lax.top_k(score, top_k)
    take = jax.vmap(lambda rows, idx: rows[idx])
    k_sel = take(k, top_idx)
    v_sel = take(v, top_idx)
    bias = rel_table[t5_bucket(top_idx - q_pos[None, :, None])]
    logits = (jnp.einsum('bqhd,bqkhd->bqhk', q, k_sel).astype(jnp.float32) * HEAD_DIM ** -0.5
              + jnp.moveaxis(bias, -1, 2).astype(jnp.float32))
    logits = jnp.where((top_score > -jnp.inf)[:, :, None, :], logits, -jnp.inf)
    p = jax.nn.softmax(logits, axis=-1).astype(v.dtype)
    return jnp.einsum('bqhk,bqkhd->bqhd', p, v_sel)

def fox_block(k, v, f_k, q_pos, q, f_q):
    n_keys = k.shape[1]
    logits = (jnp.einsum('bqhd,bshd->bhqs', q, k).astype(jnp.float32) * HEAD_DIM ** -0.5
              + f_q.transpose(0, 2, 1)[..., None] - f_k.transpose(0, 2, 1)[:, :, None, :])
    causal = jnp.arange(n_keys)[None, :] <= q_pos[:, None]
    logits = jnp.where(causal, logits, -jnp.inf)
    p = jax.nn.softmax(logits, axis=-1).astype(v.dtype)
    return jnp.einsum('bhqs,bshd->bqhd', p, v)

def mixer_ab(h, w, past):
    B, T, _ = h.shape
    z = h @ w['ab_w_in']
    qa, ka, va, qi, ki, wi, qb, kb, vb, fl = split_cols(z, AB_SIZES)
    qa = qa.reshape(B, T, H_A, HEAD_DIM)
    ka = ka.reshape(B, T, H_A, HEAD_DIM)
    va = va.reshape(B, T, H_A, HEAD_DIM)
    qi = qi.reshape(B, T, IDX_HEADS, IDX_DIM)
    qb = qb.reshape(B, T, H_B, HEAD_DIM)
    kb = kb.reshape(B, T, H_B, HEAD_DIM)
    vb = vb.reshape(B, T, H_B, HEAD_DIM)
    logf = jax.nn.log_sigmoid((fl + w['ab_b_f']).astype(jnp.float32))
    if past is None:
        offset = 0
        ka_all, va_all, ki_all, kb_all, vb_all, logf_all = ka, va, ki, kb, vb, logf
    else:
        cak, cav, caik, cbk, cbv, cblf = past
        offset = cak.shape[1]
        ka_all = jnp.concatenate([cak, ka], axis=1)
        va_all = jnp.concatenate([cav, va], axis=1)
        ki_all = jnp.concatenate([caik, ki], axis=1)
        kb_all = jnp.concatenate([cbk, kb], axis=1)
        vb_all = jnp.concatenate([cbv, vb], axis=1)
        logf_all = jnp.concatenate([cblf.astype(jnp.float32), logf], axis=1)
    n_keys = offset + T
    q_pos = offset + jnp.arange(T, dtype=jnp.int32)
    top_k = min(IDX_TOPK_MAX, n_keys // 4)
    o_a = over_query_blocks(functools.partial(dsa_block, ka_all, va_all, ki_all, w['rel_bias'], top_k),
                            q_pos, qa, qi, wi)
    f_all = jnp.cumsum(logf_all, axis=1)
    o_b = over_query_blocks(functools.partial(fox_block, kb_all, vb_all, f_all),
                            q_pos, qb, f_all[:, offset:])
    o = jnp.concatenate([o_a.reshape(B, T, D_A), o_b.reshape(B, T, D_B)], axis=-1)
    y = o @ w['ab_w_out']
    return y, (ka, va, ki, kb, vb, logf.astype(h.dtype))

def gated_delta_chunked(q, k, v, g, beta, s0):
    B, T, H, _ = q.shape
    dv = v.shape[-1]
    c = min(T, CHUNK)
    n = T // c

    def chunks4(a):
        return a.reshape(B, n, c, H, a.shape[-1]).transpose(1, 0, 3, 2, 4)

    def chunks3(a):
        return a.reshape(B, n, c, H).transpose(1, 0, 3, 2)

    q, k, v = chunks4(q), chunks4(k), chunks4(v)
    g, beta = chunks3(g), chunks3(beta)
    gc = jnp.cumsum(g, axis=-1)
    causal = jnp.tril(jnp.ones((c, c), dtype=bool))
    strict = jnp.tril(jnp.ones((c, c), dtype=bool), k=-1)
    decay = jnp.exp(jnp.where(causal, gc[..., :, None] - gc[..., None, :], -jnp.inf))
    kk = jnp.einsum('nbhid,nbhjd->nbhij', k, k)
    a_low = jnp.where(strict, beta[..., :, None] * kk * decay, 0.0)
    lhs = a_low + jnp.eye(c, dtype=a_low.dtype)
    rhs = jnp.concatenate([v * beta[..., None], k * (beta * jnp.exp(gc))[..., None]], axis=-1)
    sol = lax.linalg.triangular_solve(lhs, rhs, left_side=True, lower=True)
    u, wk = sol[..., :dv], sol[..., dv:]
    qk = jnp.where(causal, jnp.einsum('nbhid,nbhjd->nbhij', q, k) * decay, 0.0)
    q_dec = q * jnp.exp(gc)[..., None]
    k_dec = k * jnp.exp(gc[..., -1:] - gc)[..., None]
    g_last = jnp.exp(gc[..., -1])

    def step(s, xs):
        u_c, w_c, qk_c, qd_c, kd_c, gl_c = xs
        v_new = u_c - jnp.einsum('bhcd,bhde->bhce', w_c, s)
        o_c = jnp.einsum('bhcd,bhde->bhce', qd_c, s) + jnp.einsum('bhij,bhje->bhie', qk_c, v_new)
        s = s * gl_c[..., None, None] + jnp.einsum('bhcd,bhce->bhde', kd_c, v_new)
        return s, o_c

    s_fin, o = lax.scan(step, s0, (u, wk, qk, q_dec, k_dec, g_last))
    o = o.transpose(1, 0, 3, 2, 4).reshape(B, T, H, dv)
    return o, s_fin

def mixer_gdn(h, w, past):
    B, T, _ = h.shape
    z = h @ w['gdn_w_in']
    qkv, gate, b_logit, a_logit = split_cols(z, C_SIZES)
    if past is None:
        conv_prev = jnp.zeros((B, CONV_W - 1, C_QKV), qkv.dtype)
        s0 = jnp.zeros((B, H_C, DK_C, DV_C), jnp.float32)
    else:
        conv_prev, s_prev = past
        s0 = s_prev.astype(jnp.float32)
    xp = jnp.concatenate([conv_prev, qkv], axis=1)
    cw = w['gdn_conv_w']
    conv = xp[:, 0:T] * cw[0]
    for j in range(1, CONV_W):
        conv = conv + xp[:, j:j + T] * cw[j]
    conv = jax.nn.silu(conv)
    new_conv = xp[:, xp.shape[1] - (CONV_W - 1):]
    q, k, v = split_cols(conv, (H_C * DK_C, H_C * DK_C, H_C * DV_C))
    q = l2_normalize(q.reshape(B, T, H_C, DK_C).astype(jnp.float32)) * DK_C ** -0.5
    k = l2_normalize(k.reshape(B, T, H_C, DK_C).astype(jnp.float32))
    v = v.reshape(B, T, H_C, DV_C).astype(jnp.float32)
    beta = jax.nn.sigmoid(b_logit.astype(jnp.float32))
    g = -jnp.exp(w['gdn_A_log'].astype(jnp.float32)) * jax.nn.softplus(
        a_logit.astype(jnp.float32) + w['gdn_dt_bias'].astype(jnp.float32))
    o, s_new = gated_delta_chunked(q, k, v, g, beta, s0)
    o = rms_norm(o, w['gdn_norm_w']) * jax.nn.silu(gate.reshape(B, T, H_C, DV_C).astype(jnp.float32))
    y = o.reshape(B, T, H_C * DV_C).astype(h.dtype) @ w['gdn_w_out']
    return y, (new_conv, s_new.astype(h.dtype))

def ffn_sublayer(x, w, mod, l, slot, j):
    h = modulate(x, w['norm_pre'][l, slot], mod[:, slot, 0], mod[:, slot, 1])
    y = swiglu(h, w['ffn_w_gate'][l, j], w['ffn_w_up'][l, j], w['ffn_w_down'][l, j])
    return add_branch(x, y, w['norm_post'][l, slot], mod[:, slot, 2], FFN_RES)

def forward(x, c, w, past):
    B = x.shape[0]
    new_state = []
    for l in range(DEPTH):
        mod = (jax.nn.silu(c) @ w['ada_w'][l] + w['ada_b'][l]).reshape(B, 3, 3, D_MODEL)
        x = ffn_sublayer(x, w, mod, l, 0, 0)
        h = modulate(x, w['norm_pre'][l, 1], mod[:, 1, 0], mod[:, 1, 1])
        if l % 2 == 0:
            y, st = mixer_ab(h, w, None if past is None else past[:6])
        else:
            y, st = mixer_gdn(h, w, None if past is None else past[6:])
        x = add_branch(x, y, w['norm_post'][l, 1], mod[:, 1, 2], 1.0)
        new_state.extend(st)
        x = ffn_sublayer(x, w, mod, l, 2, 1)
    return x, new_state

def setup_inputs(seed: int = 0) -> dict:
    key = jax.random.key(seed)
    ks = jax.random.split(key, 32)

    def nrm(k, shape, s):
        return s * jax.random.normal(k, shape, jnp.float32)

    dt = jnp.exp(jax.random.uniform(ks[20], (H_C,), jnp.float32, math.log(1e-3), math.log(1e-1)))
    return {
        'x_prompt': nrm(ks[0], (BATCH, SEQ, D_MODEL), 1.0),
        'x_sample': nrm(ks[1], (DEC_BATCH, DEC_SEQ, D_MODEL), 1.0),
        'cache_a_k': nrm(ks[2], (DEC_BATCH, PAST_LEN, H_A, HEAD_DIM), 1.0),
        'cache_a_v': nrm(ks[3], (DEC_BATCH, PAST_LEN, H_A, HEAD_DIM), 1.0),
        'cache_a_idx_k': nrm(ks[4], (DEC_BATCH, PAST_LEN, IDX_DIM), 1.0),
        'cache_b_k': nrm(ks[5], (DEC_BATCH, PAST_LEN, H_B, HEAD_DIM), 1.0),
        'cache_b_v': nrm(ks[6], (DEC_BATCH, PAST_LEN, H_B, HEAD_DIM), 1.0),
        'cache_b_logf': jax.nn.log_sigmoid(2.0 + nrm(ks[7], (DEC_BATCH, PAST_LEN, H_B), 1.0)),
        'state_c_conv': nrm(ks[8], (DEC_BATCH, CONV_W - 1, C_QKV), 1.0),
        'state_c_rec': nrm(ks[9], (DEC_BATCH, H_C, DK_C, DV_C), 0.2),
        'c_prompt': nrm(ks[10], (BATCH, D_MODEL), 1.0),
        'c_sample': nrm(ks[11], (DEC_BATCH, D_MODEL), 1.0),
        'rel_bias': nrm(ks[12], (REL_BUCKETS, H_A), 0.5),
        'ab_w_in': nrm(ks[13], (D_MODEL, AB_IN), D_MODEL ** -0.5),
        'ab_b_f': 2.0 + nrm(ks[14], (H_B,), 0.1),
        'ab_w_out': nrm(ks[15], (D_A + D_B, D_MODEL), (D_A + D_B) ** -0.5),
        'gdn_w_in': nrm(ks[16], (D_MODEL, C_IN), D_MODEL ** -0.5),
        'gdn_conv_w': nrm(ks[17], (CONV_W, C_QKV), CONV_W ** -0.5),
        'gdn_A_log': jnp.log(jax.random.uniform(ks[18], (H_C,), jnp.float32, 1.0, 16.0)),
        'gdn_dt_bias': dt + jnp.log(-jnp.expm1(-dt)),
        'gdn_norm_w': 1.0 + nrm(ks[19], (DV_C,), 0.1),
        'gdn_w_out': nrm(ks[21], (H_C * DV_C, D_MODEL), (H_C * DV_C) ** -0.5),
        'norm_pre': 1.0 + nrm(ks[22], (DEPTH, 3, D_MODEL), 0.1),
        'norm_post': 1.0 + nrm(ks[23], (DEPTH, 3, D_MODEL), 0.1),
        'ada_w': nrm(ks[24], (DEPTH, D_MODEL, 9 * D_MODEL), 0.5 * D_MODEL ** -0.5),
        'ada_b': nrm(ks[25], (DEPTH, 9 * D_MODEL), 0.01),
        'ffn_w_gate': nrm(ks[26], (DEPTH, 2, D_MODEL, D_FF), D_MODEL ** -0.5),
        'ffn_w_up': nrm(ks[27], (DEPTH, 2, D_MODEL, D_FF), D_MODEL ** -0.5),
        'ffn_w_down': nrm(ks[28], (DEPTH, 2, D_FF, D_MODEL), D_FF ** -0.5),
    }

def reference(x_prompt, x_sample, cache_a_k, cache_a_v, cache_a_idx_k, cache_b_k, cache_b_v, cache_b_logf,
              state_c_conv, state_c_rec, c_prompt, c_sample, rel_bias, ab_w_in, ab_b_f, ab_w_out,
              gdn_w_in, gdn_conv_w, gdn_A_log, gdn_dt_bias, gdn_norm_w, gdn_w_out, norm_pre, norm_post,
              ada_w, ada_b, ffn_w_gate, ffn_w_up, ffn_w_down):
    w = dict(rel_bias=rel_bias, ab_w_in=ab_w_in, ab_b_f=ab_b_f, ab_w_out=ab_w_out,
             gdn_w_in=gdn_w_in, gdn_conv_w=gdn_conv_w, gdn_A_log=gdn_A_log, gdn_dt_bias=gdn_dt_bias,
             gdn_norm_w=gdn_norm_w, gdn_w_out=gdn_w_out, norm_pre=norm_pre, norm_post=norm_post,
             ada_w=ada_w, ada_b=ada_b, ffn_w_gate=ffn_w_gate, ffn_w_up=ffn_w_up, ffn_w_down=ffn_w_down)
    y_prompt, st_p = forward(x_prompt, c_prompt, w, None)
    past = (cache_a_k, cache_a_v, cache_a_idx_k, cache_b_k, cache_b_v, cache_b_logf, state_c_conv, state_c_rec)
    y_sample, st_s = forward(x_sample, c_sample, w, past)
    p_a_k, p_a_v, p_a_idx_k, p_b_k, p_b_v, p_b_logf, p_c_conv, p_c_rec = st_p
    s_a_k, s_a_v, s_a_idx_k, s_b_k, s_b_v, s_b_logf, s_c_conv, s_c_rec = st_s
    return (y_prompt, y_sample,
            p_a_k, p_a_v, p_a_idx_k, p_b_k, p_b_v, p_b_logf, p_c_conv, p_c_rec,
            s_a_k, s_a_v, s_a_idx_k, s_b_k, s_b_v, s_b_logf, s_c_conv, s_c_rec)


_drawn_inputs = setup_inputs


def setup_inputs(seed=0):
    import zlib

    import numpy as np

    out = dict(_drawn_inputs(seed))
    spreads = {}
    factors = {'cache_b_logf': 2.707}
    for name, (base, spread) in spreads.items():
        noise = np.random.default_rng([zlib.crc32(name.encode()), seed]).standard_normal(out[name].shape)
        drawn = base * np.exp(spread * noise) if base else spread * noise
        out[name] = jnp.asarray(drawn.astype(out[name].dtype))
    for name, factor in factors.items():
        out[name] = (out[name] * factor).astype(out[name].dtype)
    return out
```

```python
from contextlib import ExitStack

import numpy as np

import concourse.bass as bass
from concourse import mybir

F32 = mybir.dt.float32
F32R = mybir.dt.float32r
ALU = mybir.AluOpType
ACT = mybir.ActivationFunctionType
AX = mybir.AxisListType

P = 128
D = 1024
TP, TS = 512, 32
T = TP + TS
HT = T // 2
KD = D // P
DFF = 4 * D
KB = DFF // D
LAYERS, SUBS = 2, 3
EPS = 1e-6
NEG = -1.0e30
TAKEN = -3.0e38
SCORE_TILES = (1, 2, 3)
HD = 64
NH = 8
TOPK_P, TOPK_S = 128, 136
GROUPS = ((0, TP), (TP, T))

FFN_PAIRS = KB * (KD + KD // 2)
AB_PAIRS = 15
GDN_UNITS, GDN_PAIRS = 33, 17
OUT_PAIRS = KD // 2
PAIRS = 4 * FFN_PAIRS + AB_PAIRS + GDN_PAIRS + 2 * OUT_PAIRS
ADA_TILES = LAYERS * 9 * KD
ADA_W = 3 * P
ADA_GROUPS = (4, 4, 2, 0)
ADA_HALF = 2 * ADA_W
ADA_HALVES = LAYERS * 9 * D // ADA_HALF
ADA_HEAD = 2
ADA_FIRST_HALF = (4, 12, 20, 0)
ADA_CHUNKS_BEFORE = (2, 6, 10, 14)


def first_pairs():
    at, out = 0, {}
    for name, n in (("ffn0", FFN_PAIRS), ("ab_in", AB_PAIRS), ("ab_out", OUT_PAIRS), ("ffn1", FFN_PAIRS),
                    ("ffn2", FFN_PAIRS), ("gdn_in", GDN_PAIRS), ("gdn_out", OUT_PAIRS), ("ffn3", FFN_PAIRS)):
        out[name] = at
        at += n
    assert at == PAIRS and PAIRS % 2 == 0
    return out


FIRST = first_pairs()

Z_IK, Z_W, Z_IQ, Z_KA, Z_QA, Z_VA, Z_KB, Z_QB, Z_VB = 0, 1, 2, 6, 10, 14, 18, 22, 26
Z_TILES = 30
FOX_ROW = 32
REL = 768
REL_AT = P * (REL + 1)
NK_S = TP + TS


ARENA = 25100

CW = 4
GZ_Q, GZ_K, GZ_V, GZ_G = 0, NH, 2 * NH, 3 * NH
QKV = 3 * NH
CHUNK = 64
CHUNKS = TP // CHUNK
TILES = TP // P
ROW_K, ROW_B, ROW_Q, ROW_D = 0, 32, 64, 96
LEVELS = 6
STRIP = P + NH - 1


class Cutter:

    def __init__(self, flat, at=0):
        self.flat, self.at = flat, at

    def __call__(self, dims, **sizes):
        n = int(np.prod(list(sizes.values())))
        got = self.flat[:, self.at:self.at + n]
        self.at += n
        assert self.at <= self.flat.shape[1], self.at
        return got.rearrange(f"p ({dims}) -> p {dims}", **sizes) if len(sizes) > 1 else got


def build(nc, io):
    with ExitStack() as ctx:
        def sb(name, shape, dt=F32):
            return ctx.enter_context(nc.sbuf_tensor(name, shape, dt))

        def sem(name):
            return ctx.enter_context(nc.semaphore(name))

        x = sb("x", [P, KD, T])
        hid_at = nc.sbuf_base
        hid_hi = sb("hid_hi", [P, KD, T], F32R)
        hid_lo = sb("hid_lo", [P, KD, T], F32R)
        h_at = nc.sbuf_base
        h_hi = sb("h_hi", [P, KD, T], F32R)
        h_lo = sb("h_lo", [P, KD, T], F32R)
        raw = sb("raw", [P, 2, 2, D])
        w_hi = sb("w_hi", [P, 2, D], F32R)
        w_lo = sb("w_lo", [P, 2, D], F32R)
        mod = sb("mod", [P, ADA_TILES, 2])
        c_t = sb("c_t", [P, KD, 2])
        ada_b = sb("ada_b", [P, ADA_TILES])
        g_pre = sb("g_pre", [P, LAYERS * SUBS * KD])
        g_post = sb("g_post", [P, LAYERS * SUBS * KD])
        scale_in = sb("scale_in", [P, LAYERS * SUBS, KD, 2])
        gate_out = sb("gate_out", [P, LAYERS * SUBS, KD, 2])
        spare = nc.alloc_sbuf_tensor_at("spare", [P, 2 * KD * T], F32, offset=hid_at)
        rel_sb = sb("rel_sb", [32, NH])
        diag_mask = sb("diag_mask", [P, P])
        tail_mask = sb("tail_mask", [P, TS])
        sel = sb("sel", [P, NH])
        b_f = sb("b_f", [P, 1])
        norm_col = sb("norm_col", [P, 1])
        wi_tok = sb("wi_tok", [P, 5, NH])
        top8 = sb("top8", [P, 8])
        neg_max = sb("neg_max", [P, 2])
        p_sum = sb("p_sum", [P, 2])
        p_inv = sb("p_inv", [P, 2])
        ones = sb("ones", [P, P])
        ident = sb("ident", [P, P])
        ada_rows = sb("ada_rows", [P, ADA_W])
        one_col = sb("one_col", [P, 1])
        eps_col = sb("eps_col", [P, 1])
        arena = sb("arena", [P, ARENA])
        cut = Cutter(arena)
        y = cut("k t", k=KD, t=T)
        sq = cut("k t", k=2, t=T)
        tmp = cut("k t", k=2, t=T)
        h32 = cut("k t", k=2, t=T)
        silu = cut("k t", k=2, t=T)
        rstd = cut("t", t=T)
        lnv = cut("t", t=T)
        ada_w = cut("k n", k=KD, n=2 * ADA_HALF)
        cut = Cutter(arena)
        z = cut("k t", k=Z_TILES, t=T)
        scores = {1: cut("n", n=256), 2: cut("n", n=384), 3: cut("n", n=512), "s": cut("n", n=NK_S)}
        scores[0] = cut("n", n=P)
        p_turned = cut("r b q", r=2, b=5, q=P)
        rel_at = cut.at
        bias_p = cut("h m", h=NH, m=5 * P)
        fb = Cutter(arena, Z_VA * T)("m", m=REL)
        onehot = Cutter(arena, Z_VB * T)("m", m=REL)
        cut = Cutter(arena, Z_IQ * T)
        neg_logits = cut("r t", r=2, t=T)
        probs = cut("r t", r=2, t=T)
        cut = Cutter(spare[:])
        cache_k = cut("k t", k=4, t=TP)
        cache_v = cut("b d", b=5, d=TP)
        cache_ik = cut("t", t=TP)
        v_tok = cut("b d", b=4, d=TP)
        relu = cut("r t", r=2, t=T)
        bias_s = relu
        cut = Cutter(arena, rel_at)
        fox_k = cut("t", t=TP + NK_S)
        fox_f = cut("t", t=TP + NK_S)
        fox_keep = cut("t", t=TP + NK_S)
        fox_q = cut("h q", h=NH, q=P)
        fox_qs = cut("r q", r=2, q=P)
        fox_w = Cutter(arena, Z_VA * T)("r t", r=4, t=T)

        cut = Cutter(arena)
        gz = cut("k t", k=4 * NH, t=T)
        rows_r, rows_c, rows_e = cut("t", t=T), cut("t", t=T), cut("t", t=T)
        conv_at = cut.at
        g_mask = cut("k n", k=4 + LEVELS, n=P)
        cols = cut("b r", b=TILES, r=P)
        cols_s = cut("g k", g=2, k=4)
        rows_es = cut("n", n=P)
        keys_s = cut("n", n=P)
        state_p = cut("h e", h=NH, e=P)
        state_s = cut("h e", h=NH, e=P)
        kdec_s = cut("g n", g=2, n=P)
        u_s = cut("g n", g=2, n=P)
        qk_s = cut("g n", g=2, n=P)
        v_new = cut("r n", r=2, n=P)
        ends = cut("c", c=CHUNKS + 1)
        ends_by_head = cut("c h", c=CHUNKS + 1, h=NH)
        g_last = cut("c h", c=CHUNKS + 1, h=NH)
        strips = cut("r n", r=2, n=STRIP)
        g_sel = cut("r h", r=4, h=NH)
        g_col = cut("r", r=4)
        conv_w = cut("k j", k=QKV, j=CW)
        cut = Cutter(arena, conv_at)
        conv_in = cut("r t", r=2, t=T + CW - 1)
        conv_acc = cut("r t", r=2, t=TP)
        conv_sq = cut("r t", r=2, t=TP)
        cut = Cutter(spare[:])
        conv_s = cut("k t", k=QKV, t=TS + CW - 1)
        conv_last = cut("k j", k=QKV, j=CW - 1)
        conv_before = cut("k j", k=QKV, j=CW - 1)
        conv_sum = cut("k t", k=QKV, t=TS)
        conv_tap = cut("k t", k=QKV, t=TS)
        row_a, row_sp, row_b, row_lb, row_g, row_lr, row_keep = (cut("t", t=T) for _ in range(7))
        cut = Cutter(spare[:])
        w_neg = cut("h t", h=NH, t=T)
        qk_t = cut("h t", h=NH, t=TP)
        spare_h = nc.alloc_sbuf_tensor_at("spare_h", [P, 2 * KD * T], F32, offset=h_at)
        cut = Cutter(spare_h[:])
        low, low_m, inv, inv_t, t2, k_beta, v_beta = (cut("u n", u=2, n=TP) for _ in range(7))
        cut = Cutter(arena, 4 * NH * T)
        g_sq, g_ln, g_rstd, g_tmp, g_out = (cut("r t", r=2, t=T) for _ in range(5))

        psum = ctx.enter_context(nc.psum_tensor("psum", [P, 8, 512], F32))

        def halves(bank):
            return psum[:, bank:bank + 2, 0:HT]

        def split(ap):
            return ap.rearrange("p (b t) -> p b t", b=2)

        in_loaded = sem("in_loaded")
        out_stored = sem("out_stored")
        w_loaded = [sem("w_loaded0"), sem("w_loaded1")]
        w_rounded = sem("w_rounded")
        w_split = sem("w_split")
        unit_done = sem("unit_done")
        bank_free = [sem("bank_free0"), sem("bank_free1")]
        ada_loaded = [sem(f"ada_loaded{k}") for k in range(KD)]
        ada_used = sem("ada_used")
        ada_rows_ready = sem("ada_rows_ready")
        ada_turned = sem("ada_turned")
        ada_added = sem("ada_added")
        c_ready = sem("c_ready")
        consts = sem("consts")
        cond_ready = sem("cond_ready")
        dve_own = sem("dve_own")
        mod_ready = sem("mod_ready")
        sq_ready = sem("sq_ready")
        sq_summed = sem("sq_summed")
        ln_done = sem("ln_done")
        rstd_ready = sem("rstd_ready")
        scaled = sem("scaled")
        h32_ready = sem("h32_ready")
        h_rounded = sem("h_rounded")
        h_ready = sem("h_ready")
        silu_ready = sem("silu_ready")
        hid_rounded = sem("hid_rounded")
        hid_ready = sem("hid_ready")
        y_scaled = sem("y_scaled")
        x_ready = sem("x_ready")

        rel_made = sem("rel_made")
        onehot_loaded = sem("onehot_loaded")
        rel_copied = sem("rel_copied")
        rel_spread = sem("rel_spread")
        bias_loaded = sem("bias_loaded")
        bias_s_loaded = sem("bias_s_loaded")
        cache_loaded = {"ik": sem("cache_ik_loaded"), "A": sem("cache_a_loaded"), "B": sem("cache_b_loaded")}
        wi_turned = sem("wi_turned")
        wi_ready = sem("wi_ready")
        dots_done = sem("dots_done")
        relu_ready = sem("relu_ready")
        score_added = sem("score_added")
        masks_ready = sem("masks_ready")
        v_turned = sem("v_turned")
        v_ready = sem("v_ready")
        logits_done = sem("logits_done")
        max_ready = sem("max_ready")
        exp_done = sem("exp_done")
        p_ready = sem("p_ready")
        p_turn_done = sem("p_turn_done")
        p_turn_ready = sem("p_turn_ready")
        av_done = sem("av_done")
        o_rounded = sem("o_rounded")
        o_ready = sem("o_ready")
        fox_own = sem("fox_own")
        fox_loaded = sem("fox_loaded")
        fox_copied = sem("fox_copied")
        fox_ready = sem("fox_ready")
        state_stored = sem("state_stored")

        gdn_loaded = sem("gdn_loaded")
        conv_zeroed = sem("conv_zeroed")
        conv_done = sem("conv_done")
        conv_silu = sem("conv_silu")
        conv_sq_ready = sem("conv_sq_ready")
        lens_summed = sem("lens_summed")
        sample_conv = sem("sample_conv")
        sample_silu = sem("sample_silu")
        row_own = sem("row_own")
        rows_lin = sem("rows_lin")
        lens_ln = sem("lens_ln")
        rows_ready = sem("rows_ready")
        rows_exp = sem("rows_exp")
        ends_ready = sem("ends_ready")
        rows_turned = sem("rows_turned")
        cols_ready = sem("cols_ready")
        gdn_masks = sem("gdn_masks")
        gdn_state = sem("gdn_state")
        lq_ready = sem("lq_ready")
        kk_done = sem("kk_done")
        kq_done = sem("kq_done")
        kk_exp = sem("kk_exp")
        kq_exp = sem("kq_exp")
        kk_decayed = sem("kk_decayed")
        kq_decayed = sem("kq_decayed")
        bc_ready = sem("bc_ready")
        k_turned = sem("k_turned")
        v_turned_g = sem("v_turned_g")
        q_factor = sem("q_factor")
        kv_scaled = sem("kv_scaled")
        low_ready = sem("low_ready")
        t2_made = sem("t2_made")
        t2_copied = sem("t2_copied")
        e_made = sem("e_made")
        inv_ready = sem("inv_ready")
        wu_made = sem("wu_made")
        wu_out = sem("wu_out")
        v_made = sem("v_made")
        v_new_ready = sem("v_new_ready")
        o_made = sem("o_made")
        o_out = sem("o_out")
        kv_made = sem("kv_made")
        state_new = sem("state_new")
        g_sq_ready = sem("g_sq_ready")
        g_sq_summed = sem("g_sq_summed")
        g_ln_done = sem("g_ln_done")
        g_rstd_ready = sem("g_rstd_ready")
        g_own = sem("g_own")
        g_used = sem("g_used")
        g_ready = sem("g_ready")

        block = ctx.enter_context(nc.Block())
        N_IN = 13

        items = []
        for mixer in "AB":
            for i in (0, 1, 2, 3, "s"):
                for h in range(NH if i != "s" else 2):
                    items.append((mixer, i, h))
        first_item = {"A": 0, "B": len(items) // 2}
        n_items = len(items) // 2
        group_of, last_of_group = [], []
        for e, (mixer, i, h) in enumerate(items):
            group_of.append(group_of[-1] + 1 if e and h % 2 == 0 else (group_of[-1] if e else 0))
            last_of_group.append(h % 2 == 1)

        def keys_of(i):
            return NK_S if i == "s" else P * (i + 1)

        def score_items():
            return [(i, h) for i in (1, 2, 3, "s") for h in range(NH)]

        G_ITEMS = NH + 2

        def size(q):
            return TP if q < NH else P

        def tiles_of(q):
            return size(q) // P

        def levels_of(q):
            return LEVELS if q < NH else LEVELS - 1

        def level_at(q, l):
            return 2 * LEVELS * (q // 2) + 2 * l + q % 2

        def copies_at(q, l):
            return level_at(q, l) - 2 * (q // 2 + 1)

        def sample_heads(q):
            return slice(4 * (q - NH), 4 * (q - NH) + 4)

        def z_item(at, q):
            if q < NH:
                return gz[:, at + q, 0:TP]
            return gz[:, at + 4 * (q - NH):at + 4 * (q - NH) + 4, TP:T]

        def z_tile(at, q, t):
            if q < NH:
                return gz[:, at + q, t * P:(t + 1) * P]
            return (kdec_s if at == GZ_K else u_s)[:, q - NH, :]

        def as_tiles(ap):
            return ap.rearrange("p (t n) -> p t n", n=P)

        def as_heads(ap):
            return ap.rearrange("p (h n) -> p h n", n=TS)

        steps = [("s", h) for h in range(NH)] + [(c, h) for c in range(CHUNKS) for h in range(NH)]

        @block.sync
        def _(sp):
            sp.dma_start(c_t[:], io["c_t"]).then_inc(in_loaded, 16)
            sp.dma_start(ada_b[:], io["ada_b"]).then_inc(in_loaded, 16)
            sp.dma_start(g_pre[:], io["g_pre"]).then_inc(in_loaded, 16)
            sp.dma_start(g_post[:], io["g_post"]).then_inc(in_loaded, 16)
            sp.dma_start(x[:], io["x_t"].rearrange("(k p) t -> p k t", p=P)).then_inc(in_loaded, 16)
            sp.dma_start(ident[:], io["ident"]).then_inc(in_loaded, 16)
            for name, to in (("rel_bias", rel_sb), ("diag_mask", diag_mask), ("tail_mask", tail_mask), ("sel", sel),
                             ("b_f", b_f), ("norm_col", norm_col)):
                sp.dma_start(to[:], io[name]).then_inc(in_loaded, 16)
            sp.dma_start(eps_col[:], io["eps"]).then_inc(in_loaded, 16)
            for s in range(2):
                sp.dma_start(raw[:, s], io["w_stream"][s]).then_inc(w_loaded[s], 16)
            with sp.Fori(1, PAIRS // 2) as i:
                for s in range(2):
                    sp.wait_ge(w_split, 4 * i - 2 + 2 * s)
                    sp.dma_start(raw[:, s], io["w_stream"][2 * i + s]).then_inc(w_loaded[s], 16)
            sp.wait_ge(x_ready, KD * LAYERS * SUBS)
            sp.dma_start(io["y_t"].rearrange("(k p) t -> p k t", p=P), x[:]).then_inc(out_stored, 16)
            sp.wait_ge(out_stored, 16)
            sp.wait_ge(state_stored, 16 * 10)

        @block.gpsimd
        def _(pool):
            pool.wait_ge(consts, 1)

            def split_unit(s, u, n):
                pool.tensor_tensor(w_hi[:, u], raw[:, s, u], one_col[:].broadcast_to([P, D]), ALU.mult)\
                    .then_inc(w_rounded, 1)
                pool.wait_ge(w_rounded, n + 1)
                pool.tensor_tensor(w_lo[:, u], raw[:, s, u], w_hi[:, u].bitcast(F32), ALU.subtract)\
                    .then_inc(w_split, 1)

            for s in range(2):
                pool.wait_ge(w_loaded[s], 16)
                for u in range(2):
                    if s:
                        pool.wait_ge(unit_done, u + 1)
                    split_unit(s, u, 2 * s + u)
            with pool.Fori(1, PAIRS // 2) as i:
                for s in range(2):
                    for u in range(2):
                        pool.wait_ge(w_loaded[s], 16 * i + 16)
                        pool.wait_ge(unit_done, 4 * i + 2 * s + u - 1)
                        split_unit(s, u, 4 * i + 2 * s + u)

        @block.tensor
        def _(pe):
            def ada_step(c, k, groups):
                pe.wait_ge(ada_loaded[k], 16 * (c + 1))
                for j in range(groups):
                    mm = pe.matmul(psum[32 * j:32 * j + 2, 6, 0:ADA_W], c_t[:, k, :],
                                   ada_w[:, k, j * ADA_W:(j + 1) * ADA_W], start=(k == 0), stop=(k == KD - 1),
                                   tile_position=(0, 32 * j))
                mm.then_inc(ada_used, 1)

            def ada_turn(c):
                pe.wait_ge(ada_rows_ready, c + 1)
                for t in range(ADA_W // P):
                    mm = pe.transpose(psum[:, 7, t * P:(t + 1) * P], ada_rows[:, t * P:(t + 1) * P], ident[:])
                mm.then_inc(ada_turned, 1)

            def unit(u, n, hi, lo, ready=None, tail_ready=None):
                pe.wait_ge(w_split, 2 * n + u + 1)
                pe.wait_ge(bank_free[u], n + 1)
                for k in range(KD):
                    if ready:
                        ready(k)
                    for b in range(2):
                        w = slice(k * P, (k + 1) * P)
                        t = slice(b * HT, (b + 1) * HT)
                        for i, (a, m) in enumerate(((w_hi, hi), (w_hi, lo), (w_lo, hi))):
                            mm = pe.matmul(psum[:, 2 * u + b, 0:HT], a[:, u, w], m[:, k, t],
                                           start=(k == 0 and i == 0), stop=(k == KD - 1 and i == 2))
                mm.then_inc(unit_done, 1)

            def norm_sum(n):
                for k in range(KD):
                    pe.wait_ge(sq_ready, KD * n + k + 1)
                    for b in range(2):
                        mm = pe.matmul(psum[:, 4 + b, 0:HT], ones[:], sq[:, k % 2, b * HT:(b + 1) * HT],
                                       start=(k == 0), stop=(k == KD - 1))
                    mm.then_inc(sq_summed, 1)

            def ffn(f, n0, n_pre):
                with pe.Fori(0, KB) as kb:
                    first = n0 + kb * (FFN_PAIRS // KB)
                    chunk = ADA_CHUNKS_BEFORE[f] + kb

                    def gate_up(j):
                        unit(0, first + j, h_hi, h_lo, lambda k: pe.wait_ge(h_ready, KD * n_pre + k + 1))
                        unit(1, first + j, h_hi, h_lo)

                    def down(j):
                        unit(0, first + KD + j, hid_hi, hid_lo,
                             lambda k: pe.wait_ge(hid_ready, KD * (KB * f + kb) + k + 1))
                        unit(1, first + KD + j, hid_hi, hid_lo)

                    if ADA_GROUPS[f]:
                        for j in range(KD):
                            gate_up(j)
                            ada_step(chunk, j, ADA_GROUPS[f])
                        down(0)
                        ada_turn(chunk)
                    else:
                        with pe.Fori(0, KD) as j:
                            gate_up(j)
                        down(0)
                    with pe.Fori(1, KD // 2) as j:
                        down(j)

            pe.wait_ge(c_ready, 1)
            pe.wait_ge(consts, 3)
            for c in range(ADA_HEAD):
                for k in range(KD):
                    ada_step(c, k, 4)
                ada_turn(c)
            norm_sum(0)
            ffn(0, FIRST["ffn0"], 0)
            norm_sum(1)
            norm_sum(2)

            def product(first, pairs, hi, lo, ready=None):
                with pe.Fori(first, first + pairs) as n:
                    unit(0, n, hi, lo, ready)
                    unit(1, n, hi, lo)

            def rel_bias():
                pe.wait_ge(onehot_loaded, 16)
                for b in range(2):
                    mm = pe.matmul(psum[0:NH, 4 + b, 0:REL // 2], rel_sb[:], onehot[0:32, b * (REL // 2):(b + 1) * (REL // 2)],
                                   start=True, stop=True)
                mm.then_inc(rel_made, 1)

            def score_dots(first):
                pe.wait_ge(bank_free[0], first + 2 + 2)
                pe.wait_ge(bank_free[1], first + 2 + 2)
                for i in range(5):
                    n = P if i < 4 else TS
                    mm = pe.transpose(psum[0:n, 6 + i // 4, (i % 4) * P:(i % 4 + 1) * P],
                                      z[:, Z_W, i * P:i * P + n], ident[:])
                mm.then_inc(wi_turned, 1)
                pe.wait_ge(cache_loaded["ik"], 16)
                for e, (i, h) in enumerate(score_items()):
                    r, c = HD * (h % 2), Z_IQ + h // 2
                    if e >= 2:
                        pe.wait_ge(relu_ready, e - 1)
                    b = 4 + 2 * (e % 2)
                    if e < 2:
                        pe.wait_ge(wi_ready, 1)
                    if i == "s":
                        q = z[r:r + HD, c, TP:T]
                        pe.matmul(psum[0:TS, b, 0:HT], q, cache_ik[r:r + HD, 0:HT], start=True, stop=True)
                        pe.matmul(psum[0:TS, b + 1, 0:TP - HT], q, cache_ik[r:r + HD, HT:TP], start=True, stop=True)
                        mm = pe.matmul(psum[0:TS, b + 1, TP - HT:HT], q, z[r:r + HD, Z_IK, TP:T], start=True, stop=True)
                    else:
                        mm = pe.matmul(psum[:, b, 0:keys_of(i)], z[r:r + HD, c, i * P:(i + 1) * P],
                                       z[r:r + HD, Z_IK, 0:keys_of(i)], start=True, stop=True)
                    mm.then_inc(dots_done, 1)

            def turn_values(mixer, first):
                zv = Z_VA if mixer == "A" else Z_VB
                for b in range(5):
                    c = 5 * (mixer == "B") + b
                    n = P if b < 4 else TS
                    if c >= 2:
                        pe.wait_ge(v_ready, c - 1)
                    for d in range(4):
                        mm = pe.transpose(psum[0:n, 4 + c % 2, d * P:(d + 1) * P], z[:, zv + d, b * P:b * P + n], ident[:])
                    mm.then_inc(v_turned, 1)

            def logits(e):
                mixer, i, h = items[e]
                zq, zk = (Z_QA, Z_KA) if mixer == "A" else (Z_QB, Z_KB)
                b = 2 * (e % 2)
                if e >= 2:
                    pe.wait_ge(max_ready, e - 1)
                if i != "s":
                    n, r, c = keys_of(i), HD * (h % 2), h // 2
                    pe.matmul(psum[:, b, 0:n], z[r:r + HD, zq + c, i * P:(i + 1) * P], z[r:r + HD, zk + c, 0:n],
                              start=True, stop=False, skip_group_check=(mixer == "B"))
                    if mixer == "A":
                        mm = pe.matmul(psum[:, b, 0:n], ident[:], bias_p[:, h, TP - P * i:TP - P * i + n],
                                       start=False, stop=True)
                    else:
                        pe.wait_ge(fox_ready, i + 1)
                        pe.matmul(psum[:, b, n - P:n], ident[:], diag_mask[:], start=False, stop=False,
                                  skip_group_check=True)
                        mm = pe.matmul(psum[:, b, 0:n], fox_q[:, h, :], fox_k[:, 0:n], start=False, stop=True,
                                       skip_group_check=True)
                else:
                    r = HD * h
                    for j in range(4):
                        q = z[r:r + HD, zq + j, TP:T]
                        rows = slice(TS * j, TS * (j + 1))
                        pe.matmul(psum[rows, b, 0:HT], q, cache_k[r:r + HD, j, 0:HT], start=True, stop=False,
                                  tile_position=(r, TS * j), skip_group_check=True)
                        pe.matmul(psum[rows, b + 1, 0:TP - HT], q, cache_k[r:r + HD, j, HT:TP], start=True, stop=False,
                                  tile_position=(r, TS * j), skip_group_check=True)
                        pe.matmul(psum[rows, b + 1, TP - HT:HT], q, z[r:r + HD, zk + j, TP:T], start=False, stop=False,
                                  tile_position=(r, TS * j), skip_group_check=True)
                    if mixer == "B":
                        pe.matmul(psum[:, b + 1, TP - HT:HT], ident[:], tail_mask[:], start=False, stop=False,
                                  skip_group_check=True)
                    for d in range(2):
                        if mixer == "A":
                            mm = pe.matmul(psum[:, b + d, 0:HT], ident[:], bias_s[:, h, d * HT:(d + 1) * HT],
                                           start=False, stop=True, skip_group_check=True)
                        else:
                            pe.wait_ge(fox_ready, 4)
                            mm = pe.matmul(psum[:, b + d, 0:HT], fox_qs[:, h, :], fox_k[:, TP + d * HT:TP + (d + 1) * HT],
                                           start=False, stop=True, skip_group_check=True)
                mm.then_inc(logits_done, 1)

            def turn_probs(e):
                _, i, _ = items[e]
                pe.wait_ge(p_ready, e + 1)
                if e >= 2:
                    pe.wait_ge(p_turn_ready, e - 1)
                for k in range(min(keys_of(i) // P, 4)):
                    mm = pe.transpose(psum[:, 4 + e % 2, k * P:(k + 1) * P], probs[:, e % 2, k * P:(k + 1) * P], ident[:])
                if i == "s":
                    pe.wait_ge(o_ready, group_of[e] - 1)
                    pe.wait_ge(p_turn_ready, e)
                    mm = pe.transpose(psum[0:TS, 6 + group_of[e] % 2, P:2 * P], probs[:, e % 2, TP:NK_S], ident[:])
                mm.then_inc(p_turn_done, 1)

            def values(e):
                mixer, i, h = items[e]
                pe.wait_ge(p_turn_ready, e + 1)
                g = group_of[e]
                if i == "s" and h == 0:
                    pe.wait_ge(p_turn_ready, e + 2)
                if g >= 2:
                    pe.wait_ge(o_ready, g - 1)
                o = 6 + g % 2
                if i != "s":
                    for k in range(i + 1):
                        mm = pe.matmul(psum[HD * (h % 2):HD * (h % 2) + HD, o, 0:P], v_tok[:, k, HD * h:HD * h + HD],
                                       p_turned[:, e % 2, k, :], start=(k == 0), stop=(k == i),
                                       tile_position=(0, HD * (h % 2)))
                else:
                    for j in range(4):
                        d = HD * (2 * j + h)
                        for k in range(5):
                            n = P if k < 4 else TS
                            mm = pe.matmul(psum[HD * h:HD * h + HD, o, TS * j:TS * (j + 1)],
                                           cache_v[0:n, k, d:d + HD], p_turned[0:n, e % 2, k, TS * j:TS * (j + 1)],
                                           start=(k == 0), stop=(k == 4), tile_position=(0, HD * h))
                mm.then_inc(av_done, 1)

            def attention(mixer):
                e0 = first_item[mixer]
                for s in range(e0, e0 + n_items + 3):
                    if s < e0 + n_items:
                        logits(s)
                    if e0 <= s - 2 < e0 + n_items:
                        turn_probs(s - 2)
                    if e0 <= s - 3:
                        values(s - 3)

            n0 = FIRST["ab_in"]
            rel_bias()
            product(n0, 3, h_hi, h_lo, lambda k: pe.wait_ge(h_ready, KD + k + 1))
            score_dots(n0)
            product(n0 + 3, AB_PAIRS - 3, h_hi, h_lo)
            for u in range(2):
                pe.wait_ge(bank_free[u], n0 + AB_PAIRS + 1)
            turn_values("A", n0)
            pe.wait_ge(bias_loaded, 16)
            pe.wait_ge(bias_s_loaded, 16 * NH)
            pe.wait_ge(cache_loaded["A"], 32)
            attention("A")
            pe.wait_ge(p_turn_ready, n_items)
            turn_values("B", n0)
            pe.wait_ge(cache_loaded["B"], 32)
            attention("B")
            product(FIRST["ab_out"], OUT_PAIRS, h_hi, h_lo, lambda k: pe.wait_ge(o_ready, len(items) // 2))
            norm_sum(3)
            norm_sum(4)
            ffn(1, FIRST["ffn1"], 2)
            norm_sum(5)
            norm_sum(6)
            ffn(2, FIRST["ffn2"], 3)
            norm_sum(7)
            norm_sum(8)

            def squared_lengths(m):
                pe.wait_ge(conv_sq_ready, m + 1)
                h = m % NH
                at = NH - 1 - h
                pe.matmul(psum[:, 4, :], strips[:, m // NH, at:at + P], conv_sq[:, m % 2, :], start=(m == 0),
                          stop=(m == 2 * NH - 1)).then_inc(lens_summed, 1)

            def gdn_in():
                n0 = FIRST["gdn_in"]
                pe.wait_ge(gdn_loaded, 16 * 5)
                for p in range(GDN_PAIRS):
                    unit(0, n0 + p, h_hi, h_lo, lambda k: pe.wait_ge(h_ready, KD * 4 + k + 1))
                    unit(1, n0 + p, h_hi, h_lo)
                    for m in (2 * p - 6, 2 * p - 5):
                        if 0 <= m < 2 * NH:
                            squared_lengths(m)
                pe.wait_ge(sample_silu, 2)
                for m in range(2 * NH):
                    at = NH - 1 - m % NH
                    mm = pe.matmul(psum[:, 5, 0:TS], strips[:, m // NH, at:at + P], conv_tap[:, m, :], start=(m == 0),
                                   stop=(m == 2 * NH - 1))
                mm.then_inc(lens_summed, 1)

            def turn_rows():
                pe.wait_ge(rows_exp, 2)
                for t in range(TILES):
                    pe.transpose(psum[:, 6, t * P:(t + 1) * P], rows_e[:, t * P:(t + 1) * P], ident[:])
                pe.transpose(psum[:, 7, 0:P], rows_es, ident[:])
                pe.wait_ge(ends_ready, 2)
                pe.matmul(psum[:, 7, P:P + (CHUNKS + 1) * NH], ones[:], ends_by_head.rearrange("p c h -> p (c h)"),
                          start=True, stop=True).then_inc(rows_turned, 1)

            def gdn_products(q):
                u, b = q % 2, 4 * (q % 2)
                n = size(q)
                pe.wait_ge(lq_ready, q + 1)
                if q >= 2:
                    pe.wait_ge(inv_ready, level_at(q - 2, levels_of(q - 2) - 1) + 1)
                    pe.wait_ge(wu_out, q - 1)
                kc = (lambda t: rows_c[:, t * P:(t + 1) * P]) if q < NH else (lambda t: keys_s)
                for w, (at, lq, done) in enumerate(((GZ_K, k_beta, kk_done), (GZ_Q, v_beta, kq_done))):
                    for t in range(tiles_of(q)):
                        moving = gz[:, at + q, t * P:(t + 1) * P] if q < NH else z_item(at, q)
                        pe.matmul(psum[:, b + 2 * w, t * P:(t + 1) * P], z_tile(GZ_K, q, t), moving,
                                  start=True, stop=True)
                    pe.matmul(psum[:, b + 2 * w + 1, 0:n], ident[:],
                              g_mask[:, w + (2 if q >= NH else 0), :].unsqueeze(1).broadcast_to([P, tiles_of(q), P]),
                              start=True, stop=False, skip_group_check=True)
                    for t in range(tiles_of(q)):
                        l = lq[:, u, t * P:(t + 1) * P]
                        lhs, rhs = (l, kc(t)) if w == 0 else (kc(t), l)
                        mm = pe.matmul(psum[:, b + 2 * w + 1, t * P:(t + 1) * P], lhs, rhs,
                                       start=False, stop=True, skip_group_check=True)
                    mm.then_inc(done, 1)

            def gdn_turns(q):
                b = 4 * (q % 2)
                pe.wait_ge(kk_decayed, q + 1)
                for at, bank, done in ((GZ_K, b, k_turned), (GZ_V, b + 1, v_turned_g)):
                    for t in range(tiles_of(q)):
                        mm = pe.transpose(psum[:, bank, t * P:(t + 1) * P], z_tile(at, q, t), ident[:])
                    mm.then_inc(done, 1)
                pe.wait_ge(kq_decayed, q + 1)
                pe.wait_ge(bc_ready, q + 1)
                pe.matmul(psum[:, b + 2, 0:size(q)], ones[:], v_beta[:, q % 2, 0:size(q)], start=True, stop=True)\
                    .then_inc(q_factor, 1)

            def gdn_level(q, l):
                u, b = q % 2, 4 * (q % 2)
                tiles = [slice(t * P, (t + 1) * P) for t in range(tiles_of(q))]
                pe.wait_ge(low_ready, level_at(q, l) + 1)
                if l == 0:
                    pe.wait_ge(kq_exp, q + 1)
                    for t in tiles:
                        mm = pe.transpose(psum[:, b + 3, t], low_m[:, u, t], ident[:])
                    mm.then_inc(t2_made, 1)
                    return
                pe.wait_ge(inv_ready, level_at(q, l - 1) + 1)
                for t in tiles:
                    mm = pe.matmul(psum[:, b + 3, t], low_m[:, u, t], inv_t[:, u, t], start=True, stop=True)
                mm.then_inc(t2_made, 1)

            def gdn_level_ends(q, l):
                u, b = q % 2, 4 * (q % 2)
                tiles = [slice(t * P, (t + 1) * P) for t in range(tiles_of(q))]
                pe.wait_ge(t2_copied, copies_at(q, l) + 1)
                if l == 1:
                    pe.wait_ge(kv_scaled, q + 1)
                for t in tiles:
                    mm = pe.matmul(psum[:, b, t], inv[:, u, t], t2[:, u, t], start=True, stop=True)
                if l < levels_of(q) - 1:
                    for t in tiles:
                        mm = pe.matmul(psum[:, b + 1, t], t2[:, u, t], inv[:, u, t], start=True, stop=True)
                mm.then_inc(e_made, 1)

            def gdn_solved(q):
                u, b = q % 2, 4 * (q % 2)
                pe.wait_ge(inv_ready, level_at(q, levels_of(q) - 1) + 1)
                for w in range(2):
                    for t in range(tiles_of(q)):
                        t = slice(t * P, (t + 1) * P)
                        lhs, rhs = (k_beta[:, u, t], inv_t[:, u, t]) if w == 0 else (inv_t[:, u, t], v_beta[:, u, t])
                        mm = pe.matmul(psum[:, b + 2 + w, t], lhs, rhs, start=True, stop=True)
                mm.then_inc(wu_made, 1)

            def recur_v(n):
                c, h = steps[n]
                if n >= 2:
                    pe.wait_ge(v_new_ready, n - 1)
                if n >= 2 * NH:
                    pe.wait_ge(state_new, n - NH + 1)
                m, r, state = (TS, TS * (h % 4), state_s) if c == "s" else (CHUNK, CHUNK * (c % 2), state_p)
                t = slice(TP, T) if c == "s" else slice(CHUNK * c, CHUNK * (c + 1))
                pe.matmul(psum[r:r + m, n % 2, 0:P], w_neg[:, h, t], state[:, h, :], start=True, stop=True,
                          tile_position=(0, r)).then_inc(v_made, 1)

            def recur_os(n):
                c, h = steps[n]
                pe.wait_ge(v_new_ready, n + 1)
                if n >= 2:
                    pe.wait_ge(o_out, n - 1)
                    pe.wait_ge(state_new, n - 1)
                m, r, state = (TS, TS * (h % 4), state_s) if c == "s" else (CHUNK, CHUNK * (c % 2), state_p)
                t = slice(TP, T) if c == "s" else slice(CHUNK * c, CHUNK * (c + 1))
                qk = qk_s[r:r + m, h // 4, r:r + m] if c == "s" else qk_t[r:r + m, h, t]
                kd = kdec_s[r:r + m, h // 4, :] if c == "s" else gz[r:r + m, GZ_K + h, c // 2 * P:(c // 2 + 1) * P]
                v = v_new[r:r + m, n % 2, :]
                pe.matmul(psum[:, 2 + n % 2, 0:m], state[:, h, :], gz[:, GZ_Q + h, t], start=True, stop=False)
                pe.matmul(psum[:, 2 + n % 2, 0:m], v, qk, start=False, stop=True, tile_position=(r, 0))\
                    .then_inc(o_made, 1)
                pe.matmul(psum[:, 4 + n % 2, 0:P], kd, v, start=True, stop=True, tile_position=(r, 0))\
                    .then_inc(kv_made, 1)

            def gated_norm_sums():
                pe.wait_ge(state_new, len(steps))
                for h in range(NH):
                    pe.wait_ge(g_sq_ready, h + 1)
                    if h >= 2:
                        pe.wait_ge(g_ln_done, h - 1)
                    for b in range(2):
                        mm = pe.matmul(psum[:, 4 + 2 * (h % 2) + b, 0:HT], ones[:], g_sq[:, h % 2, b * HT:(b + 1) * HT],
                                       start=True, stop=True)
                    mm.then_inc(g_sq_summed, 1)

            gdn_in()
            turn_rows()
            pe.wait_ge(gdn_masks, 16)
            pe.wait_ge(cols_ready, 1)
            for q0 in range(0, G_ITEMS, 2):
                pair = (q0, q0 + 1)
                for step in (gdn_products, gdn_turns):
                    for q in pair:
                        step(q)
                for l in range(levels_of(q0)):
                    for q in pair:
                        gdn_level(q, l)
                    if l:
                        for q in pair:
                            gdn_level_ends(q, l)
                for q in pair:
                    gdn_solved(q)
            pe.wait_ge(wu_out, G_ITEMS)
            pe.wait_ge(gdn_state, 16)
            for n in range(len(steps) + 2):
                if n < len(steps):
                    recur_v(n)
                if n >= 2:
                    recur_os(n - 2)
            gated_norm_sums()
            product(FIRST["gdn_out"], OUT_PAIRS, h_hi, h_lo, lambda k: pe.wait_ge(g_ready, k + 1))
            norm_sum(9)
            norm_sum(10)
            ffn(3, FIRST["ffn3"], 5)
            norm_sum(11)


        @block.scalar
        def _(act):
            def squares(n, src, ready=None):
                for k in range(KD):
                    if ready:
                        ready(k)
                    if KD * n + k >= 2:
                        act.wait_ge(sq_summed, KD * n + k - 1)
                    act.activation(sq[:, k % 2], src[:, k], ACT.Square).then_inc(sq_ready, 1)

            def y_evacuated(n0, k):
                act.wait_ge(bank_free[k % 2], n0 + FFN_PAIRS - KD // 2 + k // 2 + 2)

            def rsqrt_mean(n):
                act.wait_ge(sq_summed, KD * (n + 1))
                act.activation(split(lnv), halves(4), ACT.Ln, bias=eps_col[:], scale=1.0 / D).then_inc(ln_done, 1)
                act.wait_ge(ln_done, n + 1)
                act.activation(rstd, lnv, ACT.Exp, scale=-0.5).then_inc(rstd_ready, 1)

            def modulate(n, sub):
                for k in range(KD):
                    act.wait_ge(scaled, KD * n + k + 1)
                    if KD * n + k >= 2:
                        act.wait_ge(h_ready, KD * n + k - 1)
                    for g, (a, b) in enumerate(GROUPS):
                        op = act.activation(h32[:, k % 2, a:b], tmp[:, k % 2, a:b], ACT.Identity,
                                            scale=scale_in[:, sub, k, g:g + 1],
                                            bias=mod[:, (sub * 3) * KD + k, g:g + 1])
                    op.then_inc(h32_ready, 1)

            def ada_load(c, k, half, halves_in):
                act.wait_ge(ada_used, KD * (c - 1) + k + 1)
                act.dma_start(ada_w[:, k, 0:halves_in * ADA_HALF].rearrange("p (h n) -> p h n", h=halves_in),
                              io["ada_w"][bass.ds(half, halves_in), k].rearrange("h p n -> p h n"))\
                    .then_inc(ada_loaded[k], 16)

            def ffn(f, n0):
                with act.Fori(0, KB) as kb:
                    for j in range(KD):
                        if ADA_GROUPS[f]:
                            g = ADA_GROUPS[f] // 2
                            ada_load(ADA_CHUNKS_BEFORE[f] + kb, j, ADA_FIRST_HALF[f] + kb * g, g)
                        n = n0 + kb * (3 * KD // 2) + j
                        act.wait_ge(unit_done, 2 * n + 1)
                        act.activation(split(silu[:, j % 2]), halves(0), ACT.Silu).then_inc(bank_free[0], 1)

            act.wait_ge(in_loaded, 16 * N_IN)
            act.activation(c_t[:], c_t[:], ACT.Silu).then_inc(c_ready, 1)
            for k in range(KD):
                act.dma_start(ada_w[:, k].rearrange("p (h n) -> p h n", h=2),
                              io["ada_w"][0:2, k].rearrange("h p n -> p h n")).then_inc(ada_loaded[k], 16)
            for c in range(1, ADA_HEAD):
                for k in range(KD):
                    ada_load(c, k, 2 * c, 2)
            squares(0, x)
            rsqrt_mean(0)
            modulate(0, 0)
            ffn(0, FIRST["ffn0"])
            squares(1, y, lambda k: y_evacuated(FIRST["ffn0"], k))
            rsqrt_mean(1)
            squares(2, x, lambda k: act.wait_ge(x_ready, k + 1))
            rsqrt_mean(2)
            modulate(1, 1)

            def z_out(n0, m, scale=1.0):
                act.wait_ge(unit_done, 2 * n0 + m + 1)
                act.activation(split(z[:, m]), halves(2 * (m % 2)), ACT.Copy, scale=scale)\
                    .then_inc(bank_free[m % 2], 1)

            def store(name, src):
                act.dma_start(io[name].rearrange("(k p) t -> p k t", p=P), src).then_inc(state_stored, 16)

            def spread_rel():
                act.wait_ge(rel_made, 1)
                for b in range(2):
                    op = act.activation(fb[0:NH, b * (REL // 2):(b + 1) * (REL // 2)], psum[0:NH, 4 + b, 0:REL // 2], ACT.Copy)
                op.then_inc(rel_copied, 1)
                act.wait_ge(rel_copied, 1)
                act.dma_start(bass.AP(io["rel_spread"].tensor, 0, [[REL_AT, NH], [REL + 1, P], [1, REL]]),
                              fb[0:NH, :].unsqueeze(1).broadcast_to([NH, P, REL])).then_inc(rel_spread, 16)

            def load_biases():
                act.wait_ge(rel_spread, 16)
                act.dma_start(bias_p, bass.AP(io["rel_spread"].tensor, P - 1, [[REL, P], [REL_AT, NH], [1, 5 * P]]))\
                    .then_inc(bias_loaded, 16)

            def load_sample_biases():
                act.wait_ge(score_added, 4 * NH)
                for h in range(NH):
                    act.dma_start(bias_s[TS * (h // 2):TS * (h // 2 + 1), h % 2, :],
                                  bass.AP(io["rel_spread"].tensor, h * REL_AT + P - 1, [[REL, TS], [1, NK_S]]))\
                        .then_inc(bias_s_loaded, 16)

            def load_cache(mixer):
                act.dma_start(cache_k, io[f"cache_{mixer}_k"].rearrange("(k p) t -> p k t", p=P))\
                    .then_inc(cache_loaded[mixer], 16)
                act.dma_start(cache_v[:, 0:4, :], io[f"cache_{mixer}_v"].rearrange("(b p) d -> p b d", p=P))\
                    .then_inc(cache_loaded[mixer], 16)

            def relus():
                act.wait_ge(wi_turned, 1)
                act.activation(wi_tok[:, 0:4, :], psum[:, 6, :].rearrange("p (i r) -> p i r", r=P)[:, :, 0:NH],
                               ACT.Copy, scale=NH ** -0.5)
                act.activation(wi_tok[0:TS, 4, :], psum[0:TS, 7, 0:NH], ACT.Copy, scale=NH ** -0.5).then_inc(wi_ready, 1)
                for e, (i, h) in enumerate(score_items()):
                    act.wait_ge(dots_done, e + 1)
                    if e >= 2:
                        act.wait_ge(score_added, e - 1)
                    b = 4 + 2 * (e % 2)
                    if i == "s":
                        op = act.activation(split(relu[0:TS, e % 2]), psum[0:TS, b:b + 2, 0:HT], ACT.Relu)
                    else:
                        op = act.activation(relu[:, e % 2, 0:keys_of(i)], psum[:, b, 0:keys_of(i)], ACT.Relu)
                    op.then_inc(relu_ready, 1)

            def values_out(mixer):
                for b in range(5):
                    c = 5 * (mixer == "B") + b
                    act.wait_ge(v_turned, c + 1)
                    if b < 4:
                        op = act.activation(v_tok[:, b, :], psum[:, 4 + c % 2, :], ACT.Copy)
                    else:
                        op = act.activation(cache_v[0:TS, 4, :], psum[0:TS, 4 + c % 2, :], ACT.Copy)
                    op.then_inc(v_ready, 1)

            def exps(e):
                _, i, _ = items[e]
                n = keys_of(i)
                act.wait_ge(max_ready, e + 1)
                if e >= 2:
                    act.wait_ge(p_turn_done, e - 1)
                act.activation(probs[:, e % 2, 0:n], neg_logits[:, e % 2, 0:n], ACT.Exp, scale=-1.0,
                               bias=neg_max[:, e % 2:e % 2 + 1], accum_out=p_sum[:, e % 2:e % 2 + 1])\
                    .then_inc(exp_done, 1)

            def probs_out(e):
                _, i, _ = items[e]
                act.wait_ge(p_turn_done, e + 1)
                if e >= 2:
                    act.wait_ge(av_done, e - 1)
                k = min(keys_of(i) // P, 4)
                op = act.activation(p_turned[:, e % 2, 0:k, :].rearrange("p k q -> p (k q)"),
                                    psum[:, 4 + e % 2, 0:k * P], ACT.Copy)
                if i == "s":
                    op = act.activation(p_turned[0:TS, e % 2, 4, :], psum[0:TS, 6 + group_of[e] % 2, P:2 * P],
                                        ACT.Copy)
                op.then_inc(p_turn_ready, 1)

            def attention(mixer):
                e0 = first_item[mixer]
                for s in range(e0, e0 + n_items + 2):
                    if s < e0 + n_items:
                        exps(s)
                    if e0 <= s - 2:
                        probs_out(s - 2)

            def forget_logs():
                r = slice(FOX_ROW, FOX_ROW + NH)
                v, a, ex, ln = (fox_w[r, k, :] for k in range(4))
                steps = ((v, z[r, Z_W, :], ACT.Identity, dict(bias=b_f[r, :])), (a, v, ACT.Abs, {}),
                         (ex, a, ACT.Exp, dict(scale=-1.0)), (ln, ex, ACT.Ln, dict(bias=one_col[r, :])))
                for k, (to, of, func, how) in enumerate(steps):
                    act.activation(to, of, func, **how).then_inc(fox_own, 1)
                    act.wait_ge(fox_own, k + 1)

            n0 = FIRST["ab_in"]
            act.dma_start(onehot[0:32, :], io["onehot"]).then_inc(onehot_loaded, 16)
            spread_rel()
            act.dma_start(cache_ik, io["cache_ik"]).then_inc(cache_loaded["ik"], 16)
            load_cache("A")
            load_biases()
            for m in range(6):
                z_out(n0, m, HD ** -0.5 if Z_IQ <= m < Z_KA else 1.0)
            relus()
            load_sample_biases()
            for m in range(6, Z_TILES):
                z_out(n0, m, HD ** -0.5 if Z_QA <= m < Z_VA or Z_QB <= m < Z_VB else 1.0)
            for u in range(2):
                act.wait_ge(bank_free[u], n0 + AB_PAIRS + 1)
            store("a_k", z[:, Z_KA:Z_KA + 4])
            store("a_v", z[:, Z_VA:Z_VA + 4])
            store("b_k", z[:, Z_KB:Z_KB + 4])
            store("b_v", z[:, Z_VB:Z_VB + 4])
            act.dma_start(io["a_ik"], z[0:HD, Z_IK, :]).then_inc(state_stored, 16)
            values_out("A")
            attention("A")
            act.wait_ge(av_done, n_items)
            load_cache("B")
            act.dma_start(fox_f[FOX_ROW:FOX_ROW + NH, TP:2 * TP], io["cache_logf"]).then_inc(fox_loaded, 16)
            act.wait_ge(state_stored, 16 * 5)
            forget_logs()
            values_out("B")
            attention("B")
            act.wait_ge(fox_copied, 6)
            act.dma_start(io["b_logf"], fox_w[FOX_ROW:FOX_ROW + NH, 0, :]).then_inc(state_stored, 16)
            act.wait_ge(state_stored, 16 * 6)
            squares(3, y, lambda k: act.wait_ge(bank_free[k % 2], FIRST["ab_out"] + k // 2 + 2))
            rsqrt_mean(3)

            def pre_norm(n, norm):
                squares(norm, x, lambda k: act.wait_ge(x_ready, KD * (n - 1) + k + 1))
                rsqrt_mean(norm)
                modulate(n, n)

            def feed_forward(f, n, norm, name):
                pre_norm(n, norm)
                ffn(f, FIRST[name])
                squares(norm + 1, y, lambda k: y_evacuated(FIRST[name], k))
                rsqrt_mean(norm + 1)

            feed_forward(1, 2, 4, "ffn1")
            feed_forward(2, 3, 6, "ffn2")
            pre_norm(4, 8)

            n0 = FIRST["gdn_in"]
            done = [0]

            def in_turn(ins):
                done[0] += 1
                ins.then_inc(row_own, 1)
                act.wait_ge(row_own, done[0])

            def one_plus_exp(v, to):
                in_turn(act.activation(to, v, ACT.Abs))
                in_turn(act.activation(to, to, ACT.Exp, scale=-1.0))
                act.activation(to, to, ACT.Ln, bias=one_col[:]).then_inc(rows_lin, 1)

            def conv_load(m):
                act.wait_ge(unit_done, 2 * n0 + m + 3)
                if m >= 2:
                    act.wait_ge(conv_done, m - 1)
                b = 2 * (m % 2)
                act.activation(split(conv_in[:, m % 2, CW - 1:]), halves(b), ACT.Copy)
                act.activation(conv_s[:, m, CW - 1:], psum[:, b + 1, HT - TS:HT], ACT.Copy)\
                    .then_inc(bank_free[m % 2], 1)

            def conv_store(m):
                act.wait_ge(conv_done, m + 1)
                act.activation(gz[:, m, 0:TP], conv_acc[:, m % 2], ACT.Silu).then_inc(conv_silu, 1)
                if m < 2 * NH:
                    act.wait_ge(conv_silu, m + 1)
                    if m >= 2:
                        act.wait_ge(lens_summed, m - 1)
                    act.activation(conv_sq[:, m % 2], gz[:, m, 0:TP], ACT.Square).then_inc(conv_sq_ready, 1)

            def gate_out_silu(j):
                m = QKV + j
                act.wait_ge(unit_done, 2 * n0 + m + 3)
                act.activation(split(gz[:, GZ_G + j]), halves(2 * (m % 2)), ACT.Silu).then_inc(bank_free[m % 2], 1)

            for name, to in (("strips", strips), ("g_sel", g_sel), ("g_col", g_col), ("conv_w", conv_w),
                             ("conv_before", conv_before)):
                act.dma_start(to, io[name]).then_inc(gdn_loaded, 16)
            act.wait_ge(gdn_loaded, 16 * 5)
            act.wait_ge(unit_done, 2 * n0 + 1)
            act.activation(split(row_a), halves(0), ACT.Identity, bias=g_col[:, 0:1]).then_inc(bank_free[0], 1)
            act.wait_ge(unit_done, 2 * n0 + 2)
            act.activation(split(row_b), halves(2), ACT.Copy).then_inc(bank_free[1], 1)
            act.wait_ge(bank_free[0], n0 + 2)
            act.wait_ge(bank_free[1], n0 + 2)
            one_plus_exp(row_a, row_sp)
            one_plus_exp(row_b, row_lb)
            act.activation(g_col[:, 3:4], g_col[:, 1:2], ACT.Exp).then_inc(rows_lin, 1)
            act.wait_ge(conv_zeroed, 1)
            for m in range(QKV + 1):
                if m < QKV:
                    conv_load(m)
                if m:
                    conv_store(m - 1)
            gate_out_silu(0)
            gate_out_silu(1)
            act.wait_ge(sample_conv, 1)
            act.activation(gz[:, 0:QKV, TP:T], conv_sum, ACT.Silu).then_inc(sample_silu, 1)
            act.wait_ge(sample_silu, 1)
            act.activation(conv_tap[:, 0:2 * NH, :], gz[:, 0:2 * NH, TP:T], ACT.Square).then_inc(sample_silu, 1)
            for j in range(2, NH):
                gate_out_silu(j)
            act.wait_ge(conv_done, QKV + 1)
            act.dma_start(io["p_conv"].rearrange("(k p) j -> p k j", p=P), conv_last).then_inc(state_stored, 16)
            act.dma_start(io["s_conv"].rearrange("(k p) j -> p k j", p=P), conv_s[:, :, TS:]).then_inc(state_stored, 16)
            act.wait_ge(lens_summed, 2 * NH + 1)
            act.dma_start(g_mask, io["g_mask"]).then_inc(gdn_masks, 16)
            act.dma_start(state_s, io["state_rec"].rearrange("h d e -> d h e")).then_inc(gdn_state, 16)
            act.activation(row_lr[:, 0:TP], psum[:, 4, :], ACT.Ln, bias=eps_col[:])
            act.activation(row_lr[:, TP:T], psum[:, 5, 0:TS], ACT.Ln, bias=eps_col[:]).then_inc(lens_ln, 1)
            act.wait_ge(rows_ready, 2)
            act.activation(rows_es.rearrange("p (h n) -> p h n", n=TS), rows_e[:, TP:T].unsqueeze(1)
                           .broadcast_to([P, 4, TS]), ACT.Exp)
            act.activation(ends, ends, ACT.Exp).then_inc(rows_exp, 1)
            act.activation(rows_e[:, 0:TP], rows_e[:, 0:TP], ACT.Exp).then_inc(rows_exp, 1)
            for to, at in ((kdec_s, GZ_K), (u_s, GZ_V)):
                act.activation(to.rearrange("p g (j n) -> p (g j) n", n=TS), gz[:, at:at + NH, TP:T], ACT.Copy)
            act.activation(keys_s.rearrange("p (h n) -> p h n", n=TS), rows_c[:, TP:T].unsqueeze(1)
                           .broadcast_to([P, 4, TS]), ACT.Copy).then_inc(rows_exp, 1)
            act.wait_ge(rows_exp, 3)

            def pick(to, of, of_s, kind, q):
                if q < NH:
                    return act.activation(to, of[:, 0:TP], ACT.Copy, scale=g_sel[:, kind, q:q + 1])
                for j in range(4):
                    h = 4 * (q - NH) + j
                    op = act.activation(to[:, j * TS:(j + 1) * TS], of_s, ACT.Copy, scale=g_sel[:, kind, h:h + 1])
                return op

            def gdn_rows(q):
                u, n = q % 2, size(q)
                if q >= 2:
                    act.wait_ge(wu_made, q - 1)
                pick(k_beta[:, u, 0:n], rows_r, rows_r[:, TP:T], 0, q)
                pick(v_beta[:, u, 0:n], rows_r, rows_r[:, TP:T], 1, q).then_inc(lq_ready, 1)

            def gdn_exps(q):
                u, n, b = q % 2, size(q), 4 * (q % 2)
                act.wait_ge(kk_done, q + 1)
                act.activation(t2[:, u, 0:n], psum[:, b + 1, 0:n], ACT.Exp).then_inc(kk_exp, 1)
                act.wait_ge(kq_done, q + 1)
                act.activation(low_m[:, u, 0:n], psum[:, b + 3, 0:n], ACT.Exp).then_inc(kq_exp, 1)
                pick(v_beta[:, u, 0:n], rows_e, rows_es[:, 0:TS], 2, q).then_inc(bc_ready, 1)

            def gdn_copy(q, l):
                u, n, b = q % 2, size(q), 4 * (q % 2)
                act.wait_ge(t2_made, level_at(q, l) + 1)
                act.activation(t2[:, u, 0:n], psum[:, b + 3, 0:n], ACT.Copy).then_inc(t2_copied, 1)

            def gdn_solved(q):
                u, n, b = q % 2, size(q), 4 * (q % 2)
                act.wait_ge(wu_made, q + 1)
                if q < NH:
                    act.activation(w_neg[:, q, 0:TP], psum[:, b + 2, :], ACT.Copy, scale=-1.0)
                    act.activation(gz[:, GZ_V + q, 0:TP], psum[:, b + 3, :], ACT.Copy).then_inc(wu_out, 1)
                else:
                    act.activation(w_neg[:, sample_heads(q), TP:T], as_heads(psum[:, b + 2, 0:P]), ACT.Copy, scale=-1.0)
                    act.activation(u_s[:, q - NH, :], psum[:, b + 3, 0:P], ACT.Copy).then_inc(wu_out, 1)

            act.wait_ge(state_stored, 16 * 8)
            for q0 in range(0, G_ITEMS, 2):
                pair = (q0, q0 + 1)
                for q in pair:
                    gdn_rows(q)
                for q in pair:
                    gdn_exps(q)
                for l in range(1, levels_of(q0)):
                    for q in pair:
                        gdn_copy(q, l)
                for q in pair:
                    gdn_solved(q)
            for n, (c, h) in enumerate(steps):
                m, t = (TS, slice(TP, T)) if c == "s" else (CHUNK, slice(CHUNK * c, CHUNK * (c + 1)))
                act.wait_ge(o_made, n + 1)
                act.activation(gz[:, GZ_Q + h, t], psum[:, 2 + n % 2, 0:m], ACT.Copy).then_inc(o_out, 1)
            act.wait_ge(state_new, len(steps))
            act.dma_start(io["p_rec"].rearrange("h d e -> d h e"), state_p).then_inc(state_stored, 16)
            act.dma_start(io["s_rec"].rearrange("h d e -> d h e"), state_s).then_inc(state_stored, 16)
            act.wait_ge(o_out, len(steps))
            act.wait_ge(state_stored, 16 * 10)
            for h in range(NH + 1):
                if h < NH:
                    if h >= 2:
                        act.wait_ge(g_sq_summed, h - 1)
                    act.activation(g_sq[:, h % 2], gz[:, GZ_Q + h], ACT.Square).then_inc(g_sq_ready, 1)
                if h:
                    e = h - 1
                    act.wait_ge(g_sq_summed, e + 1)
                    act.activation(split(g_ln[:, e % 2]), halves(4 + 2 * (e % 2)), ACT.Ln, bias=eps_col[:],
                                   scale=1.0 / P).then_inc(g_ln_done, 1)
                    act.wait_ge(g_ln_done, e + 1)
                    if e >= 2:
                        act.wait_ge(g_used, e - 1)
                    act.activation(g_rstd[:, e % 2], g_ln[:, e % 2], ACT.Exp, scale=-0.5).then_inc(g_rstd_ready, 1)
            squares(9, y, lambda k: act.wait_ge(bank_free[k % 2], FIRST["gdn_out"] + k // 2 + 2))
            rsqrt_mean(9)
            feed_forward(3, 5, 10, "ffn3")

        @block.vector
        def _(dve):
            own = [0]

            def then(ins):
                own[0] += 1
                ins.then_inc(dve_own, 1)
                dve.wait_ge(dve_own, own[0])

            dve.memset(one_col[:], 1.0).then_inc(consts, 1)
            dve.memset(ada_rows[:], 0.0).then_inc(consts, 1)
            dve.memset(rstd, 0.0).then_inc(bank_free[0], 1)
            dve.memset(lnv, 0.0).then_inc(bank_free[1], 1)
            dve.memset(ones[:], 1.0).then_inc(consts, 1)
            dve.wait_ge(in_loaded, 16 * N_IN)
            dve.wait_ge(consts, 3)

            def ada_copy(c, groups):
                dve.wait_ge(ada_used, KD * (c + 1))
                for j in range(groups):
                    op = dve.tensor_copy(ada_rows[32 * j:32 * j + 2, :], psum[32 * j:32 * j + 2, 6, 0:ADA_W])
                op.then_inc(ada_rows_ready, 1)

            def ada_add(c, at, groups):
                tiles = ADA_W // P
                dve.wait_ge(ada_turned, c + 1)
                for j in range(groups):
                    op = dve.tensor_tensor(mod[:, bass.ds(at + j * tiles, tiles), :],
                                           psum[:, 7, 0:ADA_W].rearrange("p (t r) -> p t r", r=P)
                                           [:, :, 32 * j:32 * j + 2],
                                           ada_b[:, bass.ds(at + j * tiles, tiles)].unsqueeze(2)
                                           .broadcast_to([P, tiles, 2]), ALU.add)
                op.then_inc(ada_added, 1)

            def conditions(s):
                g1 = g_pre[:, s * KD:(s + 1) * KD].unsqueeze(2).broadcast_to([P, KD, 2])
                g2 = g_post[:, s * KD:(s + 1) * KD].unsqueeze(2).broadcast_to([P, KD, 2])
                dve.scalar_tensor_tensor(scale_in[:, s], mod[:, (3 * s + 1) * KD:(3 * s + 2) * KD], 1.0, g1,
                                         ALU.add, ALU.mult).then_inc(cond_ready, 1)
                weight = 1.0 if s % SUBS == 1 else 0.5
                dve.scalar_tensor_tensor(gate_out[:, s], mod[:, (3 * s + 2) * KD:(3 * s + 3) * KD], weight, g2,
                                         ALU.mult, ALU.mult).then_inc(cond_ready, 1)
                dve.wait_ge(cond_ready, 2 * s + 2)

            for c in range(ADA_HEAD):
                ada_copy(c, 4)
                ada_add(c, 12 * c, 4)
            dve.wait_ge(ada_added, ADA_HEAD)
            conditions(0)

            def normalise(n, n_norm):
                dve.wait_ge(rstd_ready, n_norm + 1)
                for k in range(KD + 1):
                    if k < KD:
                        if KD * n + k >= 2:
                            dve.wait_ge(h32_ready, KD * n + k - 1)
                        dve.tensor_tensor(tmp[:, k % 2], x[:, k], rstd, ALU.mult).then_inc(scaled, 1)
                    if k > 0:
                        dve.wait_ge(h32_ready, KD * n + k)
                        dve.tensor_copy(h_hi[:, k - 1], h32[:, (k - 1) % 2]).then_inc(h_rounded, 1)
                        dve.wait_ge(h_rounded, KD * n + k)
                        dve.tensor_tensor(h_lo[:, k - 1], h32[:, (k - 1) % 2], h_hi[:, k - 1].bitcast(F32),
                                          ALU.subtract).then_inc(h_ready, 1)

            def ffn(f, n0):
                then(dve.memset(y, 0.0))
                with dve.Fori(0, KB) as kb:
                    q = KD * (KB * f + kb)
                    for j in range(KD):
                        n = n0 + kb * (3 * KD // 2) + j
                        dve.wait_ge(unit_done, 2 * n + 2)
                        dve.wait_ge(bank_free[0], n + 2)
                        dve.tensor_tensor(split(h32[:, j % 2]), split(silu[:, j % 2]), halves(2), ALU.mult)\
                            .then_inc(bank_free[1], 1)
                        dve.wait_ge(bank_free[1], n + 2)
                        dve.tensor_copy(hid_hi[:, j], h32[:, j % 2]).then_inc(hid_rounded, 1)
                        dve.wait_ge(hid_rounded, q + j + 1)
                        dve.tensor_tensor(hid_lo[:, j], h32[:, j % 2], hid_hi[:, j].bitcast(F32), ALU.subtract)\
                            .then_inc(hid_ready, 1)
                    if ADA_GROUPS[f]:
                        ada_copy(ADA_CHUNKS_BEFORE[f] + kb, ADA_GROUPS[f])
                    for m in range(KD):
                        n = n0 + kb * (3 * KD // 2) + KD + m // 2
                        dve.wait_ge(unit_done, 2 * n + m % 2 + 1)
                        dve.tensor_tensor(split(y[:, m]), split(y[:, m]), halves(2 * (m % 2)), ALU.add)\
                            .then_inc(bank_free[m % 2], 1)
                        if m == 3 and ADA_GROUPS[f]:
                            ada_add(ADA_CHUNKS_BEFORE[f] + kb, 6 * ADA_FIRST_HALF[f] + kb * (3 * ADA_GROUPS[f]),
                                    ADA_GROUPS[f])

            def add_branch(n, sub, n_norm):
                dve.wait_ge(rstd_ready, n_norm + 1)
                for k in range(KD):
                    dve.tensor_tensor(tmp[:, k % 2], y[:, k], rstd, ALU.mult).then_inc(y_scaled, 1)
                    dve.wait_ge(y_scaled, KD * n + k + 1)
                    for g, (a, b) in enumerate(GROUPS):
                        op = dve.scalar_tensor_tensor(x[:, k, a:b], tmp[:, k % 2, a:b],
                                                      gate_out[:, sub, k, g:g + 1], x[:, k, a:b],
                                                      ALU.mult, ALU.add)
                    op.then_inc(x_ready, 1)

            normalise(0, 0)
            ffn(0, FIRST["ffn0"])
            add_branch(0, 0, 1)

            def add_scores():
                dve.wait_ge(wi_ready, 1)
                for e, (i, h) in enumerate(score_items()):
                    n = keys_of(i)
                    rows, w = (TS, 4) if i == "s" else (P, i)
                    dve.wait_ge(relu_ready, e + 1)
                    if h == 0:
                        op = dve.tensor_scalar(scores[i][0:rows], relu[0:rows, e % 2, 0:n], wi_tok[0:rows, w, h:h + 1], None,
                                               ALU.mult)
                    else:
                        dve.wait_ge(score_added, e)
                        op = dve.scalar_tensor_tensor(scores[i][0:rows], relu[0:rows, e % 2, 0:n],
                                                      wi_tok[0:rows, w, h:h + 1], scores[i][0:rows], ALU.mult, ALU.add)
                    op.then_inc(score_added, 1)
                dve.wait_ge(score_added, 4 * NH)

            def choose(i):
                rows, n = (TS, NK_S) if i == "s" else (P, keys_of(i))
                sc = scores[i][0:rows]
                if i != "s":
                    then(dve.memset(scores[i][0:P // 2, n - P // 2:n], NEG))
                for _ in range((TOPK_S if i == "s" else TOPK_P) // 8):
                    then(dve.max(top8[0:rows, :], sc))
                    then(dve.match_replace(sc, top8[0:rows, :], sc, TAKEN))
                then(dve.tensor_scalar(sc, sc, TAKEN / 2, NEG, ALU.is_ge, ALU.mult))

            def masks():
                then(dve.memset(scores[0][:], 0.0))
                then(dve.memset(scores[0][0:P // 2, P // 2:P], NEG))
                for i in (1, 2, 3):
                    choose(i)
                    then(dve.memset(scores[i][0:P // 2, keys_of(i) - P // 2:keys_of(i)], NEG))
                choose("s")
                for j in range(1, 4):
                    op = dve.tensor_copy(scores["s"][TS * j:TS * (j + 1)], scores["s"][0:TS])
                op.then_inc(masks_ready, 1)
                dve.wait_ge(masks_ready, 1)

            def row_max(e):
                mixer, i, h = items[e]
                n, b = keys_of(i), 2 * (e % 2)
                dve.wait_ge(logits_done, e + 1)
                if e >= 2:
                    dve.wait_ge(exp_done, e - 1)
                if i == "s":
                    out, src = split(neg_logits[:, e % 2]), halves(b)
                else:
                    out, src = neg_logits[:, e % 2, 0:n], psum[:, b, 0:n]
                if mixer == "A":
                    mask = split(scores[i]) if i == "s" else scores[i][:, 0:n]
                    op = dve.tensor_tensor_reduce(out, src, mask, -1.0, 3.0e38, ALU.add, ALU.min,
                                                  neg_max[:, e % 2:e % 2 + 1])
                else:
                    op = dve.tensor_scalar(out, src, -1.0, None, ALU.mult, ALU.min,
                                           accum_out=neg_max[:, e % 2:e % 2 + 1])
                op.then_inc(max_ready, 1)

            def normal(e):
                _, i, _ = items[e]
                n = keys_of(i)
                dve.wait_ge(exp_done, e + 1)
                then(dve.reciprocal(p_inv[:, e % 2:e % 2 + 1], p_sum[:, e % 2:e % 2 + 1]))
                dve.tensor_scalar(probs[:, e % 2, 0:n], probs[:, e % 2, 0:n], p_inv[:, e % 2:e % 2 + 1], None,
                                  ALU.mult).then_inc(p_ready, 1)

            def outputs(e):
                mixer, i, h = items[e]
                k0 = 4 * (mixer == "B")
                g = group_of[e]
                dve.wait_ge(av_done, e + 1)
                if i == "s":
                    to, src = (slice(k0, k0 + 4), slice(TP, T)), psum[:, 6 + g % 2, 0:P].rearrange("p (k t) -> p k t", k=4)
                else:
                    to, src = (k0 + h // 2, slice(i * P, (i + 1) * P)), psum[:, 6 + g % 2, 0:P]
                dve.tensor_copy(h_hi[:, to[0], to[1]], src).then_inc(o_rounded, 1)
                dve.wait_ge(o_rounded, g + 1)
                dve.tensor_tensor(h_lo[:, to[0], to[1]], src, h_hi[:, to[0], to[1]].bitcast(F32), ALU.subtract)\
                    .then_inc(o_ready, 1)

            def attention(mixer):
                e0 = first_item[mixer]
                for s in range(e0, e0 + n_items + 4):
                    if s < e0 + n_items:
                        if mixer == "B" and items[s][1] != "s" and items[s][2] == 0:
                            forget_queries(items[s][1])
                        row_max(s)
                    if e0 <= s - 1 < e0 + n_items:
                        normal(s - 1)
                    if e0 <= s - 4 and last_of_group[s - 4]:
                        outputs(s - 4)

            def forget_sums():
                r, r0 = slice(FOX_ROW, FOX_ROW + NH), slice(0, NH)
                dve.wait_ge(fox_own, 4)
                dve.wait_ge(fox_loaded, 16)
                dve.memset(fox_k, 0.0).then_inc(fox_copied, 1)
                then(dve.scalar_tensor_tensor(fox_w[r, 0, :], fox_w[r, 0, :], 0.0, fox_w[r, 3, :], ALU.min, ALU.subtract))
                dve.tensor_copy(fox_f[r, 0:TP], fox_w[r, 0, 0:TP]).then_inc(fox_copied, 1)
                dve.tensor_copy(fox_f[r, 2 * TP:2 * TP + TS], fox_w[r, 0, TP:T]).then_inc(fox_copied, 1)
                dve.memset(fox_keep[r, :], 1.0).then_inc(fox_copied, 1)
                dve.memset(fox_q, 0.0).then_inc(fox_copied, 1)
                dve.memset(fox_qs, 0.0).then_inc(fox_copied, 1)
                dve.wait_ge(fox_copied, 6)
                then(dve.memset(fox_keep[r, TP:TP + 1], 0.0))
                then(dve.tensor_tensor_scan(fox_f[r, :], fox_keep[r, :], fox_f[r, :], 0.0, ALU.mult, ALU.add))
                then(dve.tensor_scalar(fox_k[r, :], fox_f[r, :], -1.0, None, ALU.mult))
                then(dve.memset(fox_k[r0, :], 1.0))
                then(dve.tensor_copy(fox_keep[r0, :], fox_f[r, :]))
                for h in range(NH):
                    op = dve.tensor_copy(fox_q[r, h, :], sel[r, h:h + 1].broadcast_to([NH, P]))
                then(op)
                for c in range(2):
                    for j in range(4):
                        h = 2 * j + c
                        dve.tensor_copy(fox_qs[r, c, TS * j:TS * (j + 1)], sel[r, h:h + 1].broadcast_to([NH, TS]))
                        op = dve.tensor_scalar(fox_qs[r0, c, TS * j:TS * (j + 1)], fox_keep[r0, 2 * TP:2 * TP + TS],
                                               sel[r0, h:h + 1], None, ALU.mult)
                then(op)

            def forget_queries(i):
                if i:
                    dve.wait_ge(logits_done, first_item["B"] + NH * i)
                dve.tensor_tensor(fox_q[0:NH], fox_keep[0:NH, i * P:(i + 1) * P].unsqueeze(1).broadcast_to([NH, NH, P]),
                                  sel[0:NH, :].unsqueeze(2).broadcast_to([NH, NH, P]), ALU.mult).then_inc(fox_ready, 1)

            dve.wait_ge(ada_added, ADA_HEAD + KB)
            conditions(1)
            conditions(2)
            normalise(1, 2)
            add_scores()
            masks()
            attention("A")
            forget_sums()
            attention("B")
            for m in range(KD):
                dve.wait_ge(unit_done, 2 * FIRST["ab_out"] + m + 1)
                dve.tensor_copy(split(y[:, m]), halves(2 * (m % 2))).then_inc(bank_free[m % 2], 1)
            add_branch(1, 1, 3)
            normalise(2, 4)
            ffn(1, FIRST["ffn1"])
            add_branch(2, 2, 5)
            dve.wait_ge(ada_added, ADA_HEAD + 2 * KB)
            conditions(3)
            conditions(4)
            normalise(3, 6)
            ffn(2, FIRST["ffn2"])
            add_branch(3, 3, 7)
            dve.wait_ge(ada_added, ADA_HEAD + 3 * KB)
            conditions(5)
            normalise(4, 8)

            def convolve(m):
                dve.wait_ge(bank_free[m % 2], FIRST["gdn_in"] + (m + 2) // 2 + 2)
                if m >= 2:
                    dve.wait_ge(conv_silu, m - 1)
                acc = conv_acc[:, m % 2]
                then(dve.tensor_scalar(acc, conv_in[:, m % 2, 0:TP], conv_w[:, m, 0:1], None, ALU.mult))
                for j in range(1, CW):
                    if j == CW - 1:
                        dve.tensor_copy(conv_last[:, m, :], conv_in[:, m % 2, TP:TP + CW - 1])
                    op = dve.scalar_tensor_tensor(acc, conv_in[:, m % 2, j:j + TP], conv_w[:, m, j:j + 1], acc,
                                                  ALU.mult, ALU.add)
                    if j < CW - 1:
                        then(op)
                op.then_inc(conv_done, 1)

            def convolve_sample():
                w = [conv_w[:, :, j:j + 1].broadcast_to([P, QKV, TS]) for j in range(CW)]
                then(dve.tensor_copy(conv_s[:, :, 0:CW - 1], conv_before))
                then(dve.tensor_tensor(conv_sum, conv_s[:, :, 0:TS], w[0], ALU.mult))
                for j in range(1, CW):
                    then(dve.tensor_tensor(conv_tap, conv_s[:, :, j:j + TS], w[j], ALU.mult))
                    op = dve.tensor_tensor(conv_sum, conv_sum, conv_tap, ALU.add)
                    if j < CW - 1:
                        then(op)
                op.then_inc(sample_conv, 1)
                dve.wait_ge(sample_conv, 1)
                dve.memset(row_keep, 1.0).then_inc(conv_done, 1)

            def decay_rows():
                dve.wait_ge(conv_done, QKV + 1)
                dve.wait_ge(rows_lin, 3)
                then(dve.scalar_tensor_tensor(row_sp, row_a, 0.0, row_sp, ALU.max, ALU.add))
                then(dve.tensor_scalar(row_sp, row_sp, g_col[:, 3:4], -1.0, ALU.mult, ALU.mult))
                then(dve.memset(row_keep.rearrange("p (c n) -> p c n", n=TS)[:, 0:TP // TS:CHUNK // TS, 0:1], 0.0))
                then(dve.memset(row_keep[:, TP:TP + 1], 0.0))
                then(dve.tensor_tensor_scan(row_g, row_keep, row_sp, 0.0, ALU.mult, ALU.add))
                then(dve.scalar_tensor_tensor(row_lb, row_b, 0.0, row_lb, ALU.min, ALU.subtract))
                dve.tensor_copy(ends[:, 0:CHUNKS], row_g[:, CHUNK - 1:TP:CHUNK])
                dve.tensor_copy(ends[:, CHUNKS:], row_g[:, T - 1:T]).then_inc(rows_ready, 1)
                for to in (rows_r, rows_c, rows_e):
                    op = dve.memset(to, 0.0)
                then(op)
                dve.wait_ge(lens_ln, 1)
                then(dve.tensor_scalar(row_lr, row_lr, -0.5, g_col[:, 2:3], ALU.mult, ALU.add))

                def rows(at):
                    return slice(at, at + NH)

                k, b, q, d = rows(ROW_K), rows(ROW_B), rows(ROW_Q), rows(ROW_D)
                then(dve.tensor_tensor(row_a, row_g, row_lr, ALU.add))
                then(dve.tensor_tensor(row_b, row_lr, row_g, ALU.subtract))
                dve.tensor_tensor(rows_r[k, :], row_a[k, :], row_lb[k, :], ALU.add)
                dve.tensor_tensor(rows_e[k, :], row_a[k, :], row_lb[k, :], ALU.add)
                dve.memset(rows_r[b, :], 1.0)
                dve.tensor_copy(rows_r[q, :], row_a[q, :])
                dve.memset(rows_c[k, :], 1.0)
                dve.tensor_copy(rows_c[b, :], row_b[b, :])
                dve.memset(rows_c[q, :], 1.0)
                dve.tensor_copy(rows_e[b, :], row_lb[b, :])
                dve.tensor_copy(rows_e[q, :], row_a[q, :])
                dve.tensor_tensor(rows_e[d, 0:TP].rearrange("p (c n) -> p c n", n=CHUNK),
                                  row_b[d, 0:TP].rearrange("p (c n) -> p c n", n=CHUNK),
                                  row_g[d, CHUNK - 1:TP:CHUNK].unsqueeze(2).broadcast_to([NH, CHUNKS, CHUNK]), ALU.add)
                dve.tensor_tensor(rows_e[d, TP:T], row_b[d, TP:T], row_g[d, T - 1:T].broadcast_to([NH, TS]), ALU.add)\
                    .then_inc(rows_ready, 1)

            def columns():
                dve.wait_ge(rows_exp, 1)
                dve.memset(state_p, 0.0).then_inc(ends_ready, 1)
                dve.tensor_tensor(ends_by_head, ends.unsqueeze(2).broadcast_to([P, CHUNKS + 1, NH]),
                                  g_sel[:, 3, :].unsqueeze(1).broadcast_to([P, CHUNKS + 1, NH]), ALU.mult)\
                    .then_inc(ends_ready, 1)
                dve.wait_ge(rows_turned, 1)
                dve.tensor_copy(cols, as_tiles(psum[:, 6, :]))
                dve.tensor_copy(g_last.rearrange("p c h -> p (c h)"), psum[:, 7, P:P + (CHUNKS + 1) * NH])
                for g in range(2):
                    for j in range(4):
                        r = slice(TS * j, TS * (j + 1))
                        op = dve.tensor_copy(cols_s[r, g, :], psum[r, 7, 4 * g + j:P:TS])
                op.then_inc(cols_ready, 1)
                dve.wait_ge(cols_ready, 1)

            def column(at, q):
                n = tiles_of(q)
                if q < NH:
                    return cols[:, :, at + q:at + q + 1].broadcast_to([P, n, P])
                return cols_s[:, q - NH:q - NH + 1, at // TS:at // TS + 1].broadcast_to([P, n, P])

            def gdn_decay(q):
                u, n, b = q % 2, size(q), 4 * (q % 2)
                dve.wait_ge(kk_exp, q + 1)
                dve.tensor_tensor(low[:, u, 0:n], psum[:, b, 0:n], t2[:, u, 0:n], ALU.mult).then_inc(kk_decayed, 1)
                dve.wait_ge(kq_exp, q + 1)
                dve.tensor_tensor(qk_t[:, q, :] if q < NH else qk_s[:, q - NH, :], psum[:, b + 2, 0:n],
                                  low_m[:, u, 0:n], ALU.mult).then_inc(kq_decayed, 1)
                dve.wait_ge(kk_decayed, q + 1)
                dve.wait_ge(kq_decayed, q + 1)

            def gdn_mask(q, l):
                u, n = q % 2, size(q)
                if l:
                    dve.wait_ge(t2_made, level_at(q, l - 1) + 1)
                if l == 1:
                    dve.wait_ge(kv_scaled, q + 1)
                dve.tensor_tensor(as_tiles(low_m[:, u, 0:n]), as_tiles(low[:, u, 0:n]),
                                  g_mask[:, 4 + l, :].unsqueeze(1).broadcast_to([P, tiles_of(q), P]), ALU.mult)\
                    .then_inc(low_ready, 1)

            def gdn_scale(q):
                u, n, b = q % 2, size(q), 4 * (q % 2)
                dve.wait_ge(low_ready, level_at(q, 0) + 1)
                eye = ident[:].unsqueeze(1).broadcast_to([P, tiles_of(q), P])
                dve.tensor_tensor(as_tiles(inv[:, u, 0:n]), eye, as_tiles(low_m[:, u, 0:n]), ALU.subtract)
                dve.wait_ge(k_turned, q + 1)
                k = as_tiles(psum[:, b, 0:n])
                dve.tensor_tensor(as_tiles(k_beta[:, u, 0:n]), k, column(ROW_K, q), ALU.mult)
                dve.tensor_tensor(as_tiles(gz[:, GZ_K + q, 0:TP]) if q < NH else kdec_s[:, q - NH:q - NH + 1, :], k,
                                  column(ROW_D, q), ALU.mult)
                dve.wait_ge(v_turned_g, q + 1)
                dve.wait_ge(q_factor, q + 1)
                dve.tensor_tensor(as_tiles(v_beta[:, u, 0:n]), as_tiles(psum[:, b + 1, 0:n]), column(ROW_B, q), ALU.mult)
                f = psum[:, b + 2, 0:n]
                dve.tensor_tensor(z_item(GZ_Q, q), z_item(GZ_Q, q), f if q < NH else as_heads(f), ALU.mult)\
                    .then_inc(kv_scaled, 1)

            def gdn_update(q, l):
                u, n, b = q % 2, size(q), 4 * (q % 2)
                if l == 0:
                    dve.wait_ge(t2_made, level_at(q, 0) + 1)
                    eye = ident[:].unsqueeze(1).broadcast_to([P, tiles_of(q), P])
                    op = dve.tensor_tensor(as_tiles(inv_t[:, u, 0:n]), eye, as_tiles(psum[:, b + 3, 0:n]), ALU.subtract)
                else:
                    dve.wait_ge(e_made, copies_at(q, l) + 1)
                    dve.wait_ge(inv_ready, level_at(q, l - 1) + 1)
                    if l < levels_of(q) - 1:
                        dve.tensor_tensor(inv[:, u, 0:n], inv[:, u, 0:n], psum[:, b + 1, 0:n], ALU.subtract)
                    op = dve.tensor_tensor(inv_t[:, u, 0:n], inv_t[:, u, 0:n], psum[:, b, 0:n], ALU.subtract)
                op.then_inc(inv_ready, 1)

            def recur_v(n):
                c, h = steps[n]
                dve.wait_ge(v_made, n + 1)
                if n >= 2:
                    dve.wait_ge(kv_made, n - 1)
                m, r = (TS, TS * (h % 4)) if c == "s" else (CHUNK, CHUNK * (c % 2))
                src = u_s[r:r + m, h // 4, :] if c == "s" else gz[r:r + m, GZ_V + h, c // 2 * P:(c // 2 + 1) * P]
                dve.tensor_tensor(v_new[r:r + m, n % 2, :], psum[r:r + m, n % 2, 0:P], src, ALU.add)\
                    .then_inc(v_new_ready, 1)

            def recur_state(n):
                c, h = steps[n]
                dve.wait_ge(kv_made, n + 1)
                state, at = (state_s, CHUNKS) if c == "s" else (state_p, c)
                dve.scalar_tensor_tensor(state[:, h, :], state[:, h, :], g_last[:, at, h:h + 1], psum[:, 4 + n % 2, 0:P],
                                         ALU.mult, ALU.add).then_inc(state_new, 1)

            dve.wait_ge(gdn_loaded, 16 * 5)
            dve.memset(conv_in[:, :, 0:CW - 1], 0.0).then_inc(conv_zeroed, 1)
            dve.wait_ge(conv_zeroed, 1)
            for m in range(QKV):
                convolve(m)
            convolve_sample()
            decay_rows()
            columns()
            dve.wait_ge(gdn_masks, 16)
            for q0 in range(0, G_ITEMS, 2):
                pair = (q0, q0 + 1)
                for q in pair:
                    gdn_decay(q)
                    gdn_mask(q, 0)
                for q in pair:
                    gdn_scale(q)
                for q in pair:
                    gdn_update(q, 0)
                for q in pair:
                    gdn_mask(q, 1)
                for l in range(1, levels_of(q0)):
                    for q in pair:
                        if l + 1 < levels_of(q):
                            gdn_mask(q, l + 1)
                    for q in pair:
                        gdn_update(q, l)
            dve.wait_ge(gdn_state, 16)
            for n in range(len(steps) + 2):
                if n < len(steps):
                    recur_v(n)
                if n >= 2:
                    if n - 2 >= NH:
                        dve.wait_ge(state_new, n - 2 - NH + 1)
                    recur_state(n - 2)
            for h in range(NH):
                dve.wait_ge(g_rstd_ready, h + 1)
                dve.tensor_tensor(g_tmp[:, h % 2], gz[:, GZ_Q + h], g_rstd[:, h % 2], ALU.mult).then_inc(g_used, 1)
                dve.wait_ge(g_used, h + 1)
                then(dve.scalar_tensor_tensor(g_out[:, h % 2], g_tmp[:, h % 2], norm_col[:], gz[:, GZ_G + h],
                                              ALU.mult, ALU.mult))
                dve.tensor_copy(h_hi[:, h], g_out[:, h % 2]).then_inc(g_own, 1)
                dve.wait_ge(g_own, h + 1)
                dve.tensor_tensor(h_lo[:, h], g_out[:, h % 2], h_hi[:, h].bitcast(F32), ALU.subtract).then_inc(g_ready, 1)
            for m in range(KD):
                dve.wait_ge(unit_done, 2 * FIRST["gdn_out"] + m + 1)
                dve.tensor_copy(split(y[:, m]), halves(2 * (m % 2))).then_inc(bank_free[m % 2], 1)
            add_branch(4, 4, 9)
            normalise(5, 10)
            ffn(3, FIRST["ffn3"])
            add_branch(5, 5, 11)


OUTS = {"y_t": (D, T), "a_k": (TP, T), "a_v": (TP, T), "a_ik": (HD, T), "b_k": (TP, T), "b_v": (TP, T),
        "b_logf": (NH, T), "p_conv": (QKV * P, CW - 1), "s_conv": (QKV * P, CW - 1), "p_rec": (NH, P, P),
        "s_rec": (NH, P, P)}


def arrays(i):
    f = np.float32
    tokens = np.concatenate([i["x_prompt"][0], i["x_sample"][0]], 0)

    def units(w, cols=None):
        k, n = w.shape
        return w.reshape(k // D, KD, P, n // P, P).transpose(0, 3, 2, 1, 4).reshape(k // D, n // P, P, D)

    def ffn(l, j):
        g = units(i["ffn_w_gate"][l, j])[0].reshape(KB, KD, 1, P, D)
        u = units(i["ffn_w_up"][l, j])[0].reshape(KB, KD, 1, P, D)
        gu = np.concatenate([g, u], 2)
        dn = units(i["ffn_w_down"][l, j]).reshape(KB, KD // 2, 2, P, D)
        return np.concatenate([gu, dn], 1).reshape(-1, 2, P, D)

    def product(w):
        return units(w)[0].reshape(-1, 2, P, D)

    qa, ka, va, qi, ki, wi, qb, kb, vb, fl = np.split(
        i["ab_w_in"], np.cumsum([512, 512, 512, 512, 64, 8, 512, 512, 512]), axis=1)
    gap = np.zeros((D, FOX_ROW - NH), f)
    ab_in = np.concatenate([ki, ki, wi, gap, fl, np.zeros((D, P - FOX_ROW - NH), f), qi, ka, qa, va, kb, qb, vb], 1)
    rel = np.arange(REL) - (5 * P - 1)
    n = np.abs(rel)
    far = 8 + (np.log(np.maximum(n, 1).astype(f) / f(8)) / f(np.log(32.0)) * f(8)).astype(np.int32)
    bucket = np.where(rel > 0, 16, 0) + np.where(n < 8, n, np.minimum(far, 15))
    heads = np.arange(NH)
    sel = np.zeros((P, NH), f)
    sel[heads, heads] = 1
    sel[FOX_ROW + heads, heads] = 1
    q = np.arange(P)
    b_f = np.zeros((P, 1), f)
    b_f[FOX_ROW:FOX_ROW + NH, 0] = i["ab_b_f"]

    def flat(name):
        return i[name][0].reshape(TP, -1)

    qkv, gate, b_logit, a_logit = np.split(i["gdn_w_in"], np.cumsum([QKV * P, NH * P, NH]), axis=1)

    def in_rows(a, at):
        out = np.zeros((a.shape[0], P), f)
        for r in at:
            out[:, r:r + NH] = a
        return out

    every = (ROW_K, ROW_B, ROW_Q, ROW_D)
    gdn_in = np.concatenate([in_rows(a_logit, every), in_rows(b_logit, (ROW_K, ROW_B)), qkv, gate], 1)
    eye = np.eye(NH, dtype=f)
    g_sel = np.stack([in_rows(eye, at).T for at in ((ROW_K, ROW_B), (ROW_Q, ROW_B), (ROW_Q,), (ROW_K,))], 1)
    g_col = np.zeros((P, 4), f)
    g_col[:, 0] = in_rows(i["gdn_dt_bias"][None, :], every)[0]
    g_col[:, 1] = in_rows(i["gdn_A_log"][None, :], every)[0]
    g_col[ROW_Q:ROW_Q + NH, 2] = -0.5 * np.log(P)
    strips = np.zeros((P, 2, STRIP), f)
    strips[:, 0, ROW_Q + NH - 1] = 1
    for r in (ROW_K, ROW_B, ROW_D):
        strips[:, 1, r + NH - 1] = 1

    def allow(ok):
        return np.where(ok, 0, NEG).astype(f)

    r, c = q[:, None], q[None, :]
    g_mask = [allow((r // n == c // n) & ok) for n in (CHUNK, TS) for ok in (c < r, r <= c)]
    for l in range(LEVELS):
        n = 1 << l
        g_mask.append(((r // (2 * n) == c // (2 * n)) & (r // n % 2 == 1) & (c // n % 2 == 0)).astype(f))

    stream = [ffn(0, 0), product(ab_in), product(i["ab_w_out"]), ffn(0, 1), ffn(1, 0), product(gdn_in),
              product(i["gdn_w_out"]), ffn(1, 1)]
    out = {
        "x_t": tokens.T,
        "c_t": np.stack([i["c_prompt"][0], i["c_sample"][0]], 1).reshape(KD, P, 2).transpose(1, 0, 2),
        "ada_b": i["ada_b"].reshape(ADA_TILES, P).T,
        "g_pre": i["norm_pre"].reshape(-1, P).T,
        "g_post": i["norm_post"].reshape(-1, P).T,
        "eps": np.full((P, 1), EPS, f),
        "ident": np.eye(P, dtype=f),
        "rel_bias": i["rel_bias"],
        "onehot": (np.arange(32)[:, None] == bucket[None, :]).astype(f),
        "diag_mask": np.where(q[None, :] <= q[:, None], 0, NEG).astype(f),
        "tail_mask": np.where(np.arange(TS)[None, :] <= (q % TS)[:, None], 0, NEG).astype(f),
        "sel": sel,
        "b_f": b_f,
        "cache_ik": np.concatenate([flat("cache_a_idx_k").T] * 2, 0),
        "cache_A_k": flat("cache_a_k").T,
        "cache_A_v": flat("cache_a_v"),
        "cache_B_k": flat("cache_b_k").T,
        "cache_B_v": flat("cache_b_v"),
        "cache_logf": flat("cache_b_logf").T,
        "ada_w": i["ada_w"].reshape(LAYERS, KD, P, ADA_HALVES // LAYERS, ADA_HALF).transpose(0, 3, 1, 2, 4)
                 .reshape(ADA_HALVES, KD, P, ADA_HALF),
        "strips": strips,
        "g_sel": g_sel,
        "g_col": g_col,
        "conv_w": i["gdn_conv_w"].reshape(CW, QKV, P).transpose(2, 1, 0),
        "conv_before": i["state_c_conv"][0].reshape(CW - 1, QKV, P).transpose(2, 1, 0),
        "state_rec": i["state_c_rec"][0],
        "g_mask": np.stack(g_mask, 1),
        "norm_col": i["gdn_norm_w"][:, None],
        "w_stream": np.concatenate(stream, 0).transpose(0, 2, 1, 3),
    }
    return {k: np.ascontiguousarray(v) for k, v in out.items()}


def kernel(**inputs):
    import concourse.bacc as bacc
    from concourse.bass_utils import run_bass_kernel_spmd

    nc = bacc.Bacc("TRN2", target_bir_lowering=False, num_devices=1, dynamic_dma_scratch_size=1024)
    ins = {f"in_{name}": a for name, a in arrays({k: np.asarray(v) for k, v in inputs.items()}).items()}
    io = {name[3:]: nc.dram_tensor(name, list(a.shape), mybir.dt.from_np(a.dtype), kind="ExternalInput").ap()
          for name, a in ins.items()}
    for name, shape in OUTS.items():
        io[name] = nc.dram_tensor(f"out_{name}", list(shape), F32, kind="ExternalOutput").ap()
    io["rel_spread"] = nc.dram_tensor("rel_spread", [NH, REL_AT], F32, kind="Internal").ap()
    build(nc, io)
    r = run_bass_kernel_spmd(nc, [ins], core_ids=[0]).results[0]
    got = {name: np.asarray(r[f"out_{name}"]) for name in OUTS}
    out = []
    for group, t in (("p", slice(0, TP)), ("s", slice(TP, T))):
        n = t.stop - t.start
        heads = {name: got[name].T[t].reshape(1, n, NH, HD) for name in ("a_k", "a_v", "b_k", "b_v")}
        out.append((got["y_t"].T[None, t],
                    [heads["a_k"], heads["a_v"], got["a_ik"].T[None, t], heads["b_k"], heads["b_v"],
                     got["b_logf"].T[None, t], got[group + "_conv"].T[None], got[group + "_rec"][None]]))
    return tuple(np.ascontiguousarray(a) for a in (out[0][0], out[1][0], *out[0][1], *out[1][1]))
```

```python
from contextlib import ExitStack

import numpy as np

import concourse.bass as bass
from concourse import mybir

F32 = mybir.dt.float32
F32R = mybir.dt.float32r
ALU = mybir.AluOpType
ACT = mybir.ActivationFunctionType
AX = mybir.AxisListType

P = 128
D = 1024
TP, TS = 512, 32
T = TP + TS
HT = T // 2
KD = D // P
DFF = 4 * D
KB = DFF // D
LAYERS, SUBS = 2, 3
EPS = 1e-6
NEG = -1.0e30
TAKEN = -3.0e38
LN_EXP = "natural_log_exp_and_others"
POOL_TILES = (2, 5)
SCORE_TILES = (1, 2, 3)
HD = 64
NH = 8
TOPK_P, TOPK_S = 128, 136
GROUPS = ((0, TP), (TP, T))

DVE_TILES = KD - len(POOL_TILES)
FFN_PAIRS = KB * (KD + KD // 2)
AB_PAIRS = 15
GDN_UNITS, GDN_PAIRS = 33, 17
OUT_PAIRS = KD // 2
PAIRS = 4 * FFN_PAIRS + AB_PAIRS + GDN_PAIRS + 2 * OUT_PAIRS
ADA_TILES = LAYERS * 9 * KD
ADA_HALF = 6 * P
ADA_PARTS = (2, 2, 1, 0)
ADA_HALVES = LAYERS * 9 * D // ADA_HALF
ADA_HEAD = 2
ADA_FIRST_HALF = (4, 12, 20, 0)
ADA_CHUNKS_BEFORE = (1, 5, 9, 13)


def first_pairs():
    at, out = 0, {}
    for name, n in (("ffn0", FFN_PAIRS), ("ab_in", AB_PAIRS), ("ab_out", OUT_PAIRS), ("ffn1", FFN_PAIRS),
                    ("ffn2", FFN_PAIRS), ("gdn_in", GDN_PAIRS), ("gdn_out", OUT_PAIRS), ("ffn3", FFN_PAIRS)):
        out[name] = at
        at += n
    assert at == PAIRS and PAIRS % 2 == 0
    return out


FIRST = first_pairs()

Z_IK, Z_W, Z_IQ, Z_KA, Z_QA, Z_VA, Z_KB, Z_QB, Z_VB = 0, 1, 2, 6, 10, 14, 18, 22, 26
Z_TILES = 30
FOX_ROW = 32
REL = 768
REL_AT = P * (REL + 1)
NK_S = TP + TS


ARENA = 25600

CW = 4
GZ_Q, GZ_K, GZ_V, GZ_G = 0, NH, 2 * NH, 3 * NH
QKV = 3 * NH
CHUNK = 64
CHUNKS = TP // CHUNK
TILES = TP // P
ROW_K, ROW_B, ROW_Q, ROW_D = 0, 32, 64, 96
LEVELS = 6
STRIP = P + NH - 1


class Cutter:

    def __init__(self, flat, at=0):
        self.flat, self.at = flat, at

    def __call__(self, dims, **sizes):
        n = int(np.prod(list(sizes.values())))
        got = self.flat[:, self.at:self.at + n]
        self.at += n
        assert self.at <= self.flat.shape[1], self.at
        return got.rearrange(f"p ({dims}) -> p {dims}", **sizes) if len(sizes) > 1 else got


def build(nc, io):
    with ExitStack() as ctx:
        def sb(name, shape, dt=F32):
            return ctx.enter_context(nc.sbuf_tensor(name, shape, dt))

        def sem(name):
            return ctx.enter_context(nc.semaphore(name))

        x = sb("x", [P, KD, T])
        hid_at = nc.sbuf_base
        hid_hi = sb("hid_hi", [P, KD, T], F32R)
        hid_lo = sb("hid_lo", [P, KD, T], F32R)
        h_at = nc.sbuf_base
        h_hi = sb("h_hi", [P, KD, T], F32R)
        h_lo = sb("h_lo", [P, KD, T], F32R)
        raw = sb("raw", [P, 2, 2, D])
        w_hi = sb("w_hi", [P, 2, D], F32R)
        w_lo = sb("w_lo", [P, 2, D], F32R)
        mod = sb("mod", [P, ADA_TILES, 2])
        c_t = sb("c_t", [P, KD, 2])
        ada_b = sb("ada_b", [P, ADA_TILES])
        g_pre = sb("g_pre", [P, LAYERS * SUBS * KD])
        g_post = sb("g_post", [P, LAYERS * SUBS * KD])
        scale_in = sb("scale_in", [P, LAYERS * SUBS, KD, 2])
        gate_out = sb("gate_out", [P, LAYERS * SUBS, KD, 2])
        spare = nc.alloc_sbuf_tensor_at("spare", [P, 2 * KD * T], F32, offset=hid_at)
        spare_h = nc.alloc_sbuf_tensor_at("spare_h", [P, 2 * KD * T], F32, offset=h_at)
        rel_sb = sb("rel_sb", [32, NH])
        diag_mask = sb("diag_mask", [P, P])
        tail_mask = sb("tail_mask", [P, TS])
        sel = sb("sel", [P, NH])
        b_f = sb("b_f", [P, 1])
        norm_col = sb("norm_col", [P, 1])
        wi_tok = sb("wi_tok", [P, 5, NH])
        top8 = sb("top8", [P, 8])
        neg_max = sb("neg_max", [P, 2])
        p_sum = sb("p_sum", [P, 2])
        p_inv = sb("p_inv", [P, 2])
        ones = sb("ones", [P, P])
        ident = sb("ident", [P, P])
        one_col = sb("one_col", [P, 1])
        eps_col = sb("eps_col", [P, 1])
        arena = sb("arena", [P, ARENA])
        cut = Cutter(arena)
        y = cut("k t", k=KD, t=T)
        sq = cut("k t", k=2, t=T)
        tmp = cut("k t", k=2, t=T)
        h32 = cut("k t", k=2, t=T)
        silu = cut("k t", k=2, t=T)
        rstd = cut("t", t=T)
        lnv = cut("t", t=T)
        ada_w = cut("k n", k=KD, n=2 * ADA_HALF)
        ada_sum = cut("c n", c=2, n=2 * ADA_HALF)
        cut = Cutter(arena)
        z = cut("k t", k=Z_TILES, t=T)
        scores = {1: cut("n", n=256), 2: cut("n", n=384), 3: cut("n", n=512), "s": cut("n", n=NK_S)}
        scores[0] = cut("n", n=P)
        p_turned = cut("r b q", r=2, b=5, q=P)
        rel_at = cut.at
        bias_p = cut("h m", h=NH, m=4 * P)
        fox_q = cut("h q", h=NH, q=P)
        fox_k = cut("t", t=TP + NK_S)
        fb = Cutter(arena, Z_VA * T)("m", m=REL)
        onehot = Cutter(arena, Z_VB * T)("m", m=REL)
        cut = Cutter(arena, Z_IQ * T)
        neg_logits = cut("r t", r=2, t=T)
        probs = cut("r t", r=2, t=T)
        cut = Cutter(spare[:])
        cache_k = cut("k t", k=4, t=TP)
        cache_v = cut("b d", b=5, d=TP)
        cache_ik = cut("t", t=TP)
        v_tok = cut("b d", b=4, d=TP)
        relu = cut("r t", r=2, t=T)
        bias_s = relu
        fox_qs = cut("r q", r=2, q=P)
        fox_w = Cutter(arena, Z_IQ * T)("r t", r=4, t=T)
        fox_f = Cutter(spare[:], 4 * TP + 5 * TP + TP)("t", t=TP + NK_S)
        fox_fq = z[:, Z_W, :]

        ada_second = [spare[:, k * 2 * ADA_HALF:(k + 1) * 2 * ADA_HALF] if k < 5 else
                      spare_h[:, (k - 5) * 2 * ADA_HALF:(k - 4) * 2 * ADA_HALF] for k in range(KD)]
        ada_rows = Cutter(arena, (KD + 4) * T)("n", n=2 * ADA_HALF)[0:2]
        cut = Cutter(arena)
        gz = cut("k t", k=4 * NH, t=T)
        rows_r, rows_c, rows_e = cut("t", t=T), cut("t", t=T), cut("t", t=T)
        conv_at = cut.at
        g_mask = cut("k n", k=4 + LEVELS, n=P)
        cols = cut("b r", b=TILES, r=P)
        cols_s = cut("g k", g=2, k=4)
        rows_es = cut("n", n=P)
        keys_s = cut("n", n=P)
        state_p = cut("h e", h=NH, e=P)
        state_s = cut("h e", h=NH, e=P)
        kdec_s = cut("g n", g=2, n=P)
        u_s = cut("g n", g=2, n=P)
        qk_s = cut("g n", g=2, n=P)
        v_new = cut("c r n", c=3, r=2, n=P)
        ends = cut("c", c=CHUNKS + 1)
        ends_by_head = cut("c h", c=CHUNKS + 1, h=NH)
        g_last = cut("c h", c=CHUNKS + 1, h=NH)
        strips = cut("r n", r=2, n=STRIP)
        g_sel = cut("r h", r=4, h=NH)
        g_col = cut("r", r=4)
        conv_w = cut("k j", k=QKV, j=CW)
        cut = Cutter(arena, conv_at)
        conv_in = cut("r t", r=2, t=T + CW - 1)
        conv_acc = cut("r t", r=2, t=TP)
        conv_sq = cut("r t", r=2, t=TP)
        cut = Cutter(spare[:])
        conv_s = cut("k t", k=QKV, t=TS + CW - 1)
        conv_last = cut("k j", k=QKV, j=CW - 1)
        conv_before = cut("k j", k=QKV, j=CW - 1)
        conv_sum = cut("k t", k=QKV, t=TS)
        conv_tap = cut("k t", k=QKV, t=TS)
        row_a, row_sp, row_b, row_lb, row_g, row_lr, row_keep = (cut("t", t=T) for _ in range(7))
        cut = Cutter(spare[:])
        w_neg = cut("h t", h=NH, t=T)
        qk_t = cut("h t", h=NH, t=TP)
        cut = Cutter(spare_h[:])
        low, low_m, inv, inv_t, t2, k_beta, v_beta = (cut("u n", u=2, n=TP) for _ in range(7))
        cut = Cutter(spare[:])
        g_sq, g_out = cut("r t", r=2, t=T), cut("r t", r=2, t=T)
        g_rstd = cut("h t", h=NH, t=T)

        psum = ctx.enter_context(nc.psum_tensor("psum", [P, 8, 512], F32))

        def halves(bank):
            return psum[:, bank:bank + 2, 0:HT]

        def split(ap):
            return ap.rearrange("p (b t) -> p b t", b=2)

        in_loaded = sem("in_loaded")
        out_stored = sem("out_stored")
        w_loaded = [sem("w_loaded0"), sem("w_loaded1")]
        w_rounded = sem("w_rounded")
        w_split = sem("w_split")
        unit_done = sem("unit_done")
        bank_free = [sem("bank_free0"), sem("bank_free1")]
        ada_loaded = [sem(f"ada_loaded{k}") for k in range(KD)]
        ada_second_loaded = [sem(f"ada_second_loaded{k}") for k in range(KD)]
        c_loaded = sem("c_loaded")
        ada_used = sem("ada_used")
        ada_turned = sem("ada_turned")
        ada_rows_made = sem("ada_rows_made")
        ada_rows_copied = sem("ada_rows_copied")
        ada_rows_turned = sem("ada_rows_turned")
        ada_added = sem("ada_added")
        c_ready = sem("c_ready")
        consts = sem("consts")
        cond_ready = sem("cond_ready")
        dve_own = sem("dve_own")
        sq_ready = sem("sq_ready")
        sq_summed = sem("sq_summed")
        y_sq_total = sem("y_sq_total")
        ln_done = sem("ln_done")
        rstd_ready = sem("rstd_ready")
        scaled = sem("scaled")
        h32_ready = sem("h32_ready")
        h_rounded = sem("h_rounded")
        h_ready = sem("h_ready")
        hid_rounded = sem("hid_rounded")
        hid_ready = sem("hid_ready")
        y_scaled = sem("y_scaled")
        x_ready = sem("x_ready")
        x_ready_pool = sem("x_ready_pool")
        y_gated = sem("y_gated")
        y_scaled_pool = sem("y_scaled_pool")

        rel_made = sem("rel_made")
        onehot_loaded = sem("onehot_loaded")
        rel_copied = sem("rel_copied")
        rel_spread = sem("rel_spread")
        bias_loaded = sem("bias_loaded")
        bias_s_loaded = sem("bias_s_loaded")
        cache_loaded = {"ik": sem("cache_ik_loaded"), "A": sem("cache_a_loaded"), "B": sem("cache_b_loaded")}
        wi_turned = sem("wi_turned")
        wi_ready = sem("wi_ready")
        dots_done = sem("dots_done")
        relu_ready = sem("relu_ready")
        score_added = sem("score_added")
        masks_ready = sem("masks_ready")
        v_turned = sem("v_turned")
        v_ready = sem("v_ready")
        logits_done = sem("logits_done")
        max_ready = sem("max_ready")
        exp_done = sem("exp_done")
        p_ready = sem("p_ready")
        p_turn_done = sem("p_turn_done")
        p_turn_ready = sem("p_turn_ready")
        av_done = sem("av_done")
        o_rounded = sem("o_rounded")
        o_ready = sem("o_ready")
        fox_own = sem("fox_own")
        fox_loaded = sem("fox_loaded")
        fox_copied = sem("fox_copied")
        fox_ready = sem("fox_ready")
        state_stored = sem("state_stored")
        logf_stored = sem("logf_stored")
        fox_summed = sem("fox_summed")

        gdn_loaded = sem("gdn_loaded")
        conv_zeroed = sem("conv_zeroed")
        conv_done = sem("conv_done")
        conv_silu = sem("conv_silu")
        conv_sq_ready = sem("conv_sq_ready")
        lens_summed = sem("lens_summed")
        sample_conv = sem("sample_conv")
        sample_silu = sem("sample_silu")
        row_own = sem("row_own")
        rows_lin = sem("rows_lin")
        lens_ln = sem("lens_ln")
        rows_ready = sem("rows_ready")
        rows_exp = sem("rows_exp")
        ends_ready = sem("ends_ready")
        rows_turned = sem("rows_turned")
        cols_ready = sem("cols_ready")
        gdn_masks = sem("gdn_masks")
        gdn_state = sem("gdn_state")
        lq_ready = sem("lq_ready")
        kk_done = sem("kk_done")
        kq_done = sem("kq_done")
        kk_exp = sem("kk_exp")
        kq_exp = sem("kq_exp")
        kk_decayed = sem("kk_decayed")
        kq_decayed = sem("kq_decayed")
        bc_ready = sem("bc_ready")
        k_turned = sem("k_turned")
        v_turned_g = sem("v_turned_g")
        q_factor = sem("q_factor")
        q_scaled = sem("q_scaled")
        k_scaled = sem("k_scaled")
        v_scaled = sem("v_scaled")
        low_ready = sem("low_ready")
        t2_made = sem("t2_made")
        t2_copied = sem("t2_copied")
        e_made = sem("e_made")
        inv_ready = sem("inv_ready")
        inv_t_ready = sem("inv_t_ready")
        wu_made = sem("wu_made")
        wu_out = sem("wu_out")
        v_made = sem("v_made")
        v_new_ready = sem("v_new_ready")
        o_made = sem("o_made")
        o_out = sem("o_out")
        kv_made = sem("kv_made")
        state_new = sem("state_new")
        g_sq_ready = sem("g_sq_ready")
        g_sq_summed = sem("g_sq_summed")
        g_ln_done = sem("g_ln_done")
        g_rstd_ready = sem("g_rstd_ready")
        g_own = sem("g_own")
        g_used = sem("g_used")
        g_ready = sem("g_ready")

        block = ctx.enter_context(nc.Block())
        N_IN = 12

        items = []
        for mixer in "AB":
            for i in (0, 1, 2, 3, "s"):
                for h in range(NH if i != "s" else 2):
                    items.append((mixer, i, h))
        first_item = {"A": 0, "B": len(items) // 2}
        n_items = len(items) // 2
        group_of, last_of_group = [], []
        for e, (mixer, i, h) in enumerate(items):
            group_of.append(group_of[-1] + 1 if e and h % 2 == 0 else (group_of[-1] if e else 0))
            last_of_group.append(h % 2 == 1)

        def keys_of(i):
            return NK_S if i == "s" else P * (i + 1)

        def score_items():
            return [(i, h) for i in (1, 2, 3, "s") for h in range(NH)]

        G_ITEMS = NH + 2

        def size(q):
            return TP if q < NH else P

        def tiles_of(q):
            return size(q) // P

        def levels_of(q):
            return LEVELS if q < NH else LEVELS - 1

        def level_at(q, l):
            return 2 * LEVELS * (q // 2) + 2 * l + q % 2

        def copies_at(q, l):
            return level_at(q, l) - 2 * (q // 2 + 1)

        def sample_heads(q):
            return slice(4 * (q - NH), 4 * (q - NH) + 4)

        def z_item(at, q):
            if q < NH:
                return gz[:, at + q, 0:TP]
            return gz[:, at + 4 * (q - NH):at + 4 * (q - NH) + 4, TP:T]

        def z_tile(at, q, t):
            if q < NH:
                return gz[:, at + q, t * P:(t + 1) * P]
            return (kdec_s if at == GZ_K else u_s)[:, q - NH, :]

        def as_tiles(ap):
            return ap.rearrange("p (t n) -> p t n", n=P)

        def as_heads(ap):
            return ap.rearrange("p (h n) -> p h n", n=TS)

        steps = [("s", h) for h in range(NH)] + [(c, h) for c in range(CHUNKS) for h in range(NH)]

        SCORE_UNITS = 18

        def scores_after(m):
            return range(3 * (m - 6), min(3 * (m - 5), len(score_items())))

        @block.sync
        def _(sp):
            sp.dma_start(ada_b[:], io["ada_b"]).then_inc(in_loaded, 16)
            sp.dma_start(g_pre[:], io["g_pre"]).then_inc(in_loaded, 16)
            sp.dma_start(g_post[:], io["g_post"]).then_inc(in_loaded, 16)
            sp.dma_start(x[:], io["x_t"].rearrange("(k p) t -> p k t", p=P)).then_inc(in_loaded, 16)
            sp.dma_start(ident[:], io["ident"]).then_inc(in_loaded, 16)
            for name, to in (("rel_bias", rel_sb), ("diag_mask", diag_mask), ("tail_mask", tail_mask), ("sel", sel),
                             ("b_f", b_f), ("norm_col", norm_col)):
                sp.dma_start(to[:], io[name]).then_inc(in_loaded, 16)
            sp.dma_start(eps_col[:], io["eps"]).then_inc(in_loaded, 16)
            sp.wait_ge(ada_second_loaded[KD - 3], 16)
            for s in range(2):
                sp.dma_start(raw[:, s], io["w_stream"][s]).then_inc(w_loaded[s], 16)
            with sp.Fori(1, PAIRS // 2) as i:
                for s in range(2):
                    sp.wait_ge(w_split, 4 * i - 2 + 2 * s)
                    sp.dma_start(raw[:, s], io["w_stream"][2 * i + s]).then_inc(w_loaded[s], 16)
            sp.wait_ge(x_ready, DVE_TILES * LAYERS * SUBS)
            sp.wait_ge(x_ready_pool, len(POOL_TILES) * LAYERS * SUBS)
            sp.dma_start(io["y_t"].rearrange("(k p) t -> p k t", p=P), x[:]).then_inc(out_stored, 16)
            sp.wait_ge(out_stored, 16)
            sp.wait_ge(state_stored, 16 * 9)
            sp.wait_ge(logf_stored, 16)

        @block.gpsimd
        def _(pool):
            pool.wait_ge(consts, 1)

            def split_unit(s, u, n):
                pool.tensor_tensor(w_hi[:, u], raw[:, s, u], one_col[:].broadcast_to([P, D]), ALU.mult)\
                    .then_inc(w_rounded, 1)
                pool.wait_ge(w_rounded, n + 1)
                pool.tensor_tensor(w_lo[:, u], raw[:, s, u], w_hi[:, u].bitcast(F32), ALU.subtract)\
                    .then_inc(w_split, 1)

            def split_pair(i, s):
                for u in range(2):
                    pool.wait_ge(w_loaded[s], 16 * i + 16)
                    pool.wait_ge(unit_done, 4 * i + 2 * s + u - 1)
                    split_unit(s, u, 4 * i + 2 * s + u)

            def split_pairs(a, b):
                if a % 2:
                    split_pair(a // 2, 1)
                with pool.Fori(a // 2 + a % 2, b // 2) as i:
                    for s in range(2):
                        split_pair(i, s)
                if b % 2:
                    split_pair(b // 2, 0)

            def add_branch(n):
                pool.wait_ge(rstd_ready, 2 * n + 2)
                for i, k in enumerate(POOL_TILES):
                    pool.wait_ge(y_gated, KD * n + k + 1)
                    pool.tensor_tensor(y[:, k], y[:, k], rstd, ALU.mult).then_inc(y_scaled_pool, 1)
                    pool.wait_ge(y_scaled_pool, len(POOL_TILES) * n + i + 1)
                    pool.tensor_tensor(x[:, k], x[:, k], y[:, k], ALU.add).then_inc(x_ready_pool, 1)

            pool.wait_ge(w_loaded[0], 16)
            for u in range(2):
                split_unit(0, u, u)
            done = 1
            ends = [FIRST[name] + 1 for name in ("ab_in", "ffn1", "ffn2", "gdn_in", "ffn3")] + [PAIRS]
            for n, end in enumerate(ends):
                split_pairs(done, end)
                done = end
                add_branch(n)

        @block.tensor
        def _(pe):
            def ada_product():
                for k in range(KD):
                    if k == KD // 2:
                        norm_sum(0)
                    pe.wait_ge(ada_second_loaded[k], 16)
                    for b in range(3):
                        mm = pe.matmul(psum[0:2, b, :], c_t[:, k, :], ada_second[k][:, b * 512:(b + 1) * 512],
                                       start=(k == 0), stop=(k == KD - 1))
                mm.then_inc(ada_rows_made, 1)

            def ada_turn_rows():
                pe.wait_ge(ada_rows_copied, 1)
                for t in range(2 * ADA_HALF // P):
                    mm = pe.transpose(psum[:, 6, 2 * t:2 * t + 2], ada_rows[:, t * P:(t + 1) * P], ident[0:2, 0:2])
                mm.then_inc(ada_rows_turned, 1)

            def ada_total(c, parts, part):
                pe.wait_ge(ada_used, 2 * KD * (c + 1))
                products = [(t, g) for t in range(parts * ADA_HALF // P) for g in range(2)]
                n = len(products) // 4
                for t, g in products[part * n:(part + 1) * n]:
                    mm = pe.matmul(psum[:, 7, 2 * t + g:2 * t + g + 1], ada_sum[:, g, t * P:(t + 1) * P],
                                   ones[:, 0:1], start=True, stop=True)
                if part == 3:
                    mm.then_inc(ada_turned, 1)

            def unit(u, n, hi, lo, ready=None, tail_ready=None):
                pe.wait_ge(w_split, 2 * n + u + 1)
                pe.wait_ge(bank_free[u], n + 1)
                for k in range(KD):
                    if ready:
                        ready(k)
                    for b in range(2):
                        w = slice(k * P, (k + 1) * P)
                        t = slice(b * HT, (b + 1) * HT)
                        for i, (a, m) in enumerate(((w_hi, hi), (w_hi, lo), (w_lo, hi))):
                            mm = pe.matmul(psum[:, 2 * u + b, 0:HT], a[:, u, w], m[:, k, t],
                                           start=(k == 0 and i == 0), stop=(k == KD - 1 and i == 2))
                mm.then_inc(unit_done, 1)

            def first_pair(n, hi, lo, ready):
                for u in range(2):
                    pe.wait_ge(bank_free[u], n + 1)
                pe.wait_ge(w_split, 2 * n + 2)
                lag = KD // 2
                for step in range(KD + lag):
                    for u in range(2):
                        k = step - lag * u
                        if not 0 <= k < KD:
                            continue
                        if u == 0:
                            ready(k)
                        for b in range(2):
                            w = slice(k * P, (k + 1) * P)
                            t = slice(b * HT, (b + 1) * HT)
                            for i, (a, m) in enumerate(((w_hi, hi), (w_hi, lo), (w_lo, hi))):
                                mm = pe.matmul(psum[:, 2 * u + b, 0:HT], a[:, u, w], m[:, k, t],
                                               start=(k == 0 and i == 0), stop=(k == KD - 1 and i == 2))
                        if k == KD - 1:
                            mm.then_inc(unit_done, 1)

            def y_sum(n):
                pe.wait_ge(sq_summed, KD * (n + 1))
                for b in range(2):
                    mm = pe.matmul(psum[:, 4 + b, 0:HT], ones[:], tmp[:, 0, b * HT:(b + 1) * HT], start=True, stop=True)
                mm.then_inc(y_sq_total, 1)

            def norm_sum(n):
                for k in range(KD):
                    pe.wait_ge(sq_ready, KD * n + k + 1)
                    for b in range(2):
                        mm = pe.matmul(psum[:, 4 + b, 0:HT], ones[:], sq[:, k % 2, b * HT:(b + 1) * HT],
                                       start=(k == 0), stop=(k == KD - 1))
                    mm.then_inc(sq_summed, 1)

            def ffn(f, n0, n_pre):
                def gate_up(n):
                    unit(0, n, h_hi, h_lo)
                    unit(1, n, h_hi, h_lo)

                def down(n, ready=None):
                    unit(0, n, hid_hi, hid_lo, ready)
                    unit(1, n, hid_hi, hid_lo)

                def downs(kb, first):
                    def ready(k):
                        pe.wait_ge(hid_ready, KD * (KB * f + kb) + k + 1)

                    if ADA_PARTS[f]:
                        for j in range(KD // 2):
                            unit(0, first + KD + j, hid_hi, hid_lo, None if j else ready)
                            ada_total(ADA_CHUNKS_BEFORE[f] + kb, ADA_PARTS[f], j)
                            unit(1, first + KD + j, hid_hi, hid_lo)
                    else:
                        down(first + KD, ready)
                        with pe.Fori(1, KD // 2) as j:
                            down(first + KD + j)

                first_pair(n0, h_hi, h_lo, lambda k: pe.wait_ge(h_ready, KD * n_pre + k + 1))
                with pe.Fori(1, KD) as j:
                    gate_up(n0 + j)
                downs(0, n0)
                with pe.Fori(1, KB) as kb:
                    first = n0 + kb * (FFN_PAIRS // KB)
                    with pe.Fori(0, KD) as j:
                        gate_up(first + j)
                    downs(kb, first)

            pe.wait_ge(c_ready, 1)
            pe.wait_ge(consts, 2)
            ada_product()
            for part in range(4):
                ada_total(0, 2, part)
            ada_turn_rows()
            ffn(0, FIRST["ffn0"], 0)
            y_sum(1)
            norm_sum(2)

            def product(first, pairs, hi, lo, ready=None):
                if ready:
                    first_pair(first, hi, lo, ready)
                with pe.Fori(first + bool(ready), first + pairs) as n:
                    unit(0, n, hi, lo)
                    unit(1, n, hi, lo)

            def rel_bias():
                pe.wait_ge(onehot_loaded, 16)
                for b in range(2):
                    mm = pe.matmul(psum[0:NH, 4 + b, 0:REL // 2], rel_sb[:], onehot[0:32, b * (REL // 2):(b + 1) * (REL // 2)],
                                   start=True, stop=True)
                mm.then_inc(rel_made, 1)

            def turn_weights(first):
                pe.wait_ge(bank_free[0], first + 2 + 2)
                pe.wait_ge(bank_free[1], first + 2 + 2)
                for i in range(5):
                    n = P if i < 4 else TS
                    mm = pe.transpose(psum[0:n, 6 + i // 4, (i % 4) * P:(i % 4 + 1) * P],
                                      z[:, Z_W, i * P:i * P + n], ident[:])
                mm.then_inc(wi_turned, 1)
                pe.wait_ge(cache_loaded["ik"], 16)

            def score_dots(e):
                i, h = score_items()[e]
                r, c = HD * (h % 2), Z_IQ + h // 2
                if e >= 2:
                    pe.wait_ge(relu_ready, e - 1)
                b = 4 + 2 * (e % 2)
                if e < 2:
                    pe.wait_ge(wi_ready, 1)
                if i == "s":
                    q = z[r:r + HD, c, TP:T]
                    pe.matmul(psum[0:TS, b, 0:HT], q, cache_ik[r:r + HD, 0:HT], start=True, stop=True)
                    pe.matmul(psum[0:TS, b + 1, 0:TP - HT], q, cache_ik[r:r + HD, HT:TP], start=True, stop=True)
                    mm = pe.matmul(psum[0:TS, b + 1, TP - HT:HT], q, z[r:r + HD, Z_IK, TP:T], start=True, stop=True)
                else:
                    mm = pe.matmul(psum[:, b, 0:keys_of(i)], z[r:r + HD, c, i * P:(i + 1) * P],
                                   z[r:r + HD, Z_IK, 0:keys_of(i)], start=True, stop=True)
                mm.then_inc(dots_done, 1)

            def turn_values(mixer, first):
                zv = Z_VA if mixer == "A" else Z_VB
                for b in range(5):
                    c = 5 * (mixer == "B") + b
                    n = P if b < 4 else TS
                    if c >= 2:
                        pe.wait_ge(v_ready, c - 1)
                    for d in range(4):
                        mm = pe.transpose(psum[0:n, 4 + c % 2, d * P:(d + 1) * P], z[:, zv + d, b * P:b * P + n], ident[:])
                    mm.then_inc(v_turned, 1)

            def logits(e):
                mixer, i, h = items[e]
                zq, zk = (Z_QA, Z_KA) if mixer == "A" else (Z_QB, Z_KB)
                b = 2 * (e % 2)
                if e >= 2:
                    pe.wait_ge(max_ready, e - 1)
                if i != "s":
                    n, r, c = keys_of(i), HD * (h % 2), h // 2
                    pe.matmul(psum[:, b, 0:n], z[r:r + HD, zq + c, i * P:(i + 1) * P], z[r:r + HD, zk + c, 0:n],
                              start=True, stop=False, skip_group_check=(mixer == "B"))
                    if mixer == "A":
                        mm = pe.matmul(psum[:, b, 0:n], ident[:], bias_p[:, h, TP - P * (i + 1):TP - P * (i + 1) + n],
                                       start=False, stop=True)
                    else:
                        pe.wait_ge(fox_ready, i + 1)
                        pe.matmul(psum[:, b, n - P:n], ident[:], diag_mask[:], start=False, stop=False,
                                  skip_group_check=True)
                        mm = pe.matmul(psum[:, b, 0:n], fox_q[:, h, :], fox_k[:, 0:n], start=False, stop=True,
                                       skip_group_check=True)
                else:
                    if mixer == "B":
                        pe.wait_ge(cache_loaded["B"], 32)
                    r = HD * h
                    for j in range(4):
                        q = z[r:r + HD, zq + j, TP:T]
                        rows = slice(TS * j, TS * (j + 1))
                        pe.matmul(psum[rows, b, 0:HT], q, cache_k[r:r + HD, j, 0:HT], start=True, stop=False,
                                  tile_position=(r, TS * j), skip_group_check=True)
                        pe.matmul(psum[rows, b + 1, 0:TP - HT], q, cache_k[r:r + HD, j, HT:TP], start=True, stop=False,
                                  tile_position=(r, TS * j), skip_group_check=True)
                        pe.matmul(psum[rows, b + 1, TP - HT:HT], q, z[r:r + HD, zk + j, TP:T], start=False, stop=False,
                                  tile_position=(r, TS * j), skip_group_check=True)
                    if mixer == "B":
                        pe.matmul(psum[:, b + 1, TP - HT:HT], ident[:], tail_mask[:], start=False, stop=False,
                                  skip_group_check=True)
                    for d in range(2):
                        if mixer == "A":
                            mm = pe.matmul(psum[:, b + d, 0:HT], ident[:], bias_s[:, h, d * HT:(d + 1) * HT],
                                           start=False, stop=True, skip_group_check=True)
                        else:
                            pe.wait_ge(fox_ready, 4)
                            mm = pe.matmul(psum[:, b + d, 0:HT], fox_qs[:, h, :], fox_k[:, TP + d * HT:TP + (d + 1) * HT],
                                           start=False, stop=True, skip_group_check=True)
                mm.then_inc(logits_done, 1)

            def turn_probs(e):
                _, i, _ = items[e]
                pe.wait_ge(p_ready, e + 1)
                if e >= 2:
                    pe.wait_ge(p_turn_ready, e - 1)
                for k in range(min(keys_of(i) // P, 4)):
                    mm = pe.transpose(psum[:, 4 + e % 2, k * P:(k + 1) * P], probs[:, e % 2, k * P:(k + 1) * P], ident[:])
                if i == "s":
                    pe.wait_ge(o_ready, group_of[e] - 1)
                    pe.wait_ge(p_turn_ready, e)
                    mm = pe.transpose(psum[0:TS, 6 + group_of[e] % 2, P:2 * P], probs[:, e % 2, TP:NK_S], ident[:])
                mm.then_inc(p_turn_done, 1)

            def values(e):
                mixer, i, h = items[e]
                pe.wait_ge(p_turn_ready, e + 1)
                g = group_of[e]
                if i == "s" and h == 0:
                    pe.wait_ge(p_turn_ready, e + 2)
                if g >= 2:
                    pe.wait_ge(o_ready, g - 1)
                o = 6 + g % 2
                if i != "s":
                    for k in range(i + 1):
                        mm = pe.matmul(psum[HD * (h % 2):HD * (h % 2) + HD, o, 0:P], v_tok[:, k, HD * h:HD * h + HD],
                                       p_turned[:, e % 2, k, :], start=(k == 0), stop=(k == i),
                                       tile_position=(0, HD * (h % 2)))
                else:
                    for j in range(4):
                        d = HD * (2 * j + h)
                        for k in range(5):
                            n = P if k < 4 else TS
                            mm = pe.matmul(psum[HD * h:HD * h + HD, o, TS * j:TS * (j + 1)],
                                           cache_v[0:n, k, d:d + HD], p_turned[0:n, e % 2, k, TS * j:TS * (j + 1)],
                                           start=(k == 0), stop=(k == 4), tile_position=(0, HD * h))
                mm.then_inc(av_done, 1)

            def attention(mixer):
                e0 = first_item[mixer]
                for s in range(e0, e0 + n_items + 3):
                    if s < e0 + n_items:
                        logits(s)
                    if e0 <= s - 2 < e0 + n_items:
                        turn_probs(s - 2)
                    if e0 <= s - 3:
                        values(s - 3)

            n0 = FIRST["ab_in"]
            product(n0, 3, h_hi, h_lo, lambda k: pe.wait_ge(h_ready, KD + k + 1))
            for m in range(6, SCORE_UNITS):
                unit(m % 2, n0 + m // 2, h_hi, h_lo)
                if m == 6:
                    rel_bias()
                    turn_weights(n0)
                for e in scores_after(m):
                    score_dots(e)
            product(n0 + SCORE_UNITS // 2, AB_PAIRS - SCORE_UNITS // 2, h_hi, h_lo)
            for u in range(2):
                pe.wait_ge(bank_free[u], n0 + AB_PAIRS + 1)
            turn_values("A", n0)
            pe.wait_ge(bias_loaded, 16)
            pe.wait_ge(bias_s_loaded, 16 * NH)
            pe.wait_ge(cache_loaded["A"], 32)
            attention("A")
            pe.wait_ge(p_turn_ready, n_items)
            turn_values("B", n0)
            attention("B")
            product(FIRST["ab_out"], OUT_PAIRS, h_hi, h_lo, lambda k: pe.wait_ge(o_ready, len(items) // 2))
            y_sum(3)
            norm_sum(4)
            ffn(1, FIRST["ffn1"], 2)
            y_sum(5)
            norm_sum(6)
            ffn(2, FIRST["ffn2"], 3)
            y_sum(7)
            norm_sum(8)

            def squared_lengths(m):
                pe.wait_ge(gdn_loaded, 16 * 5)
                pe.wait_ge(conv_sq_ready, m + 1)
                h = m % NH
                at = NH - 1 - h
                pe.matmul(psum[:, 4, :], strips[:, m // NH, at:at + P], conv_sq[:, m % 2, :], start=(m == 0),
                          stop=(m == 2 * NH - 1)).then_inc(lens_summed, 1)

            def sample_lengths():
                pe.wait_ge(sample_silu, 2)
                for m in range(2 * NH):
                    at = NH - 1 - m % NH
                    mm = pe.matmul(psum[:, 5, 0:TS], strips[:, m // NH, at:at + P], conv_tap[:, m, :], start=(m == 0),
                                   stop=(m == 2 * NH - 1))
                mm.then_inc(lens_summed, 1)

            def gdn_in():
                n0 = FIRST["gdn_in"]
                first_pair(n0, h_hi, h_lo, lambda k: pe.wait_ge(h_ready, KD * 4 + k + 1))
                for p in range(1, GDN_PAIRS):
                    unit(0, n0 + p, h_hi, h_lo)
                    unit(1, n0 + p, h_hi, h_lo)
                    for m in (2 * p - 6, 2 * p - 5):
                        if 0 <= m < 2 * NH:
                            squared_lengths(m)
                    if p == GDN_PAIRS - 3:
                        sample_lengths()

            def turn_rows():
                pe.wait_ge(rows_exp, 2)
                for t in range(TILES):
                    pe.transpose(psum[:, 6, t * P:(t + 1) * P], rows_e[:, t * P:(t + 1) * P], ident[:])
                pe.transpose(psum[:, 7, 0:P], rows_es, ident[:])
                pe.wait_ge(ends_ready, 2)
                pe.matmul(psum[:, 7, P:P + (CHUNKS + 1) * NH], ones[:], ends_by_head.rearrange("p c h -> p (c h)"),
                          start=True, stop=True).then_inc(rows_turned, 1)

            def gdn_products(q):
                u, b = q % 2, 4 * (q % 2)
                n = size(q)
                pe.wait_ge(lq_ready, q + 1)
                kc = (lambda t: rows_c[:, t * P:(t + 1) * P]) if q < NH else (lambda t: keys_s)
                for w, (at, lq, done) in enumerate(((GZ_K, t2, kk_done), (GZ_Q, low_m, kq_done))):
                    if q >= 2:
                        if w == 0:
                            pe.wait_ge(inv_ready, level_at(q - 2, levels_of(q - 2) - 1) + 1)
                        else:
                            pe.wait_ge(wu_out, q - 1)
                    for t in range(tiles_of(q)):
                        moving = gz[:, at + q, t * P:(t + 1) * P] if q < NH else z_item(at, q)
                        pe.matmul(psum[:, b + 2 * w, t * P:(t + 1) * P], z_tile(GZ_K, q, t), moving,
                                  start=True, stop=True)
                    pe.matmul(psum[:, b + 2 * w + 1, 0:n], ident[:],
                              g_mask[:, w + (2 if q >= NH else 0), :].unsqueeze(1).broadcast_to([P, tiles_of(q), P]),
                              start=True, stop=False, skip_group_check=True)
                    for t in range(tiles_of(q)):
                        l = lq[:, u, t * P:(t + 1) * P]
                        lhs, rhs = (l, kc(t)) if w == 0 else (kc(t), l)
                        mm = pe.matmul(psum[:, b + 2 * w + 1, t * P:(t + 1) * P], lhs, rhs,
                                       start=False, stop=True, skip_group_check=True)
                    mm.then_inc(done, 1)

            def query_factor(q):
                pe.wait_ge(kq_decayed, q + 1)
                pe.wait_ge(bc_ready, q + 1)
                pe.matmul(psum[:, 4 * (q % 2) + 2, 0:size(q)], ones[:], v_beta[:, q % 2, 0:size(q)], start=True, stop=True)\
                    .then_inc(q_factor, 1)

            def gdn_turn(q, at, free, done):
                pe.wait_ge(free, q + 1)
                for t in range(tiles_of(q)):
                    mm = pe.transpose(psum[:, 4 * (q % 2) + 2, t * P:(t + 1) * P], z_tile(at, q, t), ident[:])
                mm.then_inc(done, 1)

            def gdn_level(q, l):
                u, b = q % 2, 4 * (q % 2)
                tiles = [slice(t * P, (t + 1) * P) for t in range(tiles_of(q))]
                pe.wait_ge(low_ready, level_at(q, l) + 1)
                if l == 0:
                    pe.wait_ge(kq_exp, q + 1)
                    for t in tiles:
                        mm = pe.transpose(psum[:, b + 3, t], low_m[:, u, t], ident[:])
                    mm.then_inc(t2_made, 1)
                    return
                pe.wait_ge(inv_t_ready, level_at(q, l - 1) + 1)
                for t in tiles:
                    mm = pe.matmul(psum[:, b + 3, t], low_m[:, u, t], inv_t[:, u, t], start=True, stop=True)
                mm.then_inc(t2_made, 1)

            def gdn_level_ends(q, l):
                u, b = q % 2, 4 * (q % 2)
                tiles = [slice(t * P, (t + 1) * P) for t in range(tiles_of(q))]
                pe.wait_ge(t2_copied, copies_at(q, l) + 1)
                pe.wait_ge(inv_ready, level_at(q, l - 1) + 1)
                if l == 1:
                    pe.wait_ge(kk_decayed, q + 1)
                for t in tiles:
                    mm = pe.matmul(psum[:, b, t], inv[:, u, t], t2[:, u, t], start=True, stop=True)
                if l < levels_of(q) - 1:
                    for t in tiles:
                        mm = pe.matmul(psum[:, b + 1, t], t2[:, u, t], inv[:, u, t], start=True, stop=True)
                mm.then_inc(e_made, 1)

            def gdn_solved(q):
                u, b = q % 2, 4 * (q % 2)
                pe.wait_ge(inv_ready, level_at(q, levels_of(q) - 1) + 1)
                pe.wait_ge(v_scaled, q + 1)
                for w in range(2):
                    for t in range(tiles_of(q)):
                        t = slice(t * P, (t + 1) * P)
                        lhs, rhs = (k_beta[:, u, t], inv_t[:, u, t]) if w == 0 else (inv_t[:, u, t], v_beta[:, u, t])
                        mm = pe.matmul(psum[:, b + 2 + w, t], lhs, rhs, start=True, stop=True)
                mm.then_inc(wu_made, 1)

            def recur_v(n):
                c, h = steps[n]
                if n >= 2:
                    pe.wait_ge(v_new_ready, n - 1)
                if n >= 2 * NH:
                    pe.wait_ge(state_new, n - NH + 1)
                m, r, state = (TS, TS * (h % 4), state_s) if c == "s" else (CHUNK, CHUNK * (c % 2), state_p)
                t = slice(TP, T) if c == "s" else slice(CHUNK * c, CHUNK * (c + 1))
                pe.matmul(psum[r:r + m, n % 2, 0:P], w_neg[:, h, t], state[:, h, :], start=True, stop=True,
                          tile_position=(0, r)).then_inc(v_made, 1)

            def recur_os(n):
                c, h = steps[n]
                pe.wait_ge(v_new_ready, n + 1)
                if n >= 2:
                    pe.wait_ge(o_out, n - 1)
                    pe.wait_ge(state_new, n - 1)
                m, r, state = (TS, TS * (h % 4), state_s) if c == "s" else (CHUNK, CHUNK * (c % 2), state_p)
                t = slice(TP, T) if c == "s" else slice(CHUNK * c, CHUNK * (c + 1))
                if c == "s":
                    k = slice(r, r + m)
                    qk, kd, v, at = qk_s[k, h // 4, k], kdec_s[k, h // 4, :], v_new[k, 2, n % 2, :], (r, 0)
                else:
                    qk, kd, v, at = qk_t[:, h, t], gz[:, GZ_K + h, c // 2 * P:(c // 2 + 1) * P], v_new[:, c % 2, n % 2, :], (0, 0)
                pe.matmul(psum[:, 2 + n % 2, 0:m], state[:, h, :], gz[:, GZ_Q + h, t], start=True, stop=False)
                pe.matmul(psum[:, 2 + n % 2, 0:m], v, qk, start=False, stop=True, tile_position=at)\
                    .then_inc(o_made, 1)
                pe.matmul(psum[:, 4 + n % 2, 0:P], kd, v, start=True, stop=True, tile_position=at)\
                    .then_inc(kv_made, 1)

            def gated_norm_sums():
                pe.wait_ge(state_new, len(steps))
                for h in range(NH):
                    pe.wait_ge(g_sq_ready, h + 1)
                    if h >= 2:
                        pe.wait_ge(g_ln_done, h - 1)
                    for b in range(2):
                        mm = pe.matmul(psum[:, 4 + 2 * (h % 2) + b, 0:HT], ones[:], g_sq[:, h % 2, b * HT:(b + 1) * HT],
                                       start=True, stop=True)
                    mm.then_inc(g_sq_summed, 1)

            gdn_in()
            turn_rows()
            pe.wait_ge(gdn_masks, 16)
            pe.wait_ge(cols_ready, 1)
            for q0 in range(0, G_ITEMS, 2):
                pair = (q0, q0 + 1)
                for step in (gdn_products, query_factor):
                    for q in pair:
                        step(q)
                for l in range(levels_of(q0)):
                    for q in pair:
                        gdn_level(q, l)
                    for q in pair:
                        if l == 2:
                            gdn_turn(q, GZ_K, q_scaled, k_turned)
                        elif l == 4:
                            gdn_turn(q, GZ_V, k_scaled, v_turned_g)
                    if l:
                        for q in pair:
                            gdn_level_ends(q, l)
                for q in pair:
                    gdn_solved(q)
            pe.wait_ge(wu_out, G_ITEMS)
            pe.wait_ge(gdn_state, 16)
            for n in range(len(steps) + 2):
                if n < len(steps):
                    recur_v(n)
                if n >= 2:
                    recur_os(n - 2)
            gated_norm_sums()
            product(FIRST["gdn_out"], OUT_PAIRS, h_hi, h_lo, lambda k: pe.wait_ge(g_ready, k + 1))
            y_sum(9)
            norm_sum(10)
            ffn(3, FIRST["ffn3"], 5)
            y_sum(11)


        @block.scalar
        def _(act):
            def squares(n, src, ready=None, then=None):
                for k in range(KD):
                    if ready:
                        ready(k)
                    if KD * n + k >= 2:
                        act.wait_ge(sq_summed, KD * n + k - 1)
                    if k == KD - 1 and (n % 2 or n == 0):
                        act.preload_act_table_set(LN_EXP)
                    act.activation(sq[:, k % 2], src[:, k], ACT.Square).then_inc(sq_ready, 1)
                    if then and k:
                        then(k - 1)
                if then:
                    then(KD - 1)

            def gated(n, k):
                act.wait_ge(sq_ready, KD * n + k + 1)
                for g, (a, b) in enumerate(GROUPS):
                    op = act.activation(y[:, k, a:b], y[:, k, a:b], ACT.Copy, scale=gate_out[:, n // 2, k, g:g + 1])
                op.then_inc(y_gated, 1)

            def y_squares(n, ready):
                act.wait_ge(cond_ready, 2 * (n // 2) + 2)
                squares(n, y, ready, lambda k: gated(n, k))

            def x_added(n, k):
                if k in POOL_TILES:
                    act.wait_ge(x_ready_pool, len(POOL_TILES) * n + POOL_TILES.index(k) + 1)
                else:
                    act.wait_ge(x_ready, DVE_TILES * n + k - sum(t < k for t in POOL_TILES) + 1)

            def y_evacuated(n0, k):
                act.wait_ge(bank_free[k % 2], n0 + FFN_PAIRS - KD // 2 + k // 2 + 2)

            def rsqrt_mean(n):
                if n % 2:
                    act.wait_ge(y_sq_total, n // 2 + 1)
                else:
                    act.wait_ge(sq_summed, KD * (n + 1))
                act.activation(split(lnv), halves(4), ACT.Ln, bias=eps_col[:], scale=1.0 / D).then_inc(ln_done, 1)
                act.wait_ge(ln_done, n + 1)
                act.activation(rstd, lnv, ACT.Exp, scale=-0.5).then_inc(rstd_ready, 1)

            def modulate(n, sub):
                for k in range(KD):
                    act.wait_ge(scaled, KD * n + k + 1)
                    if KD * n + k >= 2:
                        act.wait_ge(h_ready, KD * n + k - 1)
                    for to in (h32[:, k % 2], h_hi[:, k])[:2 - k % 2]:
                        for g, (a, b) in enumerate(GROUPS):
                            op = act.activation(to[:, a:b], tmp[:, k % 2, a:b], ACT.Identity,
                                                scale=scale_in[:, sub, k, g:g + 1],
                                                bias=mod[:, (sub * 3) * KD + k, g:g + 1])
                    op.then_inc(h32_ready, 1)

            def ada_load(c, k, half, halves_in):
                act.wait_ge(ada_used, 2 * (KD * (c - 1) + k + 1))
                act.dma_start(ada_w[:, k, 0:halves_in * ADA_HALF].rearrange("p (h n) -> p h n", h=halves_in),
                              io["ada_w"][bass.ds(half, halves_in), k].rearrange("h p n -> p h n"))\
                    .then_inc(ada_loaded[k], 16)

            def ffn(f, n0):
                with act.Fori(0, KB) as kb:
                    for j in range(KD):
                        if ADA_PARTS[f]:
                            g = ADA_PARTS[f]
                            ada_load(ADA_CHUNKS_BEFORE[f] + kb, j, ADA_FIRST_HALF[f] + kb * g, g)
                        n = n0 + kb * (3 * KD // 2) + j
                        act.wait_ge(unit_done, 2 * n + 1)
                        act.activation(split(silu[:, j % 2]), halves(0), ACT.Silu).then_inc(bank_free[0], 1)

            act.dma_start(c_t[:], io["c_t"]).then_inc(c_loaded, 16)
            for k in range(KD):
                for c, to in enumerate((ada_w[:, k], ada_second[k])):
                    act.dma_start(to.rearrange("p (h n) -> p h n", h=2),
                                  io["ada_w"][2 * c:2 * c + 2, k].rearrange("h p n -> p h n"))\
                        .then_inc((ada_loaded, ada_second_loaded)[c][k], 16)
            act.wait_ge(c_loaded, 16)
            act.activation(c_t[:], c_t[:], ACT.Silu).then_inc(c_ready, 1)
            act.wait_ge(in_loaded, 16 * N_IN)
            squares(0, x)
            rsqrt_mean(0)
            act.wait_ge(ada_rows_made, 1)
            act.activation(ada_rows.rearrange("p (b n) -> p b n", b=3), psum[0:2, 0:3, :], ACT.Copy)\
                .then_inc(ada_rows_copied, 1)
            modulate(0, 0)
            ffn(0, FIRST["ffn0"])
            y_squares(1, lambda k: y_evacuated(FIRST["ffn0"], k))
            rsqrt_mean(1)
            squares(2, x, lambda k: x_added(0, k))
            rsqrt_mean(2)
            modulate(1, 1)

            def z_out(n0, m, scale=1.0):
                act.wait_ge(unit_done, 2 * n0 + m + 1)
                act.activation(split(z[:, m]), halves(2 * (m % 2)), ACT.Copy, scale=scale)\
                    .then_inc(bank_free[m % 2], 1)

            def store(name, src):
                act.dma_start(io[name].rearrange("(k p) t -> p k t", p=P), src).then_inc(state_stored, 16)

            def spread_rel():
                act.wait_ge(rel_made, 1)
                for b in range(2):
                    op = act.activation(fb[0:NH, b * (REL // 2):(b + 1) * (REL // 2)], psum[0:NH, 4 + b, 0:REL // 2], ACT.Copy)
                op.then_inc(rel_copied, 1)
                act.wait_ge(rel_copied, 1)
                act.dma_start(bass.AP(io["rel_spread"].tensor, 0, [[REL_AT, NH], [REL + 1, P], [1, REL]]),
                              fb[0:NH, :].unsqueeze(1).broadcast_to([NH, P, REL])).then_inc(rel_spread, 16)

            def load_biases():
                act.wait_ge(rel_spread, 16)
                act.dma_start(bias_p, bass.AP(io["rel_spread"].tensor, 2 * P - 1, [[REL, P], [REL_AT, NH], [1, 4 * P]]))\
                    .then_inc(bias_loaded, 16)

            def load_sample_biases():
                act.wait_ge(score_added, 4 * NH)
                for h in range(NH):
                    act.dma_start(bias_s[TS * (h // 2):TS * (h // 2 + 1), h % 2, :],
                                  bass.AP(io["rel_spread"].tensor, h * REL_AT + P - 1, [[REL, TS], [1, NK_S]]))\
                        .then_inc(bias_s_loaded, 16)

            def load_cache(mixer):
                act.dma_start(cache_k, io[f"cache_{mixer}_k"].rearrange("(k p) t -> p k t", p=P))\
                    .then_inc(cache_loaded[mixer], 16)
                act.dma_start(cache_v[:, 0:4, :], io[f"cache_{mixer}_v"].rearrange("(b p) d -> p b d", p=P))\
                    .then_inc(cache_loaded[mixer], 16)

            def weights_out():
                act.wait_ge(wi_turned, 1)
                act.activation(wi_tok[:, 0:4, :], psum[:, 6, :].rearrange("p (i r) -> p i r", r=P)[:, :, 0:NH],
                               ACT.Copy, scale=NH ** -0.5)
                act.activation(wi_tok[0:TS, 4, :], psum[0:TS, 7, 0:NH], ACT.Copy, scale=NH ** -0.5).then_inc(wi_ready, 1)

            def relu_out(e):
                i, h = score_items()[e]
                act.wait_ge(dots_done, e + 1)
                if e >= 2:
                    act.wait_ge(score_added, e - 1)
                b = 4 + 2 * (e % 2)
                if i == "s":
                    op = act.activation(split(relu[0:TS, e % 2]), psum[0:TS, b:b + 2, 0:HT], ACT.Relu)
                else:
                    op = act.activation(relu[:, e % 2, 0:keys_of(i)], psum[:, b, 0:keys_of(i)], ACT.Relu)
                op.then_inc(relu_ready, 1)

            def values_out(mixer):
                for b in range(5):
                    c = 5 * (mixer == "B") + b
                    act.wait_ge(v_turned, c + 1)
                    if b < 4:
                        op = act.activation(v_tok[:, b, :], psum[:, 4 + c % 2, :], ACT.Copy)
                    else:
                        op = act.activation(cache_v[0:TS, 4, :], psum[0:TS, 4 + c % 2, :], ACT.Copy)
                    op.then_inc(v_ready, 1)

            def exps(e):
                _, i, _ = items[e]
                n = keys_of(i)
                act.wait_ge(max_ready, e + 1)
                if e >= 2:
                    act.wait_ge(p_turn_done, e - 1)
                act.activation(probs[:, e % 2, 0:n], neg_logits[:, e % 2, 0:n], ACT.Exp, scale=-1.0,
                               bias=neg_max[:, e % 2:e % 2 + 1], accum_out=p_sum[:, e % 2:e % 2 + 1])\
                    .then_inc(exp_done, 1)

            def probs_out(e):
                _, i, _ = items[e]
                act.wait_ge(p_turn_done, e + 1)
                if e >= 2:
                    act.wait_ge(av_done, e - 1)
                k = min(keys_of(i) // P, 4)
                op = act.activation(p_turned[:, e % 2, 0:k, :].rearrange("p k q -> p (k q)"),
                                    psum[:, 4 + e % 2, 0:k * P], ACT.Copy)
                if i == "s":
                    op = act.activation(p_turned[0:TS, e % 2, 4, :], psum[0:TS, 6 + group_of[e] % 2, P:2 * P],
                                        ACT.Copy)
                op.then_inc(p_turn_ready, 1)

            def attention(mixer):
                e0 = first_item[mixer]
                for s in range(e0, e0 + n_items + 2):
                    if s < e0 + n_items:
                        exps(s)
                    if e0 <= s - 2:
                        probs_out(s - 2)

            def forget_logs():
                r = slice(FOX_ROW, FOX_ROW + NH)
                act.preload_act_table_set(LN_EXP)
                v, a, ex, ln = (fox_w[r, k, :] for k in range(4))
                steps = ((v, z[r, Z_W, :], ACT.Identity, dict(bias=b_f[r, :])), (a, v, ACT.Abs, {}),
                         (ex, a, ACT.Exp, dict(scale=-1.0)), (ln, ex, ACT.Ln, dict(bias=one_col[r, :])))
                for k, (to, of, func, how) in enumerate(steps):
                    act.activation(to, of, func, **how).then_inc(fox_own, 1)
                    act.wait_ge(fox_own, k + 1)

            n0 = FIRST["ab_in"]
            act.dma_start(onehot[0:32, :], io["onehot"]).then_inc(onehot_loaded, 16)
            act.dma_start(cache_ik, io["cache_ik"]).then_inc(cache_loaded["ik"], 16)
            load_cache("A")
            act.dma_start(fox_f[FOX_ROW:FOX_ROW + NH, TP:2 * TP], io["cache_logf"]).then_inc(fox_loaded, 16)
            for m in range(6):
                z_out(n0, m, HD ** -0.5 if Z_IQ <= m < Z_KA else 1.0)
            for m in range(6, Z_TILES):
                z_out(n0, m, HD ** -0.5 if Z_QA <= m < Z_VA or Z_QB <= m < Z_VB else 1.0)
                if m == 6:
                    spread_rel()
                    weights_out()
                for e in scores_after(m):
                    relu_out(e)
                if m == Z_VA - 1:
                    load_biases()
                if m == SCORE_UNITS:
                    load_sample_biases()
                    forget_logs()
                if m == SCORE_UNITS + 4:
                    act.wait_ge(fox_copied, 1)
                    act.dma_start(io["b_logf"], fox_w[FOX_ROW:FOX_ROW + NH, 0, :]).then_inc(logf_stored, 16)
            for u in range(2):
                act.wait_ge(bank_free[u], n0 + AB_PAIRS + 1)
            store("a_k", z[:, Z_KA:Z_KA + 4])
            store("a_v", z[:, Z_VA:Z_VA + 4])
            store("b_k", z[:, Z_KB:Z_KB + 4])
            store("b_v", z[:, Z_VB:Z_VB + 4])
            act.dma_start(io["a_ik"], z[0:HD, Z_IK, :]).then_inc(state_stored, 16)
            act.wait_ge(fox_summed, 1)
            values_out("A")
            attention("A")
            act.wait_ge(av_done, n_items)
            load_cache("B")
            values_out("B")
            attention("B")
            y_squares(3, lambda k: act.wait_ge(bank_free[k % 2], FIRST["ab_out"] + k // 2 + 2))
            rsqrt_mean(3)

            def pre_norm(n, norm):
                squares(norm, x, lambda k: x_added(n - 1, k))
                rsqrt_mean(norm)
                modulate(n, n)

            def feed_forward(f, n, norm, name):
                pre_norm(n, norm)
                ffn(f, FIRST[name])
                y_squares(norm + 1, lambda k: y_evacuated(FIRST[name], k))
                rsqrt_mean(norm + 1)

            feed_forward(1, 2, 4, "ffn1")
            feed_forward(2, 3, 6, "ffn2")
            act.wait_ge(ada_turned, 1 + 3 * KB)
            for name, to in (("strips", strips), ("g_sel", g_sel), ("g_col", g_col), ("conv_w", conv_w),
                             ("conv_before", conv_before)):
                act.dma_start(to, io[name]).then_inc(gdn_loaded, 16)
            pre_norm(4, 8)

            n0 = FIRST["gdn_in"]
            done = [0]

            def in_turn(ins):
                done[0] += 1
                ins.then_inc(row_own, 1)
                act.wait_ge(row_own, done[0])

            def one_plus_exp(v, to):
                in_turn(act.activation(to, v, ACT.Abs))
                in_turn(act.activation(to, to, ACT.Exp, scale=-1.0))
                act.activation(to, to, ACT.Ln, bias=one_col[:]).then_inc(rows_lin, 1)

            def conv_load(m):
                act.wait_ge(unit_done, 2 * n0 + m + 3)
                if m >= 2:
                    act.wait_ge(conv_done, m - 1)
                b = 2 * (m % 2)
                act.activation(split(conv_in[:, m % 2, CW - 1:]), halves(b), ACT.Copy)
                act.activation(conv_s[:, m, CW - 1:], psum[:, b + 1, HT - TS:HT], ACT.Copy)\
                    .then_inc(bank_free[m % 2], 1)

            def conv_store(m):
                act.wait_ge(conv_done, m + 1)
                act.activation(gz[:, m, 0:TP], conv_acc[:, m % 2], ACT.Silu).then_inc(conv_silu, 1)
                if m < 2 * NH:
                    act.wait_ge(conv_silu, m + 1)
                    if m >= 2:
                        act.wait_ge(lens_summed, m - 1)
                    act.activation(conv_sq[:, m % 2], gz[:, m, 0:TP], ACT.Square).then_inc(conv_sq_ready, 1)

            def gate_out_silu(j):
                m = QKV + j
                act.wait_ge(unit_done, 2 * n0 + m + 3)
                act.activation(split(gz[:, GZ_G + j]), halves(2 * (m % 2)), ACT.Silu).then_inc(bank_free[m % 2], 1)

            act.wait_ge(gdn_loaded, 16 * 5)
            act.wait_ge(unit_done, 2 * n0 + 1)
            act.activation(split(row_a), halves(0), ACT.Identity, bias=g_col[:, 0:1]).then_inc(bank_free[0], 1)
            act.wait_ge(unit_done, 2 * n0 + 2)
            act.activation(split(row_b), halves(2), ACT.Copy).then_inc(bank_free[1], 1)
            act.wait_ge(bank_free[0], n0 + 2)
            act.wait_ge(bank_free[1], n0 + 2)
            act.preload_act_table_set(LN_EXP)
            one_plus_exp(row_a, row_sp)
            one_plus_exp(row_b, row_lb)
            act.activation(g_col[:, 3:4], g_col[:, 1:2], ACT.Exp).then_inc(rows_lin, 1)
            act.wait_ge(conv_zeroed, 1)
            for m in range(QKV + 1):
                if m < QKV:
                    conv_load(m)
                if m:
                    conv_store(m - 1)
            gate_out_silu(0)
            gate_out_silu(1)
            act.wait_ge(sample_conv, 1)
            act.activation(gz[:, 0:QKV, TP:T], conv_sum, ACT.Silu).then_inc(sample_silu, 1)
            act.wait_ge(sample_silu, 1)
            act.activation(conv_tap[:, 0:2 * NH, :], gz[:, 0:2 * NH, TP:T], ACT.Square).then_inc(sample_silu, 1)
            for j in range(2, NH - 2):
                gate_out_silu(j)
            act.wait_ge(conv_done, QKV + 1)
            act.dma_start(io["p_conv"].rearrange("(k p) j -> p k j", p=P), conv_last).then_inc(state_stored, 16)
            act.dma_start(io["s_conv"].rearrange("(k p) j -> p k j", p=P), conv_s[:, :, TS:]).then_inc(state_stored, 16)
            act.wait_ge(lens_summed, 2 * NH + 1)
            act.dma_start(g_mask, io["g_mask"]).then_inc(gdn_masks, 16)
            act.dma_start(state_s, io["state_rec"].rearrange("h d e -> d h e")).then_inc(gdn_state, 16)
            act.preload_act_table_set(LN_EXP)
            act.activation(row_lr[:, 0:TP], psum[:, 4, :], ACT.Ln, bias=eps_col[:])
            act.activation(row_lr[:, TP:T], psum[:, 5, 0:TS], ACT.Ln, bias=eps_col[:]).then_inc(lens_ln, 1)
            gate_out_silu(NH - 2)
            act.wait_ge(rows_ready, 2)
            act.activation(rows_es.rearrange("p (h n) -> p h n", n=TS), rows_e[:, TP:T].unsqueeze(1)
                           .broadcast_to([P, 4, TS]), ACT.Exp)
            act.activation(ends, ends, ACT.Exp).then_inc(rows_exp, 1)
            act.activation(rows_e[:, 0:TP], rows_e[:, 0:TP], ACT.Exp).then_inc(rows_exp, 1)
            for to, at in ((kdec_s, GZ_K), (u_s, GZ_V)):
                act.activation(to.rearrange("p g (j n) -> p (g j) n", n=TS), gz[:, at:at + NH, TP:T], ACT.Copy)
            act.activation(keys_s.rearrange("p (h n) -> p h n", n=TS), rows_c[:, TP:T].unsqueeze(1)
                           .broadcast_to([P, 4, TS]), ACT.Copy).then_inc(rows_exp, 1)
            gate_out_silu(NH - 1)
            act.preload_act_table_set(LN_EXP)
            act.wait_ge(rows_exp, 3)

            def pick(to, of, of_s, kind, q):
                if q < NH:
                    return act.activation(to, of[:, 0:TP], ACT.Copy, scale=g_sel[:, kind, q:q + 1])
                for j in range(4):
                    h = 4 * (q - NH) + j
                    op = act.activation(to[:, j * TS:(j + 1) * TS], of_s, ACT.Copy, scale=g_sel[:, kind, h:h + 1])
                return op

            def gdn_rows(q):
                u, n = q % 2, size(q)
                if q >= 2:
                    act.wait_ge(e_made, copies_at(q - 2, levels_of(q - 2) - 1) + 1)
                pick(t2[:, u, 0:n], rows_r, rows_r[:, TP:T], 0, q)
                pick(low_m[:, u, 0:n], rows_r, rows_r[:, TP:T], 1, q).then_inc(lq_ready, 1)

            def gdn_exps(q):
                u, n, b = q % 2, size(q), 4 * (q % 2)
                act.wait_ge(kk_done, q + 1)
                act.activation(t2[:, u, 0:n], psum[:, b + 1, 0:n], ACT.Exp).then_inc(kk_exp, 1)
                act.wait_ge(kq_done, q + 1)
                act.activation(low_m[:, u, 0:n], psum[:, b + 3, 0:n], ACT.Exp).then_inc(kq_exp, 1)
                pick(v_beta[:, u, 0:n], rows_e, rows_es[:, 0:TS], 2, q).then_inc(bc_ready, 1)

            def gdn_copy(q, l):
                u, n, b = q % 2, size(q), 4 * (q % 2)
                act.wait_ge(t2_made, level_at(q, l) + 1)
                act.activation(t2[:, u, 0:n], psum[:, b + 3, 0:n], ACT.Copy).then_inc(t2_copied, 1)

            def gdn_solved(q):
                u, n, b = q % 2, size(q), 4 * (q % 2)
                act.wait_ge(wu_made, q + 1)
                if q < NH:
                    act.activation(w_neg[:, q, 0:TP], psum[:, b + 2, :], ACT.Copy, scale=-1.0)
                    act.activation(gz[:, GZ_V + q, 0:TP], psum[:, b + 3, :], ACT.Copy).then_inc(wu_out, 1)
                else:
                    act.activation(w_neg[:, sample_heads(q), TP:T], as_heads(psum[:, b + 2, 0:P]), ACT.Copy, scale=-1.0)
                    act.activation(u_s[:, q - NH, :], psum[:, b + 3, 0:P], ACT.Copy).then_inc(wu_out, 1)

            act.wait_ge(state_stored, 16 * 7)
            for q in range(2):
                gdn_rows(q)
            for q0 in range(0, G_ITEMS, 2):
                pair = (q0, q0 + 1)
                for q in pair:
                    gdn_exps(q)
                for l in range(1, levels_of(q0)):
                    for q in pair:
                        gdn_copy(q, l)
                if q0 + 2 < G_ITEMS:
                    for q in pair:
                        gdn_rows(q + 2)
                for q in pair:
                    gdn_solved(q)
            for n, (c, h) in enumerate(steps):
                m, t = (TS, slice(TP, T)) if c == "s" else (CHUNK, slice(CHUNK * c, CHUNK * (c + 1)))
                act.wait_ge(o_made, n + 1)
                act.activation(gz[:, GZ_Q + h, t], psum[:, 2 + n % 2, 0:m], ACT.Copy).then_inc(o_out, 1)
            act.wait_ge(o_out, len(steps))
            for h in range(NH + 1):
                if h < NH:
                    if h >= 2:
                        act.wait_ge(g_sq_summed, h - 1)
                    act.activation(g_sq[:, h % 2], gz[:, GZ_Q + h], ACT.Square).then_inc(g_sq_ready, 1)
                if h:
                    e = h - 1
                    act.wait_ge(g_sq_summed, e + 1)
                    act.activation(split(g_rstd[:, e]), halves(4 + 2 * (e % 2)), ACT.Ln, bias=eps_col[:],
                                   scale=1.0 / P).then_inc(g_ln_done, 1)
                    act.wait_ge(g_ln_done, e + 1)
                    act.activation(g_rstd[:, e], g_rstd[:, e], ACT.Exp, scale=-0.5).then_inc(g_rstd_ready, 1)
            act.wait_ge(state_new, len(steps))
            act.dma_start(io["p_rec"].rearrange("h d e -> d h e"), state_p).then_inc(state_stored, 16)
            act.dma_start(io["s_rec"].rearrange("h d e -> d h e"), state_s).then_inc(state_stored, 16)
            y_squares(9, lambda k: act.wait_ge(bank_free[k % 2], FIRST["gdn_out"] + k // 2 + 2))
            rsqrt_mean(9)
            feed_forward(3, 5, 10, "ffn3")

        @block.vector
        def _(dve):
            own = [0]

            def then(ins):
                own[0] += 1
                ins.then_inc(dve_own, 1)
                dve.wait_ge(dve_own, own[0])

            dve.memset(one_col[:], 1.0).then_inc(consts, 1)
            dve.memset(rstd, 0.0).then_inc(bank_free[0], 1)
            dve.memset(lnv, 0.0).then_inc(bank_free[1], 1)
            dve.memset(ones[:], 1.0).then_inc(consts, 1)
            dve.wait_ge(consts, 2)
            then(dve.memset(y, 0.0))

            def ada_step(c, k, parts, head=False):
                n = parts * ADA_HALF
                if k == 0 and not head:
                    dve.wait_ge(ada_turned, c)
                for g in range(2):
                    dve.wait_ge(ada_loaded[k], 16 * (c + 1))
                    if k == 0:
                        op = dve.tensor_scalar(ada_sum[:, g, 0:n], ada_w[:, k, 0:n], c_t[:, k, g:g + 1], None, ALU.mult)
                    else:
                        dve.wait_ge(ada_used, 2 * (KD * c + k - 1) + g + 1)
                        op = dve.scalar_tensor_tensor(ada_sum[:, g, 0:n], ada_w[:, k, 0:n], c_t[:, k, g:g + 1],
                                                      ada_sum[:, g, 0:n], ALU.mult, ALU.add)
                    op.then_inc(ada_used, 1)

            def ada_add(ready, at, parts, bank=7):
                tiles = parts * ADA_HALF // P
                dve.wait_ge(*ready)
                dve.tensor_tensor(mod[:, bass.ds(at, tiles), :], psum[:, bank, 0:2 * tiles].rearrange("p (t g) -> p t g", g=2),
                                  ada_b[:, bass.ds(at, tiles)].unsqueeze(2).broadcast_to([P, tiles, 2]), ALU.add)\
                    .then_inc(ada_added, 1)

            def conditions(s):
                g1 = g_pre[:, s * KD:(s + 1) * KD].unsqueeze(2).broadcast_to([P, KD, 2])
                g2 = g_post[:, s * KD:(s + 1) * KD].unsqueeze(2).broadcast_to([P, KD, 2])
                dve.scalar_tensor_tensor(scale_in[:, s], mod[:, (3 * s + 1) * KD:(3 * s + 2) * KD], 1.0, g1,
                                         ALU.add, ALU.mult).then_inc(cond_ready, 1)
                weight = 1.0 if s % SUBS == 1 else 0.5
                dve.scalar_tensor_tensor(gate_out[:, s], mod[:, (3 * s + 2) * KD:(3 * s + 3) * KD], weight, g2,
                                         ALU.mult, ALU.mult).then_inc(cond_ready, 1)
                dve.wait_ge(cond_ready, 2 * s + 2)

            dve.wait_ge(c_ready, 1)
            for k in range(KD):
                ada_step(0, k, 2, head=True)
            dve.wait_ge(in_loaded, 16 * N_IN)
            ada_add((ada_turned, 1), 0, 2)
            ada_add((ada_rows_turned, 1), 2 * ADA_HALF // P, 2, 6)
            dve.wait_ge(ada_added, ADA_HEAD)
            conditions(0)

            def normalise(n, n_norm, sums_start=False):
                if sums_start:
                    dve.wait_ge(x_ready_pool, len(POOL_TILES) * n)
                    dve.wait_ge(x_ready, DVE_TILES * n)
                    then(dve.memset(y, 0.0))
                dve.wait_ge(rstd_ready, n_norm + 1)
                for k in range(KD + 1):
                    if k < KD:
                        if KD * n + k >= 2:
                            dve.wait_ge(h32_ready, KD * n + k - 1)
                        dve.tensor_tensor(tmp[:, k % 2], x[:, k], rstd, ALU.mult).then_inc(scaled, 1)
                    if k > 0:
                        dve.wait_ge(h32_ready, KD * n + k)
                        if k % 2 == 0:
                            dve.tensor_copy(h_hi[:, k - 1], h32[:, (k - 1) % 2]).then_inc(h_rounded, 1)
                            dve.wait_ge(h_rounded, (KD * n + k) // 2)
                        dve.tensor_tensor(h_lo[:, k - 1], h32[:, (k - 1) % 2], h_hi[:, k - 1].bitcast(F32),
                                          ALU.subtract).then_inc(h_ready, 1)

            def y_squares(n, k):
                dve.wait_ge(sq_ready, KD * n + k + 1)
                if k == 0:
                    dve.tensor_copy(tmp[:, 0], sq[:, 0]).then_inc(sq_summed, 1)
                else:
                    dve.wait_ge(sq_summed, KD * n + k)
                    dve.tensor_tensor(tmp[:, 0], tmp[:, 0], sq[:, k % 2], ALU.add).then_inc(sq_summed, 1)

            def ffn(f, n0, n_norm):
                def block_of(kb, last):
                    q = KD * (KB * f + kb)
                    for j in range(KD):
                        n = n0 + kb * (3 * KD // 2) + j
                        dve.wait_ge(unit_done, 2 * n + 2)
                        dve.wait_ge(bank_free[0], n + 2)
                        dve.tensor_tensor(split(h32[:, j % 2]), split(silu[:, j % 2]), halves(2), ALU.mult)\
                            .then_inc(bank_free[1], 1)
                        dve.wait_ge(bank_free[1], n + 2)
                        dve.tensor_copy(hid_hi[:, j], h32[:, j % 2]).then_inc(hid_rounded, 1)
                        dve.wait_ge(hid_rounded, q + j + 1)
                        dve.tensor_tensor(hid_lo[:, j], h32[:, j % 2], hid_hi[:, j].bitcast(F32), ALU.subtract)\
                            .then_inc(hid_ready, 1)
                        if ADA_PARTS[f]:
                            ada_step(ADA_CHUNKS_BEFORE[f] + kb, j, ADA_PARTS[f])
                    for m in range(KD):
                        n = n0 + kb * (3 * KD // 2) + KD + m // 2
                        dve.wait_ge(unit_done, 2 * n + m % 2 + 1)
                        dve.tensor_tensor(split(y[:, m]), split(y[:, m]), halves(2 * (m % 2)), ALU.add)\
                            .then_inc(bank_free[m % 2], 1)
                        if m == KD - 1 and ADA_PARTS[f]:
                            ada_add((ada_turned, ADA_CHUNKS_BEFORE[f] + kb + 1), 6 * ADA_FIRST_HALF[f] + kb * (6 * ADA_PARTS[f]),
                                    ADA_PARTS[f])
                        if last and m:
                            y_squares(n_norm, m - 1)

                with dve.Fori(0, KB - 1) as kb:
                    block_of(kb, False)
                block_of(KB - 1, True)
                y_squares(n_norm, KD - 1)

            def y_copied(first, n_norm):
                for m in range(KD):
                    dve.wait_ge(unit_done, 2 * first + m + 1)
                    dve.tensor_copy(split(y[:, m]), halves(2 * (m % 2))).then_inc(bank_free[m % 2], 1)
                    if m:
                        y_squares(n_norm, m - 1)
                y_squares(n_norm, KD - 1)

            def add_branch(n, n_norm):
                dve.wait_ge(rstd_ready, n_norm + 1)
                for i, k in enumerate(k for k in range(KD) if k not in POOL_TILES):
                    dve.wait_ge(y_gated, KD * n + k + 1)
                    dve.tensor_tensor(y[:, k], y[:, k], rstd, ALU.mult).then_inc(y_scaled, 1)
                    dve.wait_ge(y_scaled, DVE_TILES * n + i + 1)
                    dve.tensor_tensor(x[:, k], x[:, k], y[:, k], ALU.add).then_inc(x_ready, 1)

            normalise(0, 0)
            ffn(0, FIRST["ffn0"], 1)
            add_branch(0, 1)

            def add_scores():
                dve.wait_ge(wi_ready, 1)
                for e, (i, h) in enumerate(score_items()):
                    n = keys_of(i)
                    rows, w = (TS, 4) if i == "s" else (P, i)
                    dve.wait_ge(relu_ready, e + 1)
                    if h == 0:
                        op = dve.tensor_scalar(scores[i][0:rows], relu[0:rows, e % 2, 0:n], wi_tok[0:rows, w, h:h + 1], None,
                                               ALU.mult)
                    else:
                        dve.wait_ge(score_added, e)
                        op = dve.scalar_tensor_tensor(scores[i][0:rows], relu[0:rows, e % 2, 0:n],
                                                      wi_tok[0:rows, w, h:h + 1], scores[i][0:rows], ALU.mult, ALU.add)
                    op.then_inc(score_added, 1)
                dve.wait_ge(score_added, 4 * NH)

            SAMPLE_EARLY = 6

            def choose_eight(i):
                rows = TS if i == "s" else P
                sc = scores[i][0:rows]
                then(dve.max(top8[0:rows, :], sc))
                then(dve.match_replace(sc, top8[0:rows, :], sc, TAKEN))

            def choose(i):
                n, sc = keys_of(i), scores[i][:]
                then(dve.memset(scores[i][0:P // 2, n - P // 2:n], NEG))
                for _ in range(TOPK_P // 8):
                    choose_eight(i)
                then(dve.tensor_scalar(sc, sc, TAKEN / 2, NEG, ALU.is_ge, ALU.mult))

            def masks():
                then(dve.memset(scores[0][:], 0.0))
                then(dve.memset(scores[0][0:P // 2, P // 2:P], NEG))
                for i in (1, 2, 3):
                    choose(i)
                    then(dve.memset(scores[i][0:P // 2, keys_of(i) - P // 2:keys_of(i)], NEG))
                    if i == 1:
                        forget_sums()

            def sample_mask():
                sc = scores["s"][0:TS]
                then(dve.tensor_scalar(sc, sc, TAKEN / 2, NEG, ALU.is_ge, ALU.mult))
                for j in range(1, 4):
                    op = dve.tensor_copy(scores["s"][TS * j:TS * (j + 1)], scores["s"][0:TS])
                op.then_inc(masks_ready, 1)
                dve.wait_ge(masks_ready, 1)

            def row_max(e):
                mixer, i, h = items[e]
                n, b = keys_of(i), 2 * (e % 2)
                dve.wait_ge(logits_done, e + 1)
                if e >= 2:
                    dve.wait_ge(exp_done, e - 1)
                if i == "s":
                    out, src = split(neg_logits[:, e % 2]), halves(b)
                else:
                    out, src = neg_logits[:, e % 2, 0:n], psum[:, b, 0:n]
                if mixer == "A":
                    mask = split(scores[i]) if i == "s" else scores[i][:, 0:n]
                    op = dve.tensor_tensor_reduce(out, src, mask, -1.0, 3.0e38, ALU.add, ALU.min,
                                                  neg_max[:, e % 2:e % 2 + 1])
                else:
                    op = dve.tensor_scalar(out, src, -1.0, None, ALU.mult, ALU.min,
                                           accum_out=neg_max[:, e % 2:e % 2 + 1])
                op.then_inc(max_ready, 1)

            def normal(e):
                _, i, _ = items[e]
                n = keys_of(i)
                dve.wait_ge(exp_done, e + 1)
                then(dve.reciprocal(p_inv[:, e % 2:e % 2 + 1], p_sum[:, e % 2:e % 2 + 1]))
                dve.tensor_scalar(probs[:, e % 2, 0:n], probs[:, e % 2, 0:n], p_inv[:, e % 2:e % 2 + 1], None,
                                  ALU.mult).then_inc(p_ready, 1)

            def outputs(e):
                mixer, i, h = items[e]
                k0 = 4 * (mixer == "B")
                g = group_of[e]
                dve.wait_ge(av_done, e + 1)
                if i == "s":
                    to, src = (slice(k0, k0 + 4), slice(TP, T)), psum[:, 6 + g % 2, 0:P].rearrange("p (k t) -> p k t", k=4)
                else:
                    to, src = (k0 + h // 2, slice(i * P, (i + 1) * P)), psum[:, 6 + g % 2, 0:P]
                dve.tensor_copy(h_hi[:, to[0], to[1]], src).then_inc(o_rounded, 1)
                dve.wait_ge(o_rounded, g + 1)
                dve.tensor_tensor(h_lo[:, to[0], to[1]], src, h_hi[:, to[0], to[1]].bitcast(F32), ALU.subtract)\
                    .then_inc(o_ready, 1)

            def attention(mixer):
                e0 = first_item[mixer]
                for s in range(e0, e0 + n_items + 4):
                    if s < e0 + n_items:
                        if mixer == "B" and items[s][1] != "s" and items[s][2] == 0:
                            forget_queries(items[s][1])
                        row_max(s)
                    if mixer == "A":
                        step = SAMPLE_EARLY + s - 14
                        if SAMPLE_EARLY <= step < TOPK_S // 8:
                            choose_eight("s")
                        if step == TOPK_S // 8:
                            sample_mask()
                    if e0 <= s - 1 < e0 + n_items:
                        normal(s - 1)
                    if e0 <= s - 4 and last_of_group[s - 4]:
                        outputs(s - 4)

            def fox_selectors():
                r = slice(FOX_ROW, FOX_ROW + NH)
                dve.memset(fox_k, 0.0)
                dve.memset(fox_q, 0.0)
                then(dve.memset(fox_qs, 0.0))
                for h in range(NH):
                    dve.tensor_copy(fox_q[r, h, :], sel[r, h:h + 1].broadcast_to([NH, P]))
                    j, c = h // 2, h % 2
                    op = dve.tensor_copy(fox_qs[r, c, TS * j:TS * (j + 1)], sel[r, h:h + 1].broadcast_to([NH, TS]))
                then(op)

            def forget_sums():
                r, r0 = slice(FOX_ROW, FOX_ROW + NH), slice(0, NH)
                dve.wait_ge(fox_own, 4)
                dve.wait_ge(fox_loaded, 16)
                dve.scalar_tensor_tensor(fox_w[r, 0, :], fox_w[r, 0, :], 0.0, fox_w[r, 3, :], ALU.min, ALU.subtract)\
                    .then_inc(fox_copied, 1)
                dve.wait_ge(fox_copied, 1)
                dve.tensor_copy(fox_f[r, 0:TP], fox_w[r, 0, 0:TP])
                then(dve.tensor_copy(fox_f[r, 2 * TP:2 * TP + TS], fox_w[r, 0, TP:T]))
                for a, b in ((0, TP), (TP, TP + NK_S)):
                    op = dve.tensor_tensor_scan(fox_f[r, a:b], one_col[r, :].broadcast_to([NH, b - a]), fox_f[r, a:b], 0.0,
                                                ALU.mult, ALU.add)
                then(op)
                dve.tensor_scalar(fox_k[r, :], fox_f[r, :], -1.0, None, ALU.mult)
                dve.memset(fox_k[r0, :], 1.0)
                dve.tensor_copy(fox_fq[r0, 0:TP], fox_f[r, 0:TP])
                dve.tensor_copy(fox_fq[r0, TP:T], fox_f[r, 2 * TP:2 * TP + TS]).then_inc(fox_summed, 1)
                dve.wait_ge(fox_summed, 1)
                for h in range(NH):
                    j, c = h // 2, h % 2
                    op = dve.tensor_scalar(fox_qs[r0, c, TS * j:TS * (j + 1)], fox_fq[r0, TP:T], sel[r0, h:h + 1], None,
                                           ALU.mult)
                then(op)

            def forget_queries(i):
                if i:
                    dve.wait_ge(logits_done, first_item["B"] + NH * i)
                dve.tensor_tensor(fox_q[0:NH], fox_fq[0:NH, i * P:(i + 1) * P].unsqueeze(1).broadcast_to([NH, NH, P]),
                                  sel[0:NH, :].unsqueeze(2).broadcast_to([NH, NH, P]), ALU.mult).then_inc(fox_ready, 1)

            dve.wait_ge(ada_added, ADA_HEAD + KB)
            conditions(1)
            conditions(2)
            normalise(1, 2)
            fox_selectors()
            add_scores()
            masks()
            for _ in range(SAMPLE_EARLY):
                choose_eight("s")
            dve.wait_ge(logf_stored, 16)
            attention("A")
            attention("B")
            y_copied(FIRST["ab_out"], 3)
            add_branch(1, 3)
            normalise(2, 4, sums_start=True)
            ffn(1, FIRST["ffn1"], 5)
            add_branch(2, 5)
            dve.wait_ge(ada_added, ADA_HEAD + 2 * KB)
            conditions(3)
            conditions(4)
            normalise(3, 6, sums_start=True)
            ffn(2, FIRST["ffn2"], 7)
            add_branch(3, 7)
            dve.wait_ge(ada_added, ADA_HEAD + 3 * KB)
            conditions(5)
            normalise(4, 8)

            def convolve(m):
                dve.wait_ge(bank_free[m % 2], FIRST["gdn_in"] + (m + 2) // 2 + 2)
                if m >= 2:
                    dve.wait_ge(conv_silu, m - 1)
                acc = conv_acc[:, m % 2]
                then(dve.tensor_scalar(acc, conv_in[:, m % 2, 0:TP], conv_w[:, m, 0:1], None, ALU.mult))
                for j in range(1, CW):
                    if j == CW - 1:
                        dve.tensor_copy(conv_last[:, m, :], conv_in[:, m % 2, TP:TP + CW - 1])
                    op = dve.scalar_tensor_tensor(acc, conv_in[:, m % 2, j:j + TP], conv_w[:, m, j:j + 1], acc,
                                                  ALU.mult, ALU.add)
                    if j < CW - 1:
                        then(op)
                op.then_inc(conv_done, 1)

            def convolve_sample():
                w = [conv_w[:, :, j:j + 1].broadcast_to([P, QKV, TS]) for j in range(CW)]
                then(dve.tensor_copy(conv_s[:, :, 0:CW - 1], conv_before))
                then(dve.tensor_tensor(conv_sum, conv_s[:, :, 0:TS], w[0], ALU.mult))
                for j in range(1, CW):
                    then(dve.tensor_tensor(conv_tap, conv_s[:, :, j:j + TS], w[j], ALU.mult))
                    op = dve.tensor_tensor(conv_sum, conv_sum, conv_tap, ALU.add)
                    if j < CW - 1:
                        then(op)
                op.then_inc(sample_conv, 1)
                dve.wait_ge(sample_conv, 1)
                dve.memset(row_keep, 1.0).then_inc(conv_done, 1)

            def decay_rows():
                dve.wait_ge(conv_done, QKV + 1)
                dve.wait_ge(rows_lin, 3)
                then(dve.scalar_tensor_tensor(row_sp, row_a, 0.0, row_sp, ALU.max, ALU.add))
                then(dve.tensor_scalar(row_sp, row_sp, g_col[:, 3:4], -1.0, ALU.mult, ALU.mult))
                then(dve.memset(row_keep.rearrange("p (c n) -> p c n", n=TS)[:, 0:TP // TS:CHUNK // TS, 0:1], 0.0))
                then(dve.memset(row_keep[:, TP:TP + 1], 0.0))
                then(dve.tensor_tensor_scan(row_g, row_keep, row_sp, 0.0, ALU.mult, ALU.add))
                then(dve.scalar_tensor_tensor(row_lb, row_b, 0.0, row_lb, ALU.min, ALU.subtract))
                dve.tensor_copy(ends[:, 0:CHUNKS], row_g[:, CHUNK - 1:TP:CHUNK])
                dve.tensor_copy(ends[:, CHUNKS:], row_g[:, T - 1:T]).then_inc(rows_ready, 1)
                for to in (rows_r, rows_c, rows_e):
                    op = dve.memset(to, 0.0)
                then(op)
                dve.wait_ge(lens_ln, 1)
                then(dve.tensor_scalar(row_lr, row_lr, -0.5, g_col[:, 2:3], ALU.mult, ALU.add))

                def rows(at):
                    return slice(at, at + NH)

                k, b, q, d = rows(ROW_K), rows(ROW_B), rows(ROW_Q), rows(ROW_D)
                then(dve.tensor_tensor(row_a, row_g, row_lr, ALU.add))
                then(dve.tensor_tensor(row_b, row_lr, row_g, ALU.subtract))
                dve.tensor_tensor(rows_r[k, :], row_a[k, :], row_lb[k, :], ALU.add)
                dve.tensor_tensor(rows_e[k, :], row_a[k, :], row_lb[k, :], ALU.add)
                dve.memset(rows_r[b, :], 1.0)
                dve.tensor_copy(rows_r[q, :], row_a[q, :])
                dve.memset(rows_c[k, :], 1.0)
                dve.tensor_copy(rows_c[b, :], row_b[b, :])
                dve.memset(rows_c[q, :], 1.0)
                dve.tensor_copy(rows_e[b, :], row_lb[b, :])
                dve.tensor_copy(rows_e[q, :], row_a[q, :])
                dve.tensor_tensor(rows_e[d, 0:TP].rearrange("p (c n) -> p c n", n=CHUNK),
                                  row_b[d, 0:TP].rearrange("p (c n) -> p c n", n=CHUNK),
                                  row_g[d, CHUNK - 1:TP:CHUNK].unsqueeze(2).broadcast_to([NH, CHUNKS, CHUNK]), ALU.add)
                dve.tensor_tensor(rows_e[d, TP:T], row_b[d, TP:T], row_g[d, T - 1:T].broadcast_to([NH, TS]), ALU.add)\
                    .then_inc(rows_ready, 1)

            def columns():
                dve.wait_ge(rows_exp, 1)
                dve.memset(v_new, 0.0)
                dve.memset(state_p, 0.0).then_inc(ends_ready, 1)
                dve.tensor_tensor(ends_by_head, ends.unsqueeze(2).broadcast_to([P, CHUNKS + 1, NH]),
                                  g_sel[:, 3, :].unsqueeze(1).broadcast_to([P, CHUNKS + 1, NH]), ALU.mult)\
                    .then_inc(ends_ready, 1)
                dve.wait_ge(rows_turned, 1)
                dve.tensor_copy(cols, as_tiles(psum[:, 6, :]))
                dve.tensor_copy(g_last.rearrange("p c h -> p (c h)"), psum[:, 7, P:P + (CHUNKS + 1) * NH])
                for g in range(2):
                    for j in range(4):
                        r = slice(TS * j, TS * (j + 1))
                        op = dve.tensor_copy(cols_s[r, g, :], psum[r, 7, 4 * g + j:P:TS])
                op.then_inc(cols_ready, 1)
                dve.wait_ge(cols_ready, 1)

            def column(at, q):
                n = tiles_of(q)
                if q < NH:
                    return cols[:, :, at + q:at + q + 1].broadcast_to([P, n, P])
                return cols_s[:, q - NH:q - NH + 1, at // TS:at // TS + 1].broadcast_to([P, n, P])

            def gdn_decay(q):
                u, n, b = q % 2, size(q), 4 * (q % 2)
                dve.wait_ge(kk_exp, q + 1)
                dve.tensor_tensor(low[:, u, 0:n], psum[:, b, 0:n], t2[:, u, 0:n], ALU.mult).then_inc(kk_decayed, 1)
                dve.wait_ge(kq_exp, q + 1)
                dve.tensor_tensor(qk_t[:, q, :] if q < NH else qk_s[:, q - NH, :], psum[:, b + 2, 0:n],
                                  low_m[:, u, 0:n], ALU.mult).then_inc(kq_decayed, 1)
                dve.wait_ge(kk_decayed, q + 1)
                dve.wait_ge(kq_decayed, q + 1)

            def gdn_mask(q, l):
                u, n = q % 2, size(q)
                if l:
                    dve.wait_ge(t2_made, level_at(q, l - 1) + 1)
                dve.tensor_tensor(as_tiles(low_m[:, u, 0:n]), as_tiles(low[:, u, 0:n]),
                                  g_mask[:, 4 + l, :].unsqueeze(1).broadcast_to([P, tiles_of(q), P]), ALU.mult)\
                    .then_inc(low_ready, 1)

            def gdn_start(q):
                u, n = q % 2, size(q)
                dve.wait_ge(low_ready, level_at(q, 0) + 1)
                eye = ident[:].unsqueeze(1).broadcast_to([P, tiles_of(q), P])
                dve.tensor_tensor(as_tiles(inv[:, u, 0:n]), eye, as_tiles(low_m[:, u, 0:n]), ALU.subtract)

            def gdn_scale(q, l):
                u, n, b = q % 2, size(q), 4 * (q % 2)
                f = psum[:, b + 2, 0:n]
                if l == 1:
                    dve.wait_ge(q_factor, q + 1)
                    dve.tensor_tensor(z_item(GZ_Q, q), z_item(GZ_Q, q), f if q < NH else as_heads(f), ALU.mult)\
                        .then_inc(q_scaled, 1)
                elif l == 2:
                    dve.wait_ge(k_turned, q + 1)
                    dve.tensor_tensor(as_tiles(k_beta[:, u, 0:n]), as_tiles(f), column(ROW_K, q), ALU.mult)
                elif l == 3:
                    dve.tensor_tensor(as_tiles(gz[:, GZ_K + q, 0:TP]) if q < NH else kdec_s[:, q - NH:q - NH + 1, :],
                                      as_tiles(f), column(ROW_D, q), ALU.mult).then_inc(k_scaled, 1)
                elif l == 4:
                    dve.wait_ge(v_turned_g, q + 1)
                    dve.tensor_tensor(as_tiles(v_beta[:, u, 0:n]), as_tiles(f), column(ROW_B, q), ALU.mult)\
                        .then_inc(v_scaled, 1)

            def gdn_update(q, l):
                u, n, b = q % 2, size(q), 4 * (q % 2)
                if l == 0:
                    dve.wait_ge(t2_made, level_at(q, 0) + 1)
                    eye = ident[:].unsqueeze(1).broadcast_to([P, tiles_of(q), P])
                    op = dve.tensor_tensor(as_tiles(inv_t[:, u, 0:n]), eye, as_tiles(psum[:, b + 3, 0:n]), ALU.subtract)
                else:
                    dve.wait_ge(e_made, copies_at(q, l) + 1)
                    dve.wait_ge(inv_t_ready, level_at(q, l - 1) + 1)
                    dve.wait_ge(inv_ready, level_at(q, l - 1) + 1)
                    op = dve.tensor_tensor(inv_t[:, u, 0:n], inv_t[:, u, 0:n], psum[:, b, 0:n], ALU.subtract)
                op.then_inc(inv_t_ready, 1)
                if 0 < l < levels_of(q) - 1:
                    dve.tensor_tensor(inv[:, u, 0:n], inv[:, u, 0:n], psum[:, b + 1, 0:n], ALU.subtract)\
                        .then_inc(inv_ready, 1)
                else:
                    dve.wait_ge(inv_t_ready, level_at(q, l) + 1)
                    dve.sem_inc(inv_ready, 1)

            def recur_v(n):
                c, h = steps[n]
                dve.wait_ge(v_made, n + 1)
                if n >= 2:
                    dve.wait_ge(kv_made, n - 1)
                m, r = (TS, TS * (h % 4)) if c == "s" else (CHUNK, CHUNK * (c % 2))
                src = u_s[r:r + m, h // 4, :] if c == "s" else gz[r:r + m, GZ_V + h, c // 2 * P:(c // 2 + 1) * P]
                dve.tensor_tensor(v_new[r:r + m, 2 if c == "s" else c % 2, n % 2, :], psum[r:r + m, n % 2, 0:P], src, ALU.add)\
                    .then_inc(v_new_ready, 1)

            def recur_state(n):
                c, h = steps[n]
                dve.wait_ge(kv_made, n + 1)
                state, at = (state_s, CHUNKS) if c == "s" else (state_p, c)
                dve.scalar_tensor_tensor(state[:, h, :], state[:, h, :], g_last[:, at, h:h + 1], psum[:, 4 + n % 2, 0:P],
                                         ALU.mult, ALU.add).then_inc(state_new, 1)

            dve.wait_ge(gdn_loaded, 16 * 5)
            dve.memset(conv_in[:, :, 0:CW - 1], 0.0).then_inc(conv_zeroed, 1)
            dve.wait_ge(conv_zeroed, 1)
            for m in range(QKV):
                convolve(m)
            convolve_sample()
            decay_rows()
            columns()
            dve.wait_ge(gdn_masks, 16)
            for q0 in range(0, G_ITEMS, 2):
                pair = (q0, q0 + 1)
                for q in pair:
                    gdn_decay(q)
                    gdn_mask(q, 0)
                for q in pair:
                    gdn_start(q)
                    gdn_update(q, 0)
                    gdn_mask(q, 1)
                for l in range(1, levels_of(q0)):
                    for q in pair:
                        if l + 1 < levels_of(q):
                            gdn_mask(q, l + 1)
                    for q in pair:
                        gdn_update(q, l)
                    for q in pair:
                        gdn_scale(q, l)
            dve.wait_ge(gdn_state, 16)
            for n in range(len(steps) + 2):
                if n < len(steps):
                    recur_v(n)
                if n >= 2:
                    if n - 2 >= NH:
                        dve.wait_ge(state_new, n - 2 - NH + 1)
                    recur_state(n - 2)
            dve.wait_ge(o_out, len(steps))
            for h in range(NH):
                op = dve.scalar_tensor_tensor(gz[:, GZ_G + h], gz[:, GZ_Q + h], norm_col[:], gz[:, GZ_G + h],
                                              ALU.mult, ALU.mult)
                op.then_inc(g_used, 1)
            for h in range(NH):
                dve.wait_ge(g_used, h + 1)
                dve.wait_ge(g_rstd_ready, h + 1)
                if h >= 2:
                    dve.wait_ge(g_ready, h - 1)
                then(dve.tensor_tensor(g_out[:, h % 2], gz[:, GZ_G + h], g_rstd[:, h], ALU.mult))
                dve.tensor_copy(h_hi[:, h], g_out[:, h % 2]).then_inc(g_own, 1)
                dve.wait_ge(g_own, h + 1)
                dve.tensor_tensor(h_lo[:, h], g_out[:, h % 2], h_hi[:, h].bitcast(F32), ALU.subtract).then_inc(g_ready, 1)
            y_copied(FIRST["gdn_out"], 9)
            add_branch(4, 9)
            normalise(5, 10, sums_start=True)
            ffn(3, FIRST["ffn3"], 11)
            add_branch(5, 11)


OUTS = {"y_t": (D, T), "a_k": (TP, T), "a_v": (TP, T), "a_ik": (HD, T), "b_k": (TP, T), "b_v": (TP, T),
        "b_logf": (NH, T), "p_conv": (QKV * P, CW - 1), "s_conv": (QKV * P, CW - 1), "p_rec": (NH, P, P),
        "s_rec": (NH, P, P)}


def arrays(i):
    f = np.float32
    tokens = np.concatenate([i["x_prompt"][0], i["x_sample"][0]], 0)

    def units(w, cols=None):
        k, n = w.shape
        return w.reshape(k // D, KD, P, n // P, P).transpose(0, 3, 2, 1, 4).reshape(k // D, n // P, P, D)

    def ffn(l, j):
        g = units(i["ffn_w_gate"][l, j])[0].reshape(KB, KD, 1, P, D)
        u = units(i["ffn_w_up"][l, j])[0].reshape(KB, KD, 1, P, D)
        gu = np.concatenate([g, u], 2)
        dn = units(i["ffn_w_down"][l, j]).reshape(KB, KD // 2, 2, P, D)
        return np.concatenate([gu, dn], 1).reshape(-1, 2, P, D)

    def product(w):
        return units(w)[0].reshape(-1, 2, P, D)

    qa, ka, va, qi, ki, wi, qb, kb, vb, fl = np.split(
        i["ab_w_in"], np.cumsum([512, 512, 512, 512, 64, 8, 512, 512, 512]), axis=1)
    gap = np.zeros((D, FOX_ROW - NH), f)
    ab_in = np.concatenate([ki, ki, wi, gap, fl, np.zeros((D, P - FOX_ROW - NH), f), qi, ka, qa, va, kb, qb, vb], 1)
    rel = np.arange(REL) - (5 * P - 1)
    n = np.abs(rel)
    far = 8 + (np.log(np.maximum(n, 1).astype(f) / f(8)) / f(np.log(32.0)) * f(8)).astype(np.int32)
    bucket = np.where(rel > 0, 16, 0) + np.where(n < 8, n, np.minimum(far, 15))
    heads = np.arange(NH)
    sel = np.zeros((P, NH), f)
    sel[heads, heads] = 1
    sel[FOX_ROW + heads, heads] = 1
    q = np.arange(P)
    b_f = np.zeros((P, 1), f)
    b_f[FOX_ROW:FOX_ROW + NH, 0] = i["ab_b_f"]

    def flat(name):
        return i[name][0].reshape(TP, -1)

    qkv, gate, b_logit, a_logit = np.split(i["gdn_w_in"], np.cumsum([QKV * P, NH * P, NH]), axis=1)

    def in_rows(a, at):
        out = np.zeros((a.shape[0], P), f)
        for r in at:
            out[:, r:r + NH] = a
        return out

    every = (ROW_K, ROW_B, ROW_Q, ROW_D)
    gdn_in = np.concatenate([in_rows(a_logit, every), in_rows(b_logit, (ROW_K, ROW_B)), qkv, gate], 1)
    eye = np.eye(NH, dtype=f)
    g_sel = np.stack([in_rows(eye, at).T for at in ((ROW_K, ROW_B), (ROW_Q, ROW_B), (ROW_Q,), (ROW_K,))], 1)
    g_col = np.zeros((P, 4), f)
    g_col[:, 0] = in_rows(i["gdn_dt_bias"][None, :], every)[0]
    g_col[:, 1] = in_rows(i["gdn_A_log"][None, :], every)[0]
    g_col[ROW_Q:ROW_Q + NH, 2] = -0.5 * np.log(P)
    strips = np.zeros((P, 2, STRIP), f)
    strips[:, 0, ROW_Q + NH - 1] = 1
    for r in (ROW_K, ROW_B, ROW_D):
        strips[:, 1, r + NH - 1] = 1

    def allow(ok):
        return np.where(ok, 0, NEG).astype(f)

    r, c = q[:, None], q[None, :]
    g_mask = [allow((r // n == c // n) & ok) for n in (CHUNK, TS) for ok in (c < r, r <= c)]
    for l in range(LEVELS):
        n = 1 << l
        g_mask.append(((r // (2 * n) == c // (2 * n)) & (r // n % 2 == 1) & (c // n % 2 == 0)).astype(f))

    stream = [ffn(0, 0), product(ab_in), product(i["ab_w_out"]), ffn(0, 1), ffn(1, 0), product(gdn_in),
              product(i["gdn_w_out"]), ffn(1, 1)]
    out = {
        "x_t": tokens.T,
        "c_t": np.stack([i["c_prompt"][0], i["c_sample"][0]], 1).reshape(KD, P, 2).transpose(1, 0, 2),
        "ada_b": i["ada_b"].reshape(ADA_TILES, P).T,
        "g_pre": i["norm_pre"].reshape(-1, P).T,
        "g_post": i["norm_post"].reshape(-1, P).T,
        "eps": np.full((P, 1), EPS, f),
        "ident": np.eye(P, dtype=f),
        "rel_bias": i["rel_bias"],
        "onehot": (np.arange(32)[:, None] == bucket[None, :]).astype(f),
        "diag_mask": np.where(q[None, :] <= q[:, None], 0, NEG).astype(f),
        "tail_mask": np.where(np.arange(TS)[None, :] <= (q % TS)[:, None], 0, NEG).astype(f),
        "sel": sel,
        "b_f": b_f,
        "cache_ik": np.concatenate([flat("cache_a_idx_k").T] * 2, 0),
        "cache_A_k": flat("cache_a_k").T,
        "cache_A_v": flat("cache_a_v"),
        "cache_B_k": flat("cache_b_k").T,
        "cache_B_v": flat("cache_b_v"),
        "cache_logf": flat("cache_b_logf").T,
        "ada_w": i["ada_w"].reshape(LAYERS, KD, P, ADA_HALVES // LAYERS, ADA_HALF).transpose(0, 3, 1, 2, 4)
                 .reshape(ADA_HALVES, KD, P, ADA_HALF),
        "strips": strips,
        "g_sel": g_sel,
        "g_col": g_col,
        "conv_w": i["gdn_conv_w"].reshape(CW, QKV, P).transpose(2, 1, 0),
        "conv_before": i["state_c_conv"][0].reshape(CW - 1, QKV, P).transpose(2, 1, 0),
        "state_rec": i["state_c_rec"][0],
        "g_mask": np.stack(g_mask, 1),
        "norm_col": i["gdn_norm_w"][:, None],
        "w_stream": np.concatenate(stream, 0).transpose(0, 2, 1, 3),
    }
    return {k: np.ascontiguousarray(v) for k, v in out.items()}


def kernel(**inputs):
    import concourse.bacc as bacc
    from concourse.bass_utils import run_bass_kernel_spmd

    nc = bacc.Bacc("TRN2", target_bir_lowering=False, num_devices=1, dynamic_dma_scratch_size=1024)
    ins = {f"in_{name}": a for name, a in arrays({k: np.asarray(v) for k, v in inputs.items()}).items()}
    io = {name[3:]: nc.dram_tensor(name, list(a.shape), mybir.dt.from_np(a.dtype), kind="ExternalInput").ap()
          for name, a in ins.items()}
    for name, shape in OUTS.items():
        io[name] = nc.dram_tensor(f"out_{name}", list(shape), F32, kind="ExternalOutput").ap()
    io["rel_spread"] = nc.dram_tensor("rel_spread", [NH, REL_AT], F32, kind="Internal").ap()
    build(nc, io)
    r = run_bass_kernel_spmd(nc, [ins], core_ids=[0]).results[0]
    got = {name: np.asarray(r[f"out_{name}"]) for name in OUTS}
    out = []
    for group, t in (("p", slice(0, TP)), ("s", slice(TP, T))):
        n = t.stop - t.start
        heads = {name: got[name].T[t].reshape(1, n, NH, HD) for name in ("a_k", "a_v", "b_k", "b_v")}
        out.append((got["y_t"].T[None, t],
                    [heads["a_k"], heads["a_v"], got["a_ik"].T[None, t], heads["b_k"], heads["b_v"],
                     got["b_logf"].T[None, t], got[group + "_conv"].T[None], got[group + "_rec"][None]]))
    return tuple(np.ascontiguousarray(a) for a in (out[0][0], out[1][0], *out[0][1], *out[1][1]))
```
